# Optimizing a Trainium2 kernel written in Bass

```python
import jax, jax.numpy as jnp
from jax import lax
import numpy as np

D_MODEL = 1024
BATCH = 1
SEQ = 1024
DEPTH = 1

EPS = 1e-6
CONV_WIDTH = 3
D_CONV = D_MODEL
GLA_HEADS = 4
GLA_DK = D_MODEL // 2
GLA_DV = D_MODEL
GLA_HEAD_DK = GLA_DK // GLA_HEADS
GLA_HEAD_DV = GLA_DV // GLA_HEADS
GLA_LOWRANK = 16
GLA_TAU = 16.0
GLA_CHUNK = 64
PEER_HEADS = 8
PEER_NKEYS = 128
PEER_EXPERTS = PEER_NKEYS ** 2
PEER_TOPK = 16
PEER_QDIM = 256
PEER_TOK_BLOCK = 128
IN_SIZES = (D_CONV, D_CONV, D_CONV,
            GLA_DK, GLA_DK, GLA_DV, GLA_DV,
            GLA_LOWRANK, GLA_LOWRANK,
            D_MODEL, D_MODEL)
IN_SPLITS = tuple(int(s) for s in np.cumsum(IN_SIZES)[:-1])
W_IN_COLS = int(sum(IN_SIZES))

kernel_name = 'hybrid_shortconv_gla_peer_encoder_block'

def _rmsnorm(x, g):
    xf = x.astype(jnp.float32)
    xf = xf * lax.rsqrt(jnp.mean(xf * xf, axis=-1, keepdims=True) + EPS)
    return (xf * g.astype(jnp.float32)).astype(x.dtype)

def _centred_depthwise_conv(u, w, b):
    pad = CONV_WIDTH // 2
    T = u.shape[1]
    up = jnp.pad(u, ((0, 0), (pad, pad), (0, 0)))
    y = b
    for j in range(CONV_WIDTH):
        y = y + up[:, j:j + T] * w[j]
    return y

def _gla_one_direction(q, k, v, log_a):
    Bsz, T, H, dk = q.shape
    dv = v.shape[-1]
    n = T // GLA_CHUNK
    f32 = jnp.float32

    def chunks(t):
        return t.astype(f32).reshape(Bsz, n, GLA_CHUNK, H, t.shape[-1])

    q, k, v, la = chunks(q), chunks(k), chunks(v), chunks(log_a)
    b = jnp.cumsum(la, axis=2)
    b_last = b[:, :, -1]
    b_ref = b[:, :, GLA_CHUNK // 2][:, :, None]
    q_in = q * jnp.exp(b - b_ref)
    k_in = k * jnp.exp(b_ref - b)
    mask = jnp.tril(jnp.ones((GLA_CHUNK, GLA_CHUNK), dtype=bool))
    scores = jnp.einsum('bnihd,bnjhd->bnhij', q_in, k_in)
    scores = jnp.where(mask, scores, 0.0)
    o_intra = jnp.einsum('bnhij,bnjhe->bnihe', scores, v)
    k_to_end = k * jnp.exp(b_last[:, :, None] - b)
    u = jnp.einsum('bnjhd,bnjhe->bnhde', k_to_end, v)
    decay = jnp.exp(b_last)

    def step(S, inp):
        dec, uc = inp
        return dec[..., None] * S + uc, S

    S0 = jnp.zeros((Bsz, H, dk, dv), f32)
    _, S_prev = lax.scan(step, S0, (jnp.moveaxis(decay, 1, 0), jnp.moveaxis(u, 1, 0)))
    S_prev = jnp.moveaxis(S_prev, 0, 1)
    o_inter = jnp.einsum('bnihd,bnhde->bnihe', q * jnp.exp(b), S_prev)
    return (o_intra + o_inter).reshape(Bsz, T, H, dv)

def _bidirectional_gla(q, k, v, la_f, la_b):
    o_f = _gla_one_direction(q, k, v, la_f)

    def flip(t):
        return jnp.flip(t, axis=1)

    o_b = flip(_gla_one_direction(flip(q), flip(k), flip(v), flip(la_b)))
    return o_f + o_b

def _mixer(xn, w_in, conv_w, conv_b, wa_proj, decay_up_f, decay_bias_f, decay_up_b,
           decay_bias_b, gla_norm_g, wb_proj, gate_bias, w_out):
    Bsz, T, _ = xn.shape
    h = xn @ w_in
    xa, ba, ca, q, k, v, r, zf, zb, ga, gb = jnp.split(h, IN_SPLITS, axis=-1)

    ya = ba * _centred_depthwise_conv(ca * xa, conv_w, conv_b)
    out_a = ya @ wa_proj

    def heads(t, d):
        return t.reshape(Bsz, T, GLA_HEADS, d)

    qh = heads(q, GLA_HEAD_DK) * (GLA_HEAD_DK ** -0.5)
    kh = heads(k, GLA_HEAD_DK)
    vh = heads(v, GLA_HEAD_DV)
    la_f = jax.nn.log_sigmoid((zf @ decay_up_f + decay_bias_f).astype(jnp.float32)) / GLA_TAU
    la_b = jax.nn.log_sigmoid((zb @ decay_up_b + decay_bias_b).astype(jnp.float32)) / GLA_TAU
    o = _bidirectional_gla(qh, kh, vh, heads(la_f, GLA_HEAD_DK), heads(la_b, GLA_HEAD_DK))
    o = _rmsnorm(o, gla_norm_g.reshape(GLA_HEADS, GLA_HEAD_DV))
    o = o.reshape(Bsz, T, GLA_DV).astype(xn.dtype) * jax.nn.silu(r)
    out_b = o @ wb_proj

    gate_a = jax.nn.sigmoid(ga + gate_bias[0])
    gate_b = jax.nn.sigmoid(gb + gate_bias[1])
    return (gate_a * out_a + gate_b * out_b) @ w_out

def _peer(xn, wq, keys, u_tab, v_tab):
    Bsz, T, D = xn.shape
    BT = Bsz * T
    xt = xn.reshape(BT, D)
    q = (xt @ wq).reshape(BT, PEER_HEADS, 2, PEER_QDIM // 2)
    s = jnp.einsum('thpd,hpkd->thpk', q, keys).astype(jnp.float32)
    top_s, top_i = lax.top_k(s, PEER_TOPK)
    cand = (top_s[:, :, 0, :, None] + top_s[:, :, 1, None, :]).reshape(BT, PEER_HEADS, PEER_TOPK * PEER_TOPK)
    best_s, best_c = lax.top_k(cand, PEER_TOPK)
    i1 = jnp.take_along_axis(top_i[:, :, 0], best_c // PEER_TOPK, axis=-1)
    i2 = jnp.take_along_axis(top_i[:, :, 1], best_c % PEER_TOPK, axis=-1)
    experts = (i1 * PEER_NKEYS + i2).reshape(BT, PEER_HEADS * PEER_TOPK)
    gates = jax.nn.softmax(best_s, axis=-1).reshape(BT, PEER_HEADS * PEER_TOPK).astype(xn.dtype)
    nb = BT // PEER_TOK_BLOCK

    def block(args):
        xb, eb, gbk = args
        hidden = jax.nn.gelu(jnp.einsum('td,tkd->tk', xb, u_tab[eb]), approximate=False)
        return jnp.einsum('tk,tkd->td', gbk * hidden, v_tab[eb])

    out = lax.map(block, (xt.reshape(nb, PEER_TOK_BLOCK, D),
                          experts.reshape(nb, PEER_TOK_BLOCK, -1),
                          gates.reshape(nb, PEER_TOK_BLOCK, -1)))
    return out.reshape(Bsz, T, D)

def setup_inputs(seed: int = 0) -> dict:
    key = jax.random.key(seed)
    ks = jax.random.split(key, 24)

    def nrm(k, shape, scale):
        return jax.random.normal(k, shape, jnp.float32) * scale

    L = DEPTH
    return {
        'x': nrm(ks[0], (BATCH, SEQ, D_MODEL), 1.0),
        'norm1_g': 1.0 + nrm(ks[1], (L, D_MODEL), 0.02),
        'w_in': nrm(ks[2], (L, D_MODEL, W_IN_COLS), D_MODEL ** -0.5),
        'conv_w': nrm(ks[3], (L, CONV_WIDTH, D_CONV), CONV_WIDTH ** -0.5),
        'conv_b': nrm(ks[4], (L, D_CONV), 0.01),
        'wa_proj': nrm(ks[5], (L, D_CONV, D_MODEL), D_CONV ** -0.5),
        'decay_up_f': nrm(ks[6], (L, GLA_LOWRANK, GLA_DK), GLA_LOWRANK ** -0.5),
        'decay_bias_f': 1.0 + nrm(ks[7], (L, GLA_DK), 0.5),
        'decay_up_b': nrm(ks[8], (L, GLA_LOWRANK, GLA_DK), GLA_LOWRANK ** -0.5),
        'decay_bias_b': 1.0 + nrm(ks[9], (L, GLA_DK), 0.5),
        'gla_norm_g': 1.0 + nrm(ks[10], (L, GLA_DV), 0.02),
        'wb_proj': nrm(ks[11], (L, GLA_DV, D_MODEL), GLA_DV ** -0.5),
        'gate_bias': nrm(ks[12], (L, 2, D_MODEL), 0.01),
        'w_out': nrm(ks[13], (L, D_MODEL, D_MODEL), D_MODEL ** -0.5),
        'norm2_g': 1.0 + nrm(ks[14], (L, D_MODEL), 0.02),
        'peer_wq': nrm(ks[15], (L, D_MODEL, PEER_HEADS * PEER_QDIM), D_MODEL ** -0.5),
        'peer_keys': nrm(ks[16], (L, PEER_HEADS, 2, PEER_NKEYS, PEER_QDIM // 2), (PEER_QDIM // 2) ** -0.5),
        'peer_u': nrm(ks[17], (L, PEER_EXPERTS, D_MODEL), D_MODEL ** -0.5),
        'peer_v': nrm(ks[18], (L, PEER_EXPERTS, D_MODEL), (PEER_HEADS * PEER_TOPK) ** -0.5),
        'final_norm_g': 1.0 + nrm(ks[19], (D_MODEL,), 0.02),
    }

def reference(x, norm1_g, w_in, conv_w, conv_b, wa_proj, decay_up_f, decay_bias_f,
              decay_up_b, decay_bias_b, gla_norm_g, wb_proj, gate_bias, w_out, norm2_g,
              peer_wq, peer_keys, peer_u, peer_v, final_norm_g):
    for l in range(DEPTH):
        xn = _rmsnorm(x, norm1_g[l])
        x = x + _mixer(xn, w_in[l], conv_w[l], conv_b[l], wa_proj[l], decay_up_f[l],
                       decay_bias_f[l], decay_up_b[l], decay_bias_b[l], gla_norm_g[l],
                       wb_proj[l], gate_bias[l], w_out[l])
        xn = _rmsnorm(x, norm2_g[l])
        x = x + _peer(xn, peer_wq[l], peer_keys[l], peer_u[l], peer_v[l])
    return _rmsnorm(x, final_norm_g)


_drawn_inputs = setup_inputs


def setup_inputs(seed=0):
    import zlib

    import numpy as np

    out = dict(_drawn_inputs(seed))
    spreads = {}
    factors = {'conv_b': 8.0,
     'decay_up_f': 2.949,
     'decay_up_b': 2.887,
     'gla_norm_g': 8.0,
     'gate_bias': 8.0,
     'norm2_g': 8.0,
     'final_norm_g': 2.839}
    for name, (base, spread) in spreads.items():
        noise = np.random.default_rng([zlib.crc32(name.encode()), seed]).standard_normal(out[name].shape)
        drawn = base * np.exp(spread * noise) if base else spread * noise
        out[name] = __import__('jax').numpy.asarray(drawn.astype(out[name].dtype))
    for name, factor in factors.items():
        out[name] = (out[name] * factor).astype(out[name].dtype)
    return out
```

```python
import numpy as np
import concourse.bass as bass
from concourse import mybir
from contextlib import ExitStack

F32 = mybir.dt.float32
F32R = mybir.dt.float32r
U32 = mybir.dt.uint32
ALU = mybir.AluOpType
ACT = mybir.ActivationFunctionType
AX = mybir.AxisListType

P = 128
T = 1024
D = 1024
NB = T // P
NC = D // P
HALF = 512
NH = 4
DK = 128
DV = 256
NE = DV // P
CH = 64
NCH = T // CH
RANK = 16
TAU = 16.0
EPS = 1e-6
PH = 8
NKEYS = 128
TOPK = 16
SLOTS = PH * TOPK
RING = 16
NEG = -3.4e38

S_Z, S_KQ, S_V, S_R, S_BG, S_CONV, S_AG = 0, 1, 9, 17, 25, 41, 65


class Weights:

    def __init__(self, ctx, nc, tag):
        self.raw = ctx.enter_context(nc.sbuf_tensor(f"w_raw_{tag}", [P, 2, NC, P], F32))
        self.hi = ctx.enter_context(nc.sbuf_tensor(f"w_hi_{tag}", [P, 2, NC, P], F32R))
        self.lo = ctx.enter_context(nc.sbuf_tensor(f"w_lo_{tag}", [P, 2, NC, P], F32R))
        self.loaded = [ctx.enter_context(nc.semaphore(f"w_loaded{s}_{tag}")) for s in range(2)]
        self.high = ctx.enter_context(nc.semaphore(f"w_high_{tag}"))
        self.split = ctx.enter_context(nc.semaphore(f"w_split_{tag}"))
        self.used = ctx.enter_context(nc.semaphore(f"w_used_{tag}"))


def load_weights(sp, w, stream, first, count):
    for s in range(2):
        sp.dma_start(w.raw[:, s], stream[first + s]).then_inc(w.loaded[s], 16)
    with sp.Fori(1, count // 2) as i:
        for s in range(2):
            sp.wait_ge(w.split, i * 2 + s - 1)
            sp.dma_start(w.raw[:, s], stream[bass.ds(i * 2 + (first + s), 1)].rearrange("o p k m -> (o p) k m")).then_inc(w.loaded[s], 16)
    if count % 2:
        sp.wait_ge(w.split, count - 2)
        sp.dma_start(w.raw[:, 0], stream[first + count - 1]).then_inc(w.loaded[0], 16)


def split_chunk(nc, pool, C, w, s, n, loaded16):
    pool.wait_ge(w.loaded[s], loaded16)
    C.settle(pool, "pool")
    nc.gpsimd.tensor_copy(w.hi[:, s], w.raw[:, s]).then_inc(w.high, 1)
    pool.wait_ge(w.high, n + 1)
    nc.gpsimd.tensor_tensor(w.lo[:, s], w.raw[:, s], w.hi[:, s].bitcast(F32), ALU.subtract).then_inc(w.split, 1)


def split_weights(nc, pool, C, w, count):
    for s in range(2):
        split_chunk(nc, pool, C, w, s, s, 16)
    with pool.Fori(1, count // 2) as i:
        for s in range(2):
            pool.wait_ge(w.used, i * 2 + s - 1)
            split_chunk(nc, pool, C, w, s, i * 2 + s, i * 16 + 16)


def project(nc, w, s, act_hi, act_lo, out):
    last = None
    for k in range(NC):
        for part, act, flag in ((w.hi, act_hi, 0), (w.hi, act_lo, 1), (w.lo, act_hi, 2)):
            for t in range(2):
                last = nc.tensor.matmul(out[:, t], part[:, s, k], act[:, k, t * HALF:(t + 1) * HALF],
                                        start=(k == 0 and flag == 0), stop=(k == NC - 1 and flag == 2))
    return last


def norm_first(nc, A, C, xn_hi, xn_lo):
    with ExitStack() as ctx:
        sb = lambda n, s, d=F32: ctx.enter_context(nc.sbuf_tensor(n, s, d))
        sem = lambda n: ctx.enter_context(nc.semaphore(n))
        x = sb("n1_x", [P, NB, D])
        junk = sb("n1_junk", [P, D])
        ss = sb("n1_ss", [P, NB])
        rs = sb("n1_rs", [P, NB])
        rstd = sb("n1_rstd", [P, NB])
        ps = ctx.enter_context(nc.psum_tensor("n1_ps", [P, 2, 2, HALF], F32))
        x_in = [sem(f"n1_x_in{b}") for b in range(NB // 2)]
        consts_in, squared, rooted, inverted, scaled, turned, high, low = (
            sem(f"n1_{n}") for n in ("consts_in", "squared", "rooted", "inverted", "scaled", "turned", "high", "low"))
        made = sem("n1_consts_made")
        filled = sem("n1_consts_filled")
        with nc.Block() as block:
            @block.sync
            def _(sp):
                sp.dma_start(C.cols[:], A["cols"]).then_inc(consts_in, 16)
                for b in range(NB // 2):
                    sp.dma_start(x[:, 2 * b:2 * b + 2], A["x"][2 * b:2 * b + 2].rearrange("b p d -> p b d")).then_inc(x_in[b], 16)
                sp.dma_start(C.up[:], A["up"]).then_inc(consts_in, 16)

            @block.gpsimd
            def _(pool):
                nc.gpsimd.memset(C.ident[:], 0.0).then_inc(filled, 1)
                nc.gpsimd.memset(C.ones[:], 1.0).then_inc(filled, 1)
                nc.gpsimd.memset(C.mask[:], 1.0).then_inc(filled, 1)
                nc.gpsimd.memset(C.eps[:], EPS).then_inc(C.begun, 1)
                pool.wait_ge(filled, 3)
                nc.gpsimd.affine_select(out=C.ident[:], in_=C.ident[:], compare_op=ALU.not_equal, fill=1.0, base=0,
                                        pattern=[[-1, P]], channel_multiplier=1).then_inc(made, 1)
                nc.gpsimd.affine_select(out=C.mask[:, 0], in_=C.mask[:, 0], compare_op=ALU.is_ge, fill=0.0, base=0,
                                        pattern=[[1, P]], channel_multiplier=-1).then_inc(made, 1)
                nc.gpsimd.affine_select(out=C.mask[:, 1], in_=C.mask[:, 1], compare_op=ALU.is_ge, fill=0.0, base=0,
                                        pattern=[[-1, P]], channel_multiplier=1).then_inc(made, 1)
                pool.wait_ge(made, 3)
                nc.gpsimd.memset(C.mask[0:CH, 0, CH:P], 0.0).then_inc(made, 1)
                nc.gpsimd.memset(C.mask[CH:P, 1, 0:CH], 0.0).then_inc(made, 1)

            @block.scalar
            def _(act):
                act.wait_ge(C.begun, 1)
                for b in range(NB):
                    act.wait_ge(x_in[b // 2], 16)
                    if b:
                        act.wait_ge(squared, b)
                    nc.scalar.activation(junk[:], x[:, b], ACT.Square, accum_out=ss[:, b:b + 1]).then_inc(squared, 1)
                act.wait_ge(squared, NB)
                nc.scalar.activation(rs[:], ss[:], ACT.Sqrt, bias=C.eps[:, 0:1], scale=1.0 / D).then_inc(rooted, 1)
                act.wait_ge(consts_in, 32)
                for c in range(NC):
                    act.wait_ge(turned, c + 1)
                    nc.scalar.mul(xn_hi[:, c], ps[:, c % 2].rearrange("p a b -> p (a b)"), C.norm1_g(c)).then_inc(high, 1)

            @block.vector
            def _(dve):
                dve.wait_ge(rooted, 1)
                nc.vector.reciprocal(rstd[:], rs[:]).then_inc(inverted, 1)
                dve.wait_ge(inverted, 1)
                for b in range(NB):
                    nc.vector.tensor_scalar(x[:, b], x[:, b], rstd[:, b:b + 1], None, ALU.mult).then_inc(scaled, 1)
                for c in range(NC):
                    dve.wait_ge(high, c + 1)
                    nc.vector.scalar_tensor_tensor(out=xn_lo[:, c], in0=ps[:, c % 2].rearrange("p a b -> p (a b)"), scalar=C.norm1_g(c),
                                                   in1=xn_hi[:, c].bitcast(F32), op0=ALU.mult, op1=ALU.subtract).then_inc(low, 1)

            @block.tensor
            def _(pe):
                pe.wait_ge(made, 5)
                for c in range(NC):
                    if c >= 2:
                        pe.wait_ge(low, c - 1)
                    for b in range(NB):
                        if c == 0:
                            pe.wait_ge(scaled, b + 1)
                        last = nc.tensor.transpose(ps[:, c % 2, b // 4, (b % 4) * P:(b % 4 + 1) * P], x[:, b, c * P:(c + 1) * P], C.ident[:])
                    last.then_inc(turned, 1)


def gla_inputs(nc, A, C, xn_hi, xn_lo, qk, v, bcum):
    with ExitStack() as ctx:
        sb = lambda n, s, d=F32: ctx.enter_context(nc.sbuf_tensor(n, s, d))
        sem = lambda n: ctx.enter_context(nc.semaphore(n))
        w = Weights(ctx, nc, "g")
        z = sb("gi_z", [P, T])
        keep = sb("gi_keep", [P, 2, T], mybir.dt.bfloat16)
        kept = sem("gi_kept")
        ps = ctx.enter_context(nc.psum_tensor("gi_ps", [P, 4, 2, HALF], F32))
        soft = v[:, :].rearrange("p h b e -> p (h b e)")[:, 0:2 * NH * T].rearrange("p (d h t) -> p d h t", d=2, h=NH)
        z_out, up_done, up_out, exped, logged, clipped, summed, out_ = (
            sem(f"gi_{n}") for n in ("z_out", "up_done", "up_out", "exped", "logged", "clipped", "summed", "out"))
        absed = sem("gi_absed")
        v_done, v_out = sem("gi_v_done"), sem("gi_v_out")
        n_qk = 1 + 2 * NH
        n_chunks = n_qk + 2 * NH
        with nc.Block() as block:
            @block.sync
            def _(sp):
                load_weights(sp, w, A["stream_g"], 0, n_chunks)

            @block.gpsimd
            def _(pool):
                nc.gpsimd.memset(keep[:], 1.0).then_inc(kept, 1)
                pool.wait_ge(kept, 1)
                for d, at in ((0, 0), (1, CH - 1)):
                    nc.gpsimd.memset(keep[:, d].rearrange("p (n c) -> p n c", c=CH)[:, :, at:at + 1], 0.0).then_inc(kept, 1)
                split_weights(nc, pool, C, w, n_qk - 1)
                pool.wait_ge(w.used, n_qk - 2)
                split_chunk(nc, pool, C, w, 0, n_qk - 1, 16 * (n_qk + 1) // 2)
                pool.wait_ge(w.used, n_qk - 1)
                split_chunk(nc, pool, C, w, 1, n_qk, 16 * (n_qk + 1) // 2)
                pool.wait_ge(w.used, n_qk)
                split_chunk(nc, pool, C, w, 0, n_qk + 1, 16 * (n_qk + 3) // 2)
                with pool.Fori(1, NH) as h:
                    pool.wait_ge(v_done, h * 4)
                    split_chunk(nc, pool, C, w, 1, h * 2 + n_qk, h * 16 + 16 * (n_qk + 1) // 2)
                    split_chunk(nc, pool, C, w, 0, h * 2 + n_qk + 1, h * 16 + 16 * (n_qk + 3) // 2)

            @block.tensor
            def _(pe):
                pe.wait_ge(w.split, 1)
                project(nc, w, 0, xn_hi, xn_lo, ps[:, 0]).then_inc(w.used, 1)
                pe.wait_ge(z_out, 1)
                for n in range(2 * NH):
                    d, h = n // NH, n % NH
                    if n >= 2:
                        pe.wait_ge(absed, n - 1)
                    for t in range(2):
                        last = nc.tensor.matmul(ps[:, 2 + n % 2, t], C.up[32 * d:32 * d + RANK, h * DK:(h + 1) * DK],
                                                z[32 * d:32 * d + RANK, t * HALF:(t + 1) * HALF], start=True, stop=True)
                    last.then_inc(up_done, 1)
                with pe.Fori(0, NH) as h:
                    for s in range(2):
                        pe.wait_ge(w.split, h * 2 + (2 + s))
                        pe.wait_ge(out_, h * 2 + s)
                        project(nc, w, 1 - s, xn_hi, xn_lo, ps[:, s]).then_inc(w.used, 1)
                pe.wait_ge(out_, 2 * NH)
                with pe.Fori(0, NH) as h:
                    pe.wait_ge(w.split, h * 2 + (n_qk + 2))
                    for b in range(NB):
                        if b % 2 == 0:
                            pe.wait_ge(v_out, h * 4 + b // 2)
                        for k in range(NC):
                            for i, (a, part) in enumerate(((xn_hi, w.hi), (xn_lo, w.hi), (xn_hi, w.lo))):
                                last = nc.tensor.matmul(
                                    ps[:, b // 4, (b // 2) % 2, (b % 2) * DV:(b % 2 + 1) * DV].rearrange("p (a m) -> p a m", a=2),
                                    a[:, k, b * P:(b + 1) * P], part[:, :, k], start=(b % 2 == 0 and k == 0 and i == 0),
                                    stop=(b % 2 == 1 and k == NC - 1 and i == 2), skip_group_check=True)
                        if b % 2:
                            last.then_inc(v_done, 1)

            @block.scalar
            def _(act):
                act.wait_ge(w.used, 1)
                nc.scalar.copy(z[:], ps[:, 0].rearrange("p a b -> p (a b)")).then_inc(z_out, 1)
                for n in range(2 * NH):
                    act.wait_ge(up_out, n + 1)
                    nc.scalar.activation(soft[:, n // NH, n % NH], ps[:, 2 + n % 2].rearrange("p a b -> p (a b)"), ACT.Abs,
                                         bias=C.decay_bias(n // NH, n % NH)).then_inc(absed, 1)
                act.wait_ge(absed, 2 * NH)
                nc.scalar.activation(soft, soft, ACT.Exp, scale=-1.0).then_inc(exped, 1)
                act.wait_ge(exped, 1)
                nc.scalar.activation(soft, soft, ACT.Ln, bias=1.0).then_inc(logged, 1)
                with act.Fori(0, NH) as h:
                    for s in range(2):
                        act.wait_ge(w.used, h * 2 + (s + 2))
                        C.settle(act, "act")
                        nc.scalar.mul(qk[:, bass.ds(h * 2 + s, 1)].rearrange("p o t -> p (o t)"), ps[:, s].rearrange("p a b -> p (a b)"),
                                      1.0 if s == 0 else DK ** -0.5).then_inc(out_, 1)
                act.wait_ge(summed, 2 * NH)
                with act.Fori(0, NH) as h:
                    for g in range(4):
                        act.wait_ge(v_done, h * 4 + (g + 1))
                        C.settle(act, "act")
                        nc.scalar.copy(v[:, bass.ds(h, 1), 2 * g:2 * g + 2].rearrange("p o b e -> p (o b e)"),
                                       ps[:, g // 2, g % 2]).then_inc(v_out, 1)

            @block.vector
            def _(dve):
                for n in range(2 * NH):
                    d, h = n // NH, n % NH
                    dve.wait_ge(up_done, n + 1)
                    y = ps[:, 2 + n % 2].rearrange("p a b -> p (a b)")
                    nc.vector.tensor_scalar(bcum[:, d, h], y, C.decay_bias(d, h), 0.0, ALU.add, ALU.min).then_inc(up_out, 1)
                dve.wait_ge(logged, 1)
                dve.wait_ge(kept, 3)
                dve.wait_ge(up_out, 2 * NH)
                for n in range(2 * NH):
                    d, h = n // NH, n % NH
                    nc.vector.tensor_tensor(soft[:, d, h], bcum[:, d, h], soft[:, d, h], ALU.subtract).then_inc(clipped, 1)
                    dve.wait_ge(clipped, n + 1)
                    way = slice(None) if d == 0 else slice(None, None, -1)
                    nc.vector.tensor_tensor_scan(out=bcum[:, d, h, way], data0=keep[:, d, way], data1=soft[:, d, h, way],
                                                 initial=0.0, op0=ALU.mult, op1=ALU.add).then_inc(summed, 1)


def gla(nc, A, C, qk, v, bcum):
    with ExitStack() as ctx:
        sb = lambda n, s, d=F32: ctx.enter_context(nc.sbuf_tensor(n, s, d))
        sem = lambda n: ctx.enter_context(nc.semaphore(n))
        qki = sb("gl_qk_in", [P, 2, T])
        q_dec = sb("gl_q_dec", [P, T])
        k_end = sb("gl_k_end", [P, T])
        k_tok = sb("gl_k_tok", [P, NB, DK])
        sc = sb("gl_sc", [P, 2, NB, P])
        v_h = sb("gl_v_h", [P, NB, DV])
        state = sb("gl_state", [P, 4, DV])
        dec = sb("gl_dec", [P, 2, NCH])
        o_ps = ctx.enter_context(nc.psum_tensor("gl_o", [P, NE, 2, HALF], F32))
        sc_ps = ctx.enter_context(nc.psum_tensor("gl_sc_ps", [P, 2, 4, P], F32))
        u_ps = ctx.enter_context(nc.psum_tensor("gl_u_ps", [P, 2, HALF], F32))[:, :, 0:DV]
        (d1, d2, ex_q, ex_k, ex_end, ex_dec, ex_last, m_in, m_end, m_dec, v_in, scored, masked, turned, tok, u_done, s_done,
         inter, intra, sq, ssum, rooted, inv, o_out, zeroed) = (sem(f"gl_{n}") for n in (
             "diff", "end_diff", "exp_q", "exp_k", "exp_end", "exp_dec", "exp_last", "in_ready", "end_ready", "dec_ready", "v_copied",
             "scored", "masked", "turned", "tok_ready", "u_done", "state_ready", "inter_done", "intra_done", "squared",
             "sq_summed", "rooted", "inverted", "o_out", "zeroed"))

        def chunked(ap):
            return ap.rearrange("p (n c) -> p n c", c=CH)

        def head(tile, h):
            return tile[:, bass.ds(h, 1)].rearrange("p o t -> p (o t)")

        def sums(d, h):
            return bcum[:, d, bass.ds(h, 1)].rearrange("p o t -> p (o t)")

        def at(d, h, i):
            return chunked(sums(d, h))[:, :, i:i + 1].to_broadcast([P, NCH, CH])

        REF = (CH // 2, CH - 1 - CH // 2)
        LAST = (CH - 1, 0)
        US = NCH - 1
        with nc.Block() as block:
            @block.vector
            def _(dve):
                nc.vector.memset(sc[:], 0.0).then_inc(zeroed, 1)
                dve.wait_ge(zeroed, 1)
                with dve.Fori(0, NH) as h:
                    for d in range(2):
                        n = h * 2 + d
                        dve.wait_ge(scored, n * 2)
                        if d == 0:
                            dve.wait_ge(ssum, h)
                        nc.vector.tensor_tensor(chunked(qki[:, 1]), chunked(sums(d, h)), at(d, h, REF[d]), ALU.subtract).then_inc(d1, 1)
                        dve.wait_ge(ex_q, n + 1)
                        nc.vector.tensor_tensor(qki[:, 1], qki[:, 1], head(qk, h * 2 + 1), ALU.mult).then_inc(m_in, 1)
                        dve.wait_ge(ex_k, n + 1)
                        nc.vector.tensor_tensor(qki[:, 0], qki[:, 0], head(qk, h * 2), ALU.mult).then_inc(m_in, 1)
                        for g in range(2):
                            dve.wait_ge(scored, n * 2 + (g + 1))
                            if g == 0:
                                dve.wait_ge(intra, n)
                            C.settle(dve, "dve")
                            nc.vector.copy_predicated(sc[:, d, 4 * g:4 * g + 4], C.mask[:, d:d + 1].to_broadcast([P, 4, P]).bitcast(U32),
                                                      sc_ps[:, g]).then_inc(masked, 1)
                        dve.wait_ge(ex_last, n + 1)
                        for i in range(US):
                            c = i if d == 0 else NCH - 1 - i
                            dve.wait_ge(u_done, n * US + (i + 1))
                            if i < 4:
                                dve.wait_ge(inter, n * US)
                            else:
                                dve.wait_ge(inter, n * US + (i - 3))
                            if i == 0:
                                nc.vector.tensor_copy(state[:, 0], u_ps[:, 0]).then_inc(s_done, 1)
                            else:
                                dve.wait_ge(s_done, n * US + i)
                                nc.vector.scalar_tensor_tensor(out=state[:, i % 4], in0=state[:, (i - 1) % 4], scalar=dec[:, d, c:c + 1],
                                                               in1=u_ps[:, i % 2], op0=ALU.mult, op1=ALU.add).then_inc(s_done, 1)
                    dve.wait_ge(rooted, h + 1)
                    nc.vector.reciprocal(k_end[:], k_end[:]).then_inc(inv, 1)
                    dve.wait_ge(inv, h + 1)
                    dve.wait_ge(m_dec, h * 2 + 2)
                    dve.wait_ge(m_end, h * 2 + 2)
                    for e in range(NE):
                        nc.vector.tensor_tensor(head(qk, h * 2 + e), o_ps[:, e].rearrange("p a b -> p (a b)"), k_end[:], ALU.mult).then_inc(o_out, 1)

            @block.gpsimd
            def _(pool):
                with pool.Fori(0, NH) as h:
                    pool.wait_ge(inter, h * (2 * US))
                    C.settle(pool, "pool")
                    nc.gpsimd.tensor_copy(v_h[:], v[:, bass.ds(h, 1)].rearrange("p o b e -> p (o b) e")).then_inc(v_in, 1)
                    for d in range(2):
                        n = h * 2 + d
                        pool.wait_ge(turned, n * 2)
                        if d == 0:
                            pool.wait_ge(o_out, h * NE)
                        C.settle(pool, "pool")
                        nc.gpsimd.tensor_tensor(chunked(k_end[:]), at(d, h, LAST[d]), chunked(sums(d, h)), ALU.subtract).then_inc(d2, 1)
                        pool.wait_ge(ex_end, n + 1)
                        C.settle(pool, "pool")
                        nc.gpsimd.tensor_tensor(k_end[:], k_end[:], head(qk, h * 2), ALU.mult).then_inc(m_end, 1)
                        pool.wait_ge(ex_dec, n + 1)
                        C.settle(pool, "pool")
                        nc.gpsimd.tensor_tensor(q_dec[:], q_dec[:], head(qk, h * 2 + 1), ALU.mult).then_inc(m_dec, 1)

            @block.scalar
            def _(act):
                with act.Fori(0, NH) as h:
                    for d in range(2):
                        n = h * 2 + d
                        act.wait_ge(d1, n + 1)
                        nc.scalar.activation(qki[:, 0], qki[:, 1], ACT.Exp, scale=-1.0 / TAU).then_inc(ex_k, 1)
                        act.wait_ge(ex_k, n + 1)
                        nc.scalar.activation(qki[:, 1], qki[:, 1], ACT.Exp, scale=1.0 / TAU).then_inc(ex_q, 1)
                        act.wait_ge(d2, n + 1)
                        nc.scalar.activation(k_end[:], k_end[:], ACT.Exp, scale=1.0 / TAU).then_inc(ex_end, 1)
                        act.wait_ge(s_done, n * US)
                        C.settle(act, "act")
                        nc.scalar.activation(dec[:, d].rearrange("p (n o) -> p n o", o=1), chunked(sums(d, h))[:, :, LAST[d]:LAST[d] + 1],
                                             ACT.Exp, scale=1.0 / TAU).then_inc(ex_last, 1)
                        act.wait_ge(inter, n * US)
                        C.settle(act, "act")
                        nc.scalar.activation(q_dec[:], sums(d, h), ACT.Exp, scale=1.0 / TAU).then_inc(ex_dec, 1)
                        for g in range(2):
                            act.wait_ge(turned, n * 2 + (g + 1))
                            if g == 0:
                                act.wait_ge(u_done, n * US)
                            nc.scalar.copy(k_tok[:, 4 * g:4 * g + 4], sc_ps[:, g]).then_inc(tok, 1)
                    act.wait_ge(inter, h * (2 * US) + 2 * US)
                    for e in range(NE):
                        nc.scalar.activation(qki[:, e], o_ps[:, e].rearrange("p a b -> p (a b)"), ACT.Square).then_inc(sq, 1)
                    act.wait_ge(ssum, h + 1)
                    nc.scalar.activation(k_end[:], sc_ps[:].rearrange("p a b c -> p (a b c)"), ACT.Sqrt, bias=C.eps[:, 0:1], scale=1.0 / DV).then_inc(rooted, 1)

            @block.tensor
            def _(pe):
                with pe.Fori(0, NH) as h:
                    pe.wait_ge(v_in, h + 1)
                    for d in range(2):
                        n = h * 2 + d
                        pe.wait_ge(m_in, n * 2 + 2)
                        if d == 0:
                            pe.wait_ge(rooted, h)
                        else:
                            pe.wait_ge(tok, h * 4 + 2)
                        for b in range(NB):
                            m = nc.tensor.matmul(sc_ps[:, b // 4, b % 4], qki[:, 0, b * P:(b + 1) * P], qki[:, 1, b * P:(b + 1) * P],
                                                 start=(b % 4 == 0), stop=(b % 4 == 3), skip_group_check=True)
                            if b % 4 == 3:
                                m.then_inc(scored, 1)
                        pe.wait_ge(m_end, n + 1)
                        for g in range(2):
                            pe.wait_ge(masked, n * 2 + (g + 1))
                            for b in range(4):
                                m = nc.tensor.transpose(sc_ps[:, g, b], k_end[:, (4 * g + b) * P:(4 * g + b + 1) * P], C.ident[:])
                            m.then_inc(turned, 1)
                        pe.wait_ge(masked, n * 2 + 2)
                        if d == 0:
                            pe.wait_ge(o_out, h * NE)
                        for b in range(NB):
                            for e in range(NE):
                                m = nc.tensor.matmul(o_ps[:, e, b // 4, (b % 4) * P:(b % 4 + 1) * P], v_h[:, b, e * P:(e + 1) * P],
                                                     sc[:, d, b], start=(d == 0 and b % 4 == 0), stop=False, skip_group_check=True)
                        m.then_inc(intra, 1)
                        pe.wait_ge(tok, n * 2 + 2)
                        pe.wait_ge(m_dec, n + 1)

                        def update(i):
                            c = i if d == 0 else NCH - 1 - i
                            rows = slice((c % 2) * CH, (c % 2 + 1) * CH)
                            pe.wait_ge(s_done, n * US + max(i - 1, 0))
                            nc.tensor.matmul(u_ps[:, i % 2], k_tok[rows, c // 2], v_h[rows, c // 2], start=True, stop=True,
                                             skip_group_check=True).then_inc(u_done, 1)

                        update(0)
                        for i in range(US):
                            if i + 1 < US:
                                update(i + 1)
                            c = i + 1 if d == 0 else NCH - 2 - i
                            pe.wait_ge(s_done, n * US + (i + 1))
                            for e in range(NE):
                                m = nc.tensor.matmul(o_ps[:, e, c // 8, (c % 8) * CH:(c % 8 + 1) * CH], state[:, i % 4, e * P:(e + 1) * P],
                                                     q_dec[:, c * CH:(c + 1) * CH], start=False, stop=False, skip_group_check=True)
                            m.then_inc(inter, 1)
                    pe.wait_ge(tok, h * 4 + 4)
                    for e in range(NE):
                        pe.wait_ge(sq, h * NE + (e + 1))
                        for t in range(2):
                            m = nc.tensor.matmul(sc_ps[:, t].rearrange("p a b -> p (a b)"), C.ones[:], qki[:, e, t * HALF:(t + 1) * HALF],
                                                 start=(e == 0), stop=(e == NE - 1), skip_group_check=True)
                    m.then_inc(ssum, 1)


def gla_gate(nc, A, C, xn_hi, xn_lo, o, on_hi, on_lo):
    with ExitStack() as ctx:
        sb = lambda n, s, d=F32: ctx.enter_context(nc.sbuf_tensor(n, s, d))
        sem = lambda n: ctx.enter_context(nc.semaphore(n))
        w = Weights(ctx, nc, "r")
        gated = sb("gg_gated", [P, 2, T])
        ps = ctx.enter_context(nc.psum_tensor("gg_ps", [P, 2, 2, HALF], F32))
        silu, mixed, high, low = (sem(f"gg_{n}") for n in ("silu", "mixed", "high", "low"))
        with nc.Block() as block:
            @block.sync
            def _(sp):
                load_weights(sp, w, A["stream_r"], 0, NC)

            @block.gpsimd
            def _(pool):
                split_weights(nc, pool, C, w, NC)

            @block.tensor
            def _(pe):
                with pe.Fori(0, NC // 2) as i:
                    for s in range(2):
                        pe.wait_ge(w.split, i * 2 + (s + 1))
                        pe.wait_ge(silu, i * 2)
                        project(nc, w, s, xn_hi, xn_lo, ps[:, s]).then_inc(w.used, 1)

            @block.scalar
            def _(act):
                with act.Fori(0, NC // 2) as i:
                    for s in range(2):
                        act.wait_ge(w.used, i * 2 + (s + 1))
                        act.wait_ge(low, i * 2)
                        nc.scalar.activation(gated[:, s], ps[:, s].rearrange("p a b -> p (a b)"), ACT.Silu).then_inc(silu, 1)
                    for s in range(2):
                        act.wait_ge(mixed, i * 2 + (s + 1))
                        C.settle(act, "act")
                        nc.scalar.copy(chunk(on_hi, i * 2 + s), gated[:, s]).then_inc(high, 1)

            @block.vector
            def _(dve):
                with dve.Fori(0, NC // 2) as i:
                    for s in range(2):
                        dve.wait_ge(silu, i * 2 + (s + 1))
                        nc.vector.scalar_tensor_tensor(out=gated[:, s], in0=chunk(o, i * 2 + s), scalar=C.col(16, i * 2 + s),
                                                       in1=gated[:, s], op0=ALU.mult, op1=ALU.mult).then_inc(mixed, 1)
                    for s in range(2):
                        dve.wait_ge(high, i * 2 + (s + 1))
                        nc.vector.tensor_tensor(chunk(on_lo, i * 2 + s), gated[:, s], chunk(on_hi, i * 2 + s).bitcast(F32),
                                                ALU.subtract).then_inc(low, 1)


def chunk(tile, c):
    return tile[:, bass.ds(c, 1)].rearrange("p o t -> p (o t)")


def branch(nc, A, C, tag, stream, bias, act_hi, act_lo, xn_hi, xn_lo, m, add):
    with ExitStack() as ctx:
        sb = lambda n, s, d=F32: ctx.enter_context(nc.sbuf_tensor(n, s, d))
        sem = lambda n: ctx.enter_context(nc.semaphore(n))
        w = Weights(ctx, nc, tag)
        gate = sb(f"{tag}_gate", [P, 2, T])
        ps = ctx.enter_context(nc.psum_tensor(f"{tag}_ps", [P, 2, 2, 2, HALF], F32))
        gated, product = (sem(f"{tag}_{n}") for n in ("gated", "product"))
        mixed = sem(f"{tag}_mixed") if add else product
        flat = lambda ap: ap.rearrange("p a b -> p (a b)")
        with nc.Block() as block:
            @block.sync
            def _(sp):
                load_weights(sp, w, A[stream], 0, 2 * NC)

            @block.gpsimd
            def _(pool):
                split_weights(nc, pool, C, w, 2 * NC)

            @block.tensor
            def _(pe):
                with pe.Fori(0, NC // 2) as i:
                    for s in range(2):
                        pe.wait_ge(gated, i * 2)
                        pe.wait_ge(w.split, i * 4 + (2 * s + 1))
                        project(nc, w, 0, xn_hi, xn_lo, ps[:, s, 0]).then_inc(w.used, 1)
                        pe.wait_ge(w.split, i * 4 + (2 * s + 2))
                        pe.wait_ge(product, i * 2)
                        project(nc, w, 1, act_hi, act_lo, ps[:, s, 1]).then_inc(w.used, 1)

            @block.scalar
            def _(act):
                with act.Fori(0, NC // 2) as i:
                    for s in range(2):
                        act.wait_ge(w.used, i * 4 + (2 * s + 1))
                        act.wait_ge(mixed, i * 2)
                        C.settle(act, "act")
                        nc.scalar.activation(gate[:, s], flat(ps[:, s, 0]), ACT.Sigmoid, bias=C.col(bias, i * 2 + s)).then_inc(gated, 1)

            @block.vector
            def _(dve):
                with dve.Fori(0, NC // 2) as i:
                    for s in range(2):
                        dve.wait_ge(w.used, i * 4 + (2 * s + 2))
                        dve.wait_ge(gated, i * 2 + (s + 1))
                        if not add:
                            nc.vector.tensor_tensor(chunk(m, i * 2 + s), flat(ps[:, s, 1]), gate[:, s], ALU.mult).then_inc(product, 1)
                        else:
                            nc.vector.tensor_tensor(gate[:, s], flat(ps[:, s, 1]), gate[:, s], ALU.mult).then_inc(product, 1)
                            dve.wait_ge(product, i * 2 + (s + 1))
                            nc.vector.tensor_tensor(chunk(m, i * 2 + s), chunk(m, i * 2 + s), gate[:, s], ALU.add).then_inc(mixed, 1)


def conv(nc, A, C, xn_hi, xn_lo, y_hi, y_lo):
    with ExitStack() as ctx:
        sb = lambda n, s, d=F32: ctx.enter_context(nc.sbuf_tensor(n, s, d))
        sem = lambda n: ctx.enter_context(nc.semaphore(n))
        w = Weights(ctx, nc, "c")
        ca = sb("cv_ca", [P, T])
        u = sb("cv_u", [P, T + 2])
        y = sb("cv_y", [P, T])
        ps = ctx.enter_context(nc.psum_tensor("cv_ps", [P, 3, 2, HALF], F32))
        ca_out, padded, u_done, step, y_done, high, low = (sem(f"cv_{n}") for n in ("ca_out", "padded", "u_done", "step", "y_done", "high", "low"))
        flat = lambda ap: ap.rearrange("p a b -> p (a b)")
        with nc.Block() as block:
            @block.sync
            def _(sp):
                load_weights(sp, w, A["stream_conv"], 0, 3 * NC)

            @block.gpsimd
            def _(pool):
                split_weights(nc, pool, C, w, 3 * NC)

            @block.tensor
            def _(pe):
                with pe.Fori(0, NC // 2) as i:
                    for n in range(6):
                        pe.wait_ge(w.split, i * 6 + (n + 1))
                        pe.wait_ge((ca_out, u_done, y_done)[n % 3], i * 2 + n // 3)
                        project(nc, w, n % 2, xn_hi, xn_lo, ps[:, n % 3]).then_inc(w.used, 1)

            @block.scalar
            def _(act):
                with act.Fori(0, NC // 2) as i:
                    for s in range(2):
                        act.wait_ge(w.used, i * 6 + (3 * s + 1))
                        act.wait_ge(u_done, i * 2 + s)
                        nc.scalar.copy(ca[:], flat(ps[:, 0])).then_inc(ca_out, 1)
                        act.wait_ge(y_done, i * 2 + (s + 1))
                        C.settle(act, "act")
                        nc.scalar.copy(chunk(y_hi, i * 2 + s), y[:]).then_inc(high, 1)

            @block.vector
            def _(dve):
                nc.vector.memset(u[:, 0:1], 0.0).then_inc(padded, 1)
                nc.vector.memset(u[:, T + 1:T + 2], 0.0).then_inc(padded, 1)
                dve.wait_ge(padded, 2)
                with dve.Fori(0, NC // 2) as i:
                    for s in range(2):
                        c = i * 2 + s
                        dve.wait_ge(w.used, i * 6 + (3 * s + 2))
                        dve.wait_ge(ca_out, c + 1)
                        nc.vector.tensor_tensor(u[:, 1:T + 1], flat(ps[:, 1]), ca[:], ALU.mult).then_inc(u_done, 1)
                        dve.wait_ge(u_done, c + 1)
                        nc.vector.tensor_scalar(y[:], u[:, 0:T], C.col(24, c), C.col(48, c), ALU.mult, ALU.add).then_inc(step, 1)
                        dve.wait_ge(step, c * 3 + 1)
                        nc.vector.scalar_tensor_tensor(out=y[:], in0=u[:, 1:T + 1], scalar=C.col(32, c), in1=y[:], op0=ALU.mult, op1=ALU.add).then_inc(step, 1)
                        dve.wait_ge(step, c * 3 + 2)
                        nc.vector.scalar_tensor_tensor(out=y[:], in0=u[:, 2:T + 2], scalar=C.col(40, c), in1=y[:], op0=ALU.mult, op1=ALU.add).then_inc(step, 1)
                        dve.wait_ge(step, c * 3 + 3)
                        dve.wait_ge(w.used, i * 6 + (3 * s + 3))
                        nc.vector.tensor_tensor(y[:], flat(ps[:, 2]), y[:], ALU.mult).then_inc(y_done, 1)
                        dve.wait_ge(high, c + 1)
                        nc.vector.tensor_tensor(chunk(y_lo, c), y[:], chunk(y_hi, c).bitcast(F32), ALU.subtract).then_inc(low, 1)
                        dve.wait_ge(low, c + 1)


def refine_rstd(nc, dve, sem, done, rstd, root, ss, tmp, n):
    def link(ins):
        done[0] += 1
        ins.then_inc(sem, 1)
        dve.wait_ge(sem, done[0])

    link(nc.vector.reciprocal(rstd, root))
    link(nc.vector.tensor_scalar(tmp, ss, 1.0 / n, EPS, ALU.mult, ALU.add))
    link(nc.vector.tensor_tensor(tmp, tmp, rstd, ALU.mult))
    link(nc.vector.tensor_tensor(tmp, tmp, rstd, ALU.mult))
    link(nc.vector.tensor_scalar(tmp, tmp, -0.5, 1.5, ALU.mult, ALU.add))
    link(nc.vector.tensor_tensor(rstd, rstd, tmp, ALU.mult))


def out_project(nc, A, C, m, x2, ss):
    with ExitStack() as ctx:
        sb = lambda n, s, d=F32: ctx.enter_context(nc.sbuf_tensor(n, s, d))
        sem = lambda n: ctx.enter_context(nc.semaphore(n))
        raw = sb("op_raw", [P, 2, D])
        w_hi, w_lo = sb("op_w_hi", [P, NC, D], F32R), sb("op_w_lo", [P, NC, D], F32R)
        m_hi, m_lo = sb("op_m_hi", [P, 2, NC, P], F32R), sb("op_m_lo", [P, 2, NC, P], F32R)
        x = sb("op_x", [P, 2, D])
        junk = sb("op_junk", [P, D])
        ps = ctx.enter_context(nc.psum_tensor("op_ps", [P, 2, 2, HALF], F32))
        w_in = [sem(f"op_w_in{s}") for s in range(2)]
        x_in = [sem(f"op_x_in{s}") for s in range(2)]
        w_high, w_split, m_high, m_split, made, added, squared = (
            sem(f"op_{n}") for n in ("w_high", "w_split", "m_high", "m_split", "made", "added", "squared"))
        with nc.Block() as block:
            @block.sync
            def _(sp):
                for k in range(NC):
                    if k >= 2:
                        sp.wait_ge(w_split, k - 1)
                    sp.dma_start(raw[:, k % 2], A["w_out"][k]).then_inc(w_in[k % 2], 16)
                for b in range(NB):
                    if b >= 2:
                        sp.wait_ge(added, b - 1)
                    sp.dma_start(x[:, b % 2], A["x"][b]).then_inc(x_in[b % 2], 16)

            @block.gpsimd
            def _(pool):
                for b in range(NB):
                    pool.wait_ge(m_high, b + 1)
                    nc.gpsimd.tensor_tensor(m_lo[:, b % 2], m[:, :, b * P:(b + 1) * P], m_hi[:, b % 2].bitcast(F32), ALU.subtract).then_inc(m_split, 1)

            @block.scalar
            def _(act):
                def split_m(b):
                    if b >= 2:
                        act.wait_ge(made, b - 1)
                    nc.scalar.copy(m_hi[:, b % 2], m[:, :, b * P:(b + 1) * P]).then_inc(m_high, 1)

                split_m(0)
                split_m(1)
                for k in range(NC):
                    act.wait_ge(w_in[k % 2], 16 * (k // 2 + 1))
                    nc.scalar.copy(w_hi[:, k], raw[:, k % 2]).then_inc(w_high, 1)
                for b in range(NB):
                    if b + 2 < NB:
                        split_m(b + 2)
                    act.wait_ge(added, b + 1)
                    if b:
                        act.wait_ge(squared, b)
                    nc.scalar.activation(junk[:], x2[:, b], ACT.Square, accum_out=ss[:, b:b + 1]).then_inc(squared, 1)

            @block.tensor
            def _(pe):
                for b in range(NB):
                    pe.wait_ge(m_split, b + 1)
                    if b >= 2:
                        pe.wait_ge(added, b - 1)
                    for k in range(NC):
                        if b == 0:
                            pe.wait_ge(w_split, k + 1)
                        for i, (a, part) in enumerate(((m_hi, w_hi), (m_hi, w_lo), (m_lo, w_hi))):
                            for t in range(2):
                                last = nc.tensor.matmul(ps[:, b % 2, t], a[:, b % 2, k], part[:, k, t * HALF:(t + 1) * HALF],
                                                        start=(k == 0 and i == 0), stop=(k == NC - 1 and i == 2))
                    last.then_inc(made, 1)

            @block.vector
            def _(dve):
                for k in range(NC):
                    dve.wait_ge(w_high, k + 1)
                    nc.vector.tensor_tensor(w_lo[:, k], raw[:, k % 2], w_hi[:, k].bitcast(F32), ALU.subtract).then_inc(w_split, 1)
                for b in range(NB):
                    dve.wait_ge(made, b + 1)
                    dve.wait_ge(x_in[b % 2], 16 * (b // 2 + 1))
                    nc.vector.tensor_tensor(x2[:, b], ps[:, b % 2].rearrange("p a b -> p (a b)"), x[:, b % 2], ALU.add).then_inc(added, 1)


def norm_second(nc, A, C, x2, ss, rstd, xt_hi, xt_lo):
    with ExitStack() as ctx:
        sb = lambda n, s, d=F32: ctx.enter_context(nc.sbuf_tensor(n, s, d))
        sem = lambda n: ctx.enter_context(nc.semaphore(n))
        root = sb("n2_root", [P, NB])
        g2 = sb("n2_g", [P, D])
        tmp = sb("n2_tmp", [P, NB])
        xt = sb("n2_xt", [P, 2, D])
        ps = ctx.enter_context(nc.psum_tensor("n2_ps", [P, 2, NC, P], F32))
        rows_in, rooted, link, scaled, turned, high, low = (sem(f"n2_{n}") for n in ("rows_in", "rooted", "link", "scaled", "turned", "high", "low"))
        with nc.Block() as block:
            @block.sync
            def _(sp):
                sp.dma_start(g2[:], A["norm2_g"].to_broadcast([P, D])).then_inc(rows_in, 16)

            @block.scalar
            def _(act):
                nc.scalar.activation(root[:], ss[:], ACT.Sqrt, bias=C.eps[:, 0:1], scale=1.0 / D).then_inc(rooted, 1)
                for b in range(NB):
                    act.wait_ge(turned, b + 1)
                    nc.scalar.copy(xt_hi[:, :, b * P:(b + 1) * P], ps[:, b % 2]).then_inc(high, 1)

            @block.tensor
            def _(pe):
                for b in range(NB):
                    pe.wait_ge(scaled, b + 1)
                    if b >= 2:
                        pe.wait_ge(low, b - 1)
                    for c in range(NC):
                        last = nc.tensor.transpose(ps[:, b % 2, c], xt[:, b % 2, c * P:(c + 1) * P], C.ident[:])
                    last.then_inc(turned, 1)

            @block.vector
            def _(dve):
                dve.wait_ge(rooted, 1)
                refine_rstd(nc, dve, link, [0], rstd[:], root[:], ss[:], tmp[:], D)
                dve.wait_ge(rows_in, 16)

                def scale(b):
                    if b >= 2:
                        dve.wait_ge(turned, b - 1)
                    nc.vector.scalar_tensor_tensor(out=xt[:, b % 2], in0=x2[:, b], scalar=rstd[:, b:b + 1], in1=g2[:],
                                                   op0=ALU.mult, op1=ALU.mult).then_inc(scaled, 1)

                scale(0)
                for b in range(NB):
                    if b + 1 < NB:
                        scale(b + 1)
                    dve.wait_ge(high, b + 1)
                    nc.vector.tensor_tensor(xt_lo[:, :, b * P:(b + 1) * P], ps[:, b % 2], xt_hi[:, :, b * P:(b + 1) * P].bitcast(F32),
                                            ALU.subtract).then_inc(low, 1)


def key_scores(nc, A, C, xt_hi, xt_lo, scores):
    with ExitStack() as ctx:
        sb = lambda n, s, d=F32: ctx.enter_context(nc.sbuf_tensor(n, s, d))
        sem = lambda n: ctx.enter_context(nc.semaphore(n))
        w = Weights(ctx, nc, "q")
        keys = sb("ks_keys", [P, 2 * PH, NKEYS])
        q = sb("ks_q", [P, 2, T])
        q_ps = ctx.enter_context(nc.psum_tensor("ks_q_ps", [P, 2, 2, HALF], F32))
        s_ps = ctx.enter_context(nc.psum_tensor("ks_s_ps", [P, 2, NB, NKEYS], F32))
        keys_in, q_out, made, s_out = (sem(f"ks_{n}") for n in ("keys_in", "q_out", "made", "s_out"))
        with nc.Block() as block:
            @block.sync
            def _(sp):
                sp.dma_start(keys[:], A["keys"]).then_inc(keys_in, 16)
                load_weights(sp, w, A["stream_q"], 0, 2 * PH)

            @block.gpsimd
            def _(pool):
                split_weights(nc, pool, C, w, 2 * PH)

            @block.tensor
            def _(pe):
                pe.wait_ge(keys_in, 16)
                with pe.Fori(0, PH) as h:
                    for s in range(2):
                        pe.wait_ge(w.split, h * 2 + (s + 1))
                        pe.wait_ge(q_out, h * 2)
                        project(nc, w, s, xt_hi, xt_lo, q_ps[:, s]).then_inc(w.used, 1)
                    for s in range(2):
                        pe.wait_ge(q_out, h * 2 + (s + 1))
                        pe.wait_ge(s_out, h * 2)
                        for b in range(NB):
                            last = nc.tensor.matmul(s_ps[:, s, b], q[:, s, b * P:(b + 1) * P], chunk(keys, h * 2 + s),
                                                    start=(b % 4 == 0), stop=(b % 4 == 3), skip_group_check=True)
                        last.then_inc(made, 1)

            @block.scalar
            def _(act):
                with act.Fori(0, PH) as h:
                    for s in range(2):
                        act.wait_ge(w.used, h * 2 + (s + 1))
                        act.wait_ge(made, h * 2)
                        nc.scalar.copy(q[:, s], q_ps[:, s].rearrange("p a b -> p (a b)")).then_inc(q_out, 1)

            @block.vector
            def _(dve):
                with dve.Fori(0, PH) as h:
                    for s in range(2):
                        dve.wait_ge(made, h * 2 + (s + 1))
                        nc.vector.tensor_copy(scores[:, :, bass.ds(h * 2 + s, 1)].rearrange("p b o k -> p b (o k)"), s_ps[:, s]).then_inc(s_out, 1)


def choose(nc, A, C, scores, experts, gates):
    with ExitStack() as ctx:
        sb = lambda n, s, d=F32: ctx.enter_context(nc.sbuf_tensor(n, s, d))
        sem = lambda n: ctx.enter_context(nc.semaphore(n))
        s0 = sb("ch_s0", [P, 2 * PH, NKEYS])
        s1 = sb("ch_s1", [P, 2 * PH, NKEYS])
        top = sb("ch_top", [P, 2 * PH, TOPK])
        topi = sb("ch_topi", [P, 2 * PH, TOPK], U32)
        topf = sb("ch_topf", [P, 2 * PH, TOPK])
        cand = sb("ch_cand", [P, PH, TOPK, TOPK])
        cand1 = sb("ch_cand1", [P, PH, TOPK, TOPK])
        best = sb("ch_best", [P, PH, TOPK])
        besti = sb("ch_besti", [P, PH, TOPK], U32)
        where = sb("ch_where", [P, 2, PH, TOPK], U32)
        wheref = sb("ch_wheref", [P, 2, PH, TOPK])
        half = sb("ch_half", [P, 2, PH, TOPK])
        iota = sb("ch_iota", [P, TOPK])
        shifted = sb("ch_shifted", [P, PH, TOPK])
        raised = sb("ch_raised", [P, PH, TOPK])
        total = sb("ch_total", [P, PH])
        link_, less, exped, counted = (sem(f"ch_{n}") for n in ("link", "less", "exped", "counted"))
        with nc.Block() as block:
            @block.gpsimd
            def _(pool):
                nc.gpsimd.iota(iota[:], [[1, TOPK]], base=0, channel_multiplier=0, allow_small_or_imprecise_dtypes=True).then_inc(counted, 1)

            @block.scalar
            def _(act):
                with act.Fori(0, NB) as b:
                    act.wait_ge(less, b + 1)
                    nc.scalar.activation(raised[:], shifted[:], ACT.Exp).then_inc(exped, 1)

            @block.vector
            def _(dve):
                dve.wait_ge(counted, 1)
                with dve.Fori(0, NB) as b:
                    steps = [0]
                    LINKS = 18

                    def link(ins):
                        steps[0] += 1
                        ins.then_inc(link_, 1)
                        dve.wait_ge(link_, b * LINKS + steps[0])
                        C.settle(dve, "dve")

                    def top16(source, rest, values, indices, n):
                        for at in range(2):
                            src = source if at == 0 else rest
                            for c in range(n):
                                ins = nc.vector.max(values(c, at), src(c))
                            link(ins)
                            for c in range(n):
                                ins = nc.vector.max_index(indices(c, at), values(c, at), src(c))
                            if at == 0:
                                for c in range(n):
                                    ins = nc.vector.match_replace(rest(c), values(c, at), src(c), NEG)
                            link(ins)

                    link(nc.vector.tensor_copy(s0[:], scores[:, bass.ds(b, 1)].rearrange("p o c k -> p (o c) k")))
                    top16(lambda c: s0[:, c], lambda c: s1[:, c], lambda c, a: top[:, c, 8 * a:8 * a + 8],
                          lambda c, a: topi[:, c, 8 * a:8 * a + 8], 2 * PH)
                    nc.vector.tensor_copy(topf[:], topi[:])
                    for h in range(PH):
                        ins = nc.vector.tensor_tensor(cand[:, h], top[:, 2 * h].unsqueeze(2).to_broadcast([P, TOPK, TOPK]),
                                                      top[:, 2 * h + 1:2 * h + 2].to_broadcast([P, TOPK, TOPK]), ALU.add)
                    link(ins)
                    flat = lambda t: lambda h: t[:, h].rearrange("p a b -> p (a b)")
                    top16(flat(cand), flat(cand1), lambda h, a: best[:, h, 8 * a:8 * a + 8], lambda h, a: besti[:, h, 8 * a:8 * a + 8], PH)
                    nc.vector.tensor_scalar(where[:, 0], besti[:], 4, None, ALU.logical_shift_right)
                    link(nc.vector.tensor_scalar(where[:, 1], besti[:], TOPK - 1, None, ALU.bitwise_and))
                    nc.vector.tensor_tensor(shifted[:], best[:], best[:, :, 0:1].to_broadcast([P, PH, TOPK]), ALU.subtract).then_inc(less, 1)
                    link(nc.vector.tensor_copy(wheref[:], where[:]))
                    for side, hit in ((0, cand), (1, cand1)):
                        for h in range(PH):
                            ins = nc.vector.tensor_tensor(hit[:, h], wheref[:, side, h].unsqueeze(2).to_broadcast([P, TOPK, TOPK]),
                                                          iota[:].unsqueeze(1).to_broadcast([P, TOPK, TOPK]), ALU.is_equal)
                    link(ins)
                    for side, hit in ((0, cand), (1, cand1)):
                        for h in range(PH):
                            ins = nc.vector.tensor_tensor(hit[:, h], hit[:, h], topf[:, 2 * h + side:2 * h + side + 1].to_broadcast([P, TOPK, TOPK]), ALU.mult)
                    link(ins)
                    for side, hit in ((0, cand), (1, cand1)):
                        ins = nc.vector.tensor_reduce(half[:, side], hit[:], AX.X, ALU.add)
                    link(ins)
                    nc.vector.scalar_tensor_tensor(out=experts[:, bass.ds(b, 1)].rearrange("p o (h k) -> p (o h) k", h=PH), in0=half[:, 0],
                                                   scalar=float(NKEYS), in1=half[:, 1], op0=ALU.mult, op1=ALU.add)
                    dve.wait_ge(exped, b + 1)
                    link(nc.vector.tensor_reduce(total[:], raised[:], AX.X, ALU.add))
                    link(nc.vector.reciprocal(total[:], total[:]))
                    link(nc.vector.tensor_tensor(gates[:, bass.ds(b, 1)].rearrange("p o (h k) -> p (o h) k", h=PH), raised[:],
                                                 total[:].unsqueeze(2).to_broadcast([P, PH, TOPK]), ALU.mult))
                    assert steps[0] == LINKS, steps[0]


def peer(nc, A, C, x2, rstd, experts, gates, out):
    with ExitStack() as ctx:
        sb = lambda n, s, d=F32: ctx.enter_context(nc.sbuf_tensor(n, s, d))
        sem = lambda n: ctx.enter_context(nc.semaphore(n))
        ring = sb("pe_ring", [P, RING, D])
        xt = sb("pe_xt", [P, D])
        junk = sb("pe_junk", [P, 2, D])
        index = sb("pe_index", [P, 2, TOPK], U32)
        hidden = sb("pe_hidden", [P, 2, TOPK])
        active = sb("pe_active", [P, SLOTS])
        weight = sb("pe_weight", [P, SLOTS])
        acc = sb("pe_acc", [P, 2, D])
        y = sb("pe_y", [P, D])
        ss = sb("pe_ss", [P, 1])
        root = sb("pe_root", [P, 1])
        rf = sb("pe_rf", [P, 1])
        tmp = sb("pe_tmp", [P, 1])
        res = sb("pe_res", [P, D])
        g2, gf = sb("pe_g2", [P, D]), sb("pe_gf", [P, D])
        rows_in = sem("pe_rows_in")
        ring_in = [sem(f"pe_ring_in{s}") for s in range(RING)]
        used, indexed, gelued, xt_ready, link_, squared, rooted, normed, stored, zeroed = (
            sem(f"pe_{n}") for n in ("used", "indexed", "gelued", "xt_ready", "link", "squared", "rooted", "normed", "stored", "zeroed"))
        CREDIT = 2 * RING
        UNITS = 2 * PH
        with nc.Block() as block:
            @block.gpsimd
            def _(pool):
                with pool.Fori(0, NB) as b:
                    for side, table in ((0, A["peer_u"]), (1, A["peer_v"])):
                        with pool.Fori(0, PH // 2) as i:
                            for p in range(2):
                                g = b * UNITS + i * 2 + (side * PH + p)
                                for s in range(RING):
                                    if s == 0:
                                        pool.wait_ge(indexed, g + 1)
                                    pool.wait_ge(used, g * RING + (s + 1 + CREDIT - RING))
                                    C.settle(pool, "pool")
                                    nc.gpsimd.indirect_dma_start(ring[:, s], None, table, bass.IndirectOffsetOnAxis(index[:, p, s:s + 1], 0)
                                                                 ).then_inc(ring_in[s], 16)

            @block.scalar
            def _(act):
                act.wait_ge(used, CREDIT)
                with act.Fori(0, NB) as b:
                    for side in range(2):
                        with act.Fori(0, PH // 2) as i:
                            for p in range(2):
                                g = b * UNITS + i * 2 + (side * PH + p)
                                act.wait_ge(used, g * RING + (CREDIT - RING))
                                C.settle(act, "act")
                                nc.scalar.copy(index[:, p], experts[:, bass.ds(b, 1), bass.ds((i * 2 + p) * TOPK, TOPK)].rearrange("q o k -> q (o k)")).then_inc(indexed, 1)
                                if side == 0:
                                    act.wait_ge(used, g * RING + (CREDIT + RING))
                                    C.settle(act, "act")
                                    nc.scalar.activation(active[:, bass.ds((i * 2 + p) * TOPK, TOPK)], hidden[:, p], ACT.Gelu).then_inc(gelued, 1)
                    act.wait_ge(link_, b * 11 + 3)
                    nc.scalar.activation(junk[:, 0], y[:], ACT.Square, accum_out=ss[:]).then_inc(squared, 1)
                    act.wait_ge(squared, b + 1)
                    nc.scalar.activation(root[:], ss[:], ACT.Sqrt, bias=C.eps[:, 0:1], scale=1.0 / D).then_inc(rooted, 1)

            @block.vector
            def _(dve):
                nc.vector.memset(ss[:], 0.0).then_inc(used, CREDIT)
                dve.wait_ge(rows_in, 32)
                with dve.Fori(0, NB) as b:
                    row = x2[:, bass.ds(b, 1)].rearrange("p o d -> p (o d)")
                    dve.wait_ge(squared, b)
                    nc.vector.memset(acc[:], 0.0).then_inc(zeroed, 1)
                    nc.vector.scalar_tensor_tensor(out=xt[:], in0=row, scalar=rstd[:, bass.ds(b, 1)], in1=g2[:], op0=ALU.mult, op1=ALU.mult).then_inc(xt_ready, 1)
                    dve.wait_ge(xt_ready, b + 1)
                    C.settle(dve, "dve")
                    with dve.Fori(0, PH // 2) as i:
                        for p in range(2):
                            g = b * UNITS + i * 2 + p
                            dve.wait_ge(gelued, b * PH + i * 2)
                            for s in range(RING):
                                dve.wait_ge(ring_in[s], g * 16 + 16)
                                if s >= 2:
                                    dve.wait_ge(used, g * RING + (CREDIT + s - 1))
                                else:
                                    dve.wait_ge(used, g * RING + CREDIT)
                                nc.vector.tensor_tensor_reduce(out=junk[:, s % 2], in0=ring[:, s], in1=xt[:], scale=1.0, scalar=0.0, op0=ALU.mult,
                                                               op1=ALU.add, accum_out=hidden[:, p, s:s + 1]).then_inc(used, 1)
                    dve.wait_ge(gelued, (b + 1) * PH)
                    steps = [0]

                    def link(ins):
                        steps[0] += 1
                        ins.then_inc(link_, 1)
                        dve.wait_ge(link_, b * 11 + steps[0])

                    link(nc.vector.tensor_tensor(weight[:], active[:], gates[:, bass.ds(b, 1)].rearrange("p o k -> p (o k)"), ALU.mult))
                    dve.wait_ge(zeroed, b + 1)
                    C.settle(dve, "dve")
                    with dve.Fori(0, PH // 2) as i:
                        for p in range(2):
                            g = b * UNITS + i * 2 + (PH + p)
                            for s in range(RING):
                                dve.wait_ge(ring_in[s], g * 16 + 16)
                                dve.wait_ge(used, g * RING + (CREDIT + s - 1) if s else g * RING + (CREDIT - 1))
                                nc.vector.scalar_tensor_tensor(out=acc[:, s % 2], in0=ring[:, s], scalar=weight[:, bass.ds((i * 2 + p) * TOPK + s, 1)],
                                                               in1=acc[:, s % 2], op0=ALU.mult, op1=ALU.add).then_inc(used, 1)
                    dve.wait_ge(used, (b + 1) * (UNITS * RING) + CREDIT)
                    link(nc.vector.tensor_tensor(y[:], acc[:, 0], acc[:, 1], ALU.add))
                    link(nc.vector.tensor_tensor(y[:], y[:], row, ALU.add))
                    dve.wait_ge(rooted, b + 1)
                    link(nc.vector.reciprocal(rf[:], root[:]))
                    link(nc.vector.tensor_scalar(tmp[:], ss[:], 1.0 / D, EPS, ALU.mult, ALU.add))
                    link(nc.vector.tensor_tensor(tmp[:], tmp[:], rf[:], ALU.mult))
                    link(nc.vector.tensor_tensor(tmp[:], tmp[:], rf[:], ALU.mult))
                    link(nc.vector.tensor_scalar(tmp[:], tmp[:], -0.5, 1.5, ALU.mult, ALU.add))
                    link(nc.vector.tensor_tensor(rf[:], rf[:], tmp[:], ALU.mult))
                    dve.wait_ge(stored, b * 16)
                    link(nc.vector.scalar_tensor_tensor(out=res[:], in0=y[:], scalar=rf[:], in1=gf[:], op0=ALU.mult, op1=ALU.mult))
                    link(nc.vector.memset(tmp[:], 0.0))
                    assert steps[0] == 11, steps[0]

            @block.sync
            def _(sp):
                sp.dma_start(g2[:], A["norm2_g"].to_broadcast([P, D])).then_inc(rows_in, 16)
                sp.dma_start(gf[:], A["final_g"].to_broadcast([P, D])).then_inc(rows_in, 16)
                with sp.Fori(0, NB) as b:
                    sp.wait_ge(link_, b * 11 + 10)
                    sp.dma_start(out[bass.ds(b * P, P)], res[:]).then_inc(stored, 16)
                sp.wait_ge(stored, 16 * NB)


def build(nc, A, out):
    with ExitStack() as ctx:
        C = Consts(ctx, nc)

        def sb(c, n, shape, d=F32, side=None):
            return c.enter_context(nc.sbuf_tensor(n, shape, d, side=side) if side else nc.sbuf_tensor(n, shape, d))

        with ExitStack() as mixer:
            m = sb(mixer, "qk_then_o_then_m", [P, NC, T])
            with ExitStack() as normed:
                xn_hi, xn_lo = sb(normed, "xn_hi", [P, NC, T], F32R), sb(normed, "xn_lo", [P, NC, T], F32R)
                norm_first(nc, A, C, xn_hi, xn_lo)
                with ExitStack() as g:
                    v = sb(g, "v", [P, NH, NB, DV])
                    bcum = sb(g, "bcum", [P, 2, NH, T])
                    gla_inputs(nc, A, C, xn_hi, xn_lo, m, v, bcum)
                    gla(nc, A, C, m, v, bcum)
                with ExitStack() as g:
                    hi, lo = sb(g, "branch_hi", [P, NC, T], F32R), sb(g, "branch_lo", [P, NC, T], F32R)
                    gla_gate(nc, A, C, xn_hi, xn_lo, m, hi, lo)
                    branch(nc, A, C, "bb", "stream_b", 64, hi, lo, xn_hi, xn_lo, m, False)
                    conv(nc, A, C, xn_hi, xn_lo, hi, lo)
                    branch(nc, A, C, "ba", "stream_a", 56, hi, lo, xn_hi, xn_lo, m, True)
            x2 = sb(ctx, "x2", [P, NB, D], side="right")
            ss, rstd = sb(ctx, "ss2", [P, NB], side="right"), sb(ctx, "rstd2", [P, NB], side="right")
            out_project(nc, A, C, m, x2, ss)
        scored = ctx.enter_context(ExitStack())
        scores = sb(scored, "scores", [P, NB, 2 * PH, NKEYS], side="right")
        with ExitStack() as t:
            xt_hi, xt_lo = sb(t, "xt_hi", [P, NC, T], F32R), sb(t, "xt_lo", [P, NC, T], F32R)
            norm_second(nc, A, C, x2, ss, rstd, xt_hi, xt_lo)
            key_scores(nc, A, C, xt_hi, xt_lo, scores)
        experts, gates = sb(ctx, "experts", [P, NB, SLOTS], U32), sb(ctx, "gates", [P, NB, SLOTS])
        choose(nc, A, C, scores, experts, gates)
        scored.close()
        peer(nc, A, C, x2, rstd, experts, gates, out)


def feature_chunks(w):
    return w.reshape(NC, P, w.shape[1] // P, P).transpose(2, 1, 0, 3)


def kernel(**inputs):
    import concourse.bacc as bacc
    from concourse.bass_utils import run_bass_kernel_spmd

    I = {k: np.asarray(a) for k, a in inputs.items()}
    one = lambda k: I[k][0]
    cut = np.cumsum([D, D, D, NH * DK, NH * DK, D, D, RANK, RANK, D, D])[:-1]
    xa, ba, ca, q, k, v, r, zf, zb, ga, gb = np.split(one("w_in"), cut, axis=1)
    z = np.zeros((D, P), np.float32)
    z[:, 0:RANK], z[:, 32:32 + RANK] = zf, zb
    up = np.zeros((P, NH * DK), np.float32)
    up[0:RANK], up[32:32 + RANK] = one("decay_up_f"), one("decay_up_b")
    pairs = lambda *ws: np.stack([feature_chunks(w) for w in ws], 1).reshape(-1, P, NC, P)
    col = lambda a: a.reshape(-1, P).T
    cols = np.concatenate([col(one("norm1_g")), col(one("decay_bias_f")), col(one("decay_bias_b")), col(one("gla_norm_g")),
                           col(one("conv_w")), col(one("conv_b")), col(one("gate_bias"))], 1)
    arrays = {
        "x": I["x"].reshape(NB, P, D),
        "cols": cols,
        "up": up,
        "stream_g": np.concatenate([feature_chunks(z), pairs(k, q), feature_chunks(v).reshape(NH, 2, P, NC, P)[:, ::-1].reshape(-1, P, NC, P)]),
        "stream_r": feature_chunks(r),
        "stream_b": pairs(gb, one("wb_proj")),
        "stream_conv": pairs(ca, xa, ba),
        "stream_a": pairs(ga, one("wa_proj")),
        "w_out": one("w_out").reshape(NC, P, D),
        "stream_q": feature_chunks(one("peer_wq")),
        "keys": one("peer_keys").reshape(2 * PH, NKEYS, P).transpose(2, 0, 1),
        "norm2_g": I["norm2_g"].reshape(1, D),
        "final_g": I["final_norm_g"].reshape(1, D),
        "peer_u": one("peer_u"),
        "peer_v": one("peer_v"),
    }
    arrays = {n: np.ascontiguousarray(a) for n, a in arrays.items()}
    nc = bacc.Bacc("TRN2", target_bir_lowering=False, num_devices=1)
    A = {n: nc.dram_tensor(f"in_{n}", a.shape, mybir.dt.from_np(a.dtype), kind="ExternalInput").ap() for n, a in arrays.items()}
    out = nc.dram_tensor("out_x", (T, D), F32, kind="ExternalOutput").ap()
    build(nc, A, out)
    r = run_bass_kernel_spmd(nc, [{f"in_{n}": a for n, a in arrays.items()}], core_ids=[0])
    return np.asarray(r.results[0]["out_x"]).reshape(1, T, D)


class Consts:
    NCOL = 72

    def __init__(self, ctx, nc):
        sb = lambda n, s, d=F32: ctx.enter_context(nc.sbuf_tensor(n, s, d))
        self.cols = sb("c_cols", [P, self.NCOL])
        self.up = sb("c_up", [P, NH * DK])
        self.ident = sb("c_ident", [P, P])
        self.ones = sb("c_ones", [P, P])
        self.mask = sb("c_mask", [P, 2, P])
        self.eps = sb("c_eps", [P, 1])
        self.begun = ctx.enter_context(nc.semaphore("c_begun"))
        self.passed = {e: ctx.enter_context(nc.semaphore(f"c_passed_{e}")) for e in ("act", "dve", "pool")}

    def settle(self, engine, name):
        engine.sem_inc(self.passed[name], 1)

    def col(self, first, c):
        return self.cols[:, bass.ds(c + first, 1)]

    def norm1_g(self, c):
        return self.cols[:, c:c + 1]

    def decay_bias(self, d, h):
        return self.cols[:, 8 + 4 * d + h:9 + 4 * d + h]
```

```python
import numpy as np
import concourse.bass as bass
from concourse import mybir
from contextlib import ExitStack

F32 = mybir.dt.float32
F32R = mybir.dt.float32r
U32 = mybir.dt.uint32
ALU = mybir.AluOpType
ACT = mybir.ActivationFunctionType
AX = mybir.AxisListType

P = 128
T = 1024
D = 1024
NB = T // P
NC = D // P
HALF = 512
NH = 4
DK = 128
DV = 256
NE = DV // P
CH = 64
NCH = T // CH
RANK = 16
TAU = 16.0
EPS = 1e-6
PH = 8
NKEYS = 128
TOPK = 16
SLOTS = PH * TOPK
RING = 8
DB = 4
DT = DB * P
GROUP = 4
NEG = -3.4e38

S_Z, S_KQ, S_V, S_R, S_BG, S_CONV, S_AG = 0, 1, 9, 17, 25, 41, 65


class Semaphores:

    def __init__(self, nc):
        self.nc, self.taken = nc, []

    def __call__(self, name):
        self.taken.append(self.nc.alloc_semaphore(name))
        return self.taken[-1]

    def __enter__(self):
        return self

    def __exit__(self, *error):
        if error[0] is None:
            self.nc.clear_and_free_semaphores(self.taken)
            self.nc.all_engine_barrier()


class Weights:

    def __init__(self, ctx, nc, sem, tag):
        self.raw = ctx.enter_context(nc.sbuf_tensor(f"w_raw_{tag}", [P, 2, NC, P], F32))
        self.hi = ctx.enter_context(nc.sbuf_tensor(f"w_hi_{tag}", [P, 2, NC, P], F32R))
        self.lo = ctx.enter_context(nc.sbuf_tensor(f"w_lo_{tag}", [P, 2, NC, P], F32R))
        self.loaded = [sem(f"w_loaded{s}_{tag}") for s in range(2)]
        self.high, self.split, self.used = sem(f"w_high_{tag}"), sem(f"w_split_{tag}"), sem(f"w_used_{tag}")


def load_weights(sp, w, stream, first, count):
    for s in range(2):
        sp.dma_start(w.raw[:, s], stream[first + s]).then_inc(w.loaded[s], 16)
    with sp.Fori(1, count // 2) as i:
        for s in range(2):
            sp.wait_ge(w.split, i * 2 + s - 1)
            sp.dma_start(w.raw[:, s], stream[bass.ds(i * 2 + (first + s), 1)].rearrange("o p k m -> (o p) k m")).then_inc(w.loaded[s], 16)
    if count % 2:
        sp.wait_ge(w.split, count - 2)
        sp.dma_start(w.raw[:, 0], stream[first + count - 1]).then_inc(w.loaded[0], 16)


def split_chunk(nc, pool, C, w, s, n, loaded16):
    pool.wait_ge(w.loaded[s], loaded16)
    C.settle(pool, "pool")
    nc.gpsimd.tensor_copy(w.hi[:, s], w.raw[:, s]).then_inc(w.high, 1)
    pool.wait_ge(w.high, n + 1)
    nc.gpsimd.tensor_tensor(w.lo[:, s], w.raw[:, s], w.hi[:, s].bitcast(F32), ALU.subtract).then_inc(w.split, 1)


def split_weights(nc, pool, C, w, count):
    for s in range(2):
        split_chunk(nc, pool, C, w, s, s, 16)
    with pool.Fori(1, count // 2) as i:
        for s in range(2):
            pool.wait_ge(w.used, i * 2 + s - 1)
            split_chunk(nc, pool, C, w, s, i * 2 + s, i * 16 + 16)


def project(nc, w, s, act_hi, act_lo, out):
    last = None
    for k in range(NC):
        for part, act, flag in ((w.hi, act_hi, 0), (w.hi, act_lo, 1), (w.lo, act_hi, 2)):
            for t in range(2):
                last = nc.tensor.matmul(out[:, t], part[:, s, k], half_of(act, t)[:, k],
                                        start=(k == 0 and flag == 0), stop=(k == NC - 1 and flag == 2))
    return last


def half_of(act, t):
    return act[t] if isinstance(act, tuple) else act[:, :, t * HALF:(t + 1) * HALF]


def norm_first(nc, A, C, xn_hi, xn_lo):
    with ExitStack() as ctx:
        sb = lambda n, s, d=F32: ctx.enter_context(nc.sbuf_tensor(n, s, d))
        sem = ctx.enter_context(Semaphores(nc))
        x = sb("n1_x", [P, NB, D])
        junk = sb("n1_junk", [P, D])
        ss = sb("n1_ss", [P, NB])
        rs = sb("n1_rs", [P, NB])
        rstd = sb("n1_rstd", [P, NB])
        ps = ctx.enter_context(nc.psum_tensor("n1_ps", [P, 2, 2, HALF], F32))
        x_in = [sem(f"n1_x_in{b}") for b in range(NB // 2)]
        consts_in, squared, rooted, inverted, scaled, turned, high, low = (
            sem(f"n1_{n}") for n in ("consts_in", "squared", "rooted", "inverted", "scaled", "turned", "high", "low"))
        made = sem("n1_consts_made")
        filled = sem("n1_consts_filled")
        with nc.Block() as block:
            @block.sync
            def _(sp):
                sp.dma_start(C.cols[:], A["cols"]).then_inc(consts_in, 16)
                for b in range(NB // 2):
                    sp.dma_start(x[:, 2 * b:2 * b + 2], A["x"][2 * b:2 * b + 2].rearrange("b p d -> p b d")).then_inc(x_in[b], 16)
                sp.dma_start(C.up[:], A["up"]).then_inc(consts_in, 16)

            @block.gpsimd
            def _(pool):
                nc.gpsimd.memset(C.ident[:], 0.0).then_inc(filled, 1)
                nc.gpsimd.memset(C.ones[:], 1.0).then_inc(filled, 1)
                nc.gpsimd.memset(C.mask[:], 1.0).then_inc(filled, 1)
                nc.gpsimd.memset(C.eps[:], EPS).then_inc(C.begun, 1)
                pool.wait_ge(filled, 3)
                nc.gpsimd.affine_select(out=C.ident[:], in_=C.ident[:], compare_op=ALU.not_equal, fill=1.0, base=0,
                                        pattern=[[-1, P]], channel_multiplier=1).then_inc(made, 1)
                nc.gpsimd.affine_select(out=C.mask[:, 0], in_=C.mask[:, 0], compare_op=ALU.is_ge, fill=0.0, base=0,
                                        pattern=[[1, P]], channel_multiplier=-1).then_inc(made, 1)
                nc.gpsimd.affine_select(out=C.mask[:, 1], in_=C.mask[:, 1], compare_op=ALU.is_ge, fill=0.0, base=0,
                                        pattern=[[-1, P]], channel_multiplier=1).then_inc(made, 1)
                pool.wait_ge(made, 3)
                nc.gpsimd.memset(C.mask[0:CH, 0, CH:P], 0.0).then_inc(made, 1)
                nc.gpsimd.memset(C.mask[CH:P, 1, 0:CH], 0.0).then_inc(made, 1)

            @block.scalar
            def _(act):
                act.wait_ge(C.begun, 1)
                for b in range(NB):
                    act.wait_ge(x_in[b // 2], 16)
                    if b:
                        act.wait_ge(squared, b)
                    nc.scalar.activation(junk[:], x[:, b], ACT.Square, accum_out=ss[:, b:b + 1]).then_inc(squared, 1)
                act.wait_ge(squared, NB)
                nc.scalar.activation(rs[:], ss[:], ACT.Sqrt, bias=C.eps[:, 0:1], scale=1.0 / D).then_inc(rooted, 1)
                act.wait_ge(consts_in, 32)
                for c in range(NC):
                    act.wait_ge(turned, c + 1)
                    nc.scalar.mul(xn_hi[:, c], ps[:, c % 2].rearrange("p a b -> p (a b)"), C.norm1_g(c)).then_inc(high, 1)

            @block.vector
            def _(dve):
                dve.wait_ge(rooted, 1)
                nc.vector.reciprocal(rstd[:], rs[:]).then_inc(inverted, 1)
                dve.wait_ge(inverted, 1)
                for b in range(NB):
                    nc.vector.tensor_scalar(x[:, b], x[:, b], rstd[:, b:b + 1], None, ALU.mult).then_inc(scaled, 1)
                for c in range(NC):
                    dve.wait_ge(high, c + 1)
                    nc.vector.scalar_tensor_tensor(out=xn_lo[:, c], in0=ps[:, c % 2].rearrange("p a b -> p (a b)"), scalar=C.norm1_g(c),
                                                   in1=xn_hi[:, c].bitcast(F32), op0=ALU.mult, op1=ALU.subtract).then_inc(low, 1)

            @block.tensor
            def _(pe):
                pe.wait_ge(made, 5)
                for c in range(NC):
                    if c >= 2:
                        pe.wait_ge(low, c - 1)
                    for b in range(NB):
                        if c == 0:
                            pe.wait_ge(scaled, b + 1)
                        last = nc.tensor.transpose(ps[:, c % 2, b // 4, (b % 4) * P:(b % 4 + 1) * P], x[:, b, c * P:(c + 1) * P], C.ident[:])
                    last.then_inc(turned, 1)


def gla_inputs(nc, A, C, xn_hi, xn_lo, qk, v, bcum):
    with ExitStack() as ctx:
        sb = lambda n, s, d=F32: ctx.enter_context(nc.sbuf_tensor(n, s, d))
        sem = ctx.enter_context(Semaphores(nc))
        w = Weights(ctx, nc, sem, "g")
        z = sb("gi_z", [P, T])
        keep = sb("gi_keep", [P, 2, T], mybir.dt.bfloat16)
        kept = sem("gi_kept")
        ps = ctx.enter_context(nc.psum_tensor("gi_ps", [P, 4, 2, HALF], F32))
        soft = v[:, :].rearrange("p h b e -> p (h b e)")[:, 0:2 * NH * T].rearrange("p (d h t) -> p d h t", d=2, h=NH)
        z_out, up_done, up_out, exped, logged, clipped, summed, out_ = (
            sem(f"gi_{n}") for n in ("z_out", "up_done", "up_out", "exped", "logged", "clipped", "summed", "out"))
        absed = sem("gi_absed")
        v_done, v_out = sem("gi_v_done"), sem("gi_v_out")
        n_qk = 1 + 2 * NH
        n_chunks = n_qk + 2 * NH
        with nc.Block() as block:
            @block.sync
            def _(sp):
                load_weights(sp, w, A["stream_g"], 0, n_chunks)

            @block.gpsimd
            def _(pool):
                nc.gpsimd.memset(keep[:], 1.0).then_inc(kept, 1)
                pool.wait_ge(kept, 1)
                for d, at in ((0, 0), (1, CH - 1)):
                    nc.gpsimd.memset(keep[:, d].rearrange("p (n c) -> p n c", c=CH)[:, :, at:at + 1], 0.0).then_inc(kept, 1)
                split_weights(nc, pool, C, w, n_qk - 1)
                pool.wait_ge(w.used, n_qk - 2)
                split_chunk(nc, pool, C, w, 0, n_qk - 1, 16 * (n_qk + 1) // 2)
                pool.wait_ge(w.used, n_qk - 1)
                split_chunk(nc, pool, C, w, 1, n_qk, 16 * (n_qk + 1) // 2)
                pool.wait_ge(w.used, n_qk)
                split_chunk(nc, pool, C, w, 0, n_qk + 1, 16 * (n_qk + 3) // 2)
                with pool.Fori(1, NH) as h:
                    pool.wait_ge(v_done, h * 4)
                    split_chunk(nc, pool, C, w, 1, h * 2 + n_qk, h * 16 + 16 * (n_qk + 1) // 2)
                    split_chunk(nc, pool, C, w, 0, h * 2 + n_qk + 1, h * 16 + 16 * (n_qk + 3) // 2)

            @block.tensor
            def _(pe):
                pe.wait_ge(w.split, 1)
                project(nc, w, 0, xn_hi, xn_lo, ps[:, 0]).then_inc(w.used, 1)
                pe.wait_ge(z_out, 1)
                for n in range(2 * NH):
                    d, h = n // NH, n % NH
                    if n >= 2:
                        pe.wait_ge(absed, n - 1)
                    for t in range(2):
                        last = nc.tensor.matmul(ps[:, 2 + n % 2, t], C.up[32 * d:32 * d + RANK, h * DK:(h + 1) * DK],
                                                z[32 * d:32 * d + RANK, t * HALF:(t + 1) * HALF], start=True, stop=True)
                    last.then_inc(up_done, 1)
                with pe.Fori(0, NH) as h:
                    for s in range(2):
                        pe.wait_ge(w.split, h * 2 + (2 + s))
                        pe.wait_ge(out_, h * 2 + s)
                        project(nc, w, 1 - s, xn_hi, xn_lo, ps[:, s]).then_inc(w.used, 1)
                pe.wait_ge(out_, 2 * NH)
                with pe.Fori(0, NH) as h:
                    pe.wait_ge(w.split, h * 2 + (n_qk + 2))
                    for b in range(NB):
                        if b % 2 == 0:
                            pe.wait_ge(v_out, h * 4 + b // 2)
                        for k in range(NC):
                            for i, (a, part) in enumerate(((xn_hi, w.hi), (xn_lo, w.hi), (xn_hi, w.lo))):
                                last = nc.tensor.matmul(
                                    ps[:, b // 4, (b // 2) % 2, (b % 2) * DV:(b % 2 + 1) * DV].rearrange("p (a m) -> p a m", a=2),
                                    a[:, k, b * P:(b + 1) * P], part[:, :, k], start=(b % 2 == 0 and k == 0 and i == 0),
                                    stop=(b % 2 == 1 and k == NC - 1 and i == 2), skip_group_check=True)
                        if b % 2:
                            last.then_inc(v_done, 1)

            @block.scalar
            def _(act):
                act.wait_ge(w.used, 1)
                nc.scalar.copy(z[:], ps[:, 0].rearrange("p a b -> p (a b)")).then_inc(z_out, 1)
                for n in range(2 * NH):
                    act.wait_ge(up_out, n + 1)
                    nc.scalar.activation(soft[:, n // NH, n % NH], ps[:, 2 + n % 2].rearrange("p a b -> p (a b)"), ACT.Abs,
                                         bias=C.decay_bias(n // NH, n % NH)).then_inc(absed, 1)
                act.wait_ge(absed, 2 * NH)
                nc.scalar.activation(soft, soft, ACT.Exp, scale=-1.0).then_inc(exped, 1)
                act.wait_ge(exped, 1)
                nc.scalar.activation(soft, soft, ACT.Ln, bias=1.0).then_inc(logged, 1)
                with act.Fori(0, NH) as h:
                    for s in range(2):
                        act.wait_ge(w.used, h * 2 + (s + 2))
                        C.settle(act, "act")
                        nc.scalar.mul(qk[:, bass.ds(h * 2 + s, 1)].rearrange("p o t -> p (o t)"), ps[:, s].rearrange("p a b -> p (a b)"),
                                      1.0 if s == 0 else DK ** -0.5).then_inc(out_, 1)
                act.wait_ge(summed, 2 * NH)
                with act.Fori(0, NH) as h:
                    for g in range(4):
                        act.wait_ge(v_done, h * 4 + (g + 1))
                        C.settle(act, "act")
                        nc.scalar.copy(v[:, bass.ds(h, 1), 2 * g:2 * g + 2].rearrange("p o b e -> p (o b e)"),
                                       ps[:, g // 2, g % 2]).then_inc(v_out, 1)

            @block.vector
            def _(dve):
                for n in range(2 * NH):
                    d, h = n // NH, n % NH
                    dve.wait_ge(up_done, n + 1)
                    y = ps[:, 2 + n % 2].rearrange("p a b -> p (a b)")
                    nc.vector.tensor_scalar(bcum[:, d, h], y, C.decay_bias(d, h), 0.0, ALU.add, ALU.min).then_inc(up_out, 1)
                dve.wait_ge(logged, 1)
                dve.wait_ge(kept, 3)
                dve.wait_ge(up_out, 2 * NH)
                for n in range(2 * NH):
                    d, h = n // NH, n % NH
                    nc.vector.tensor_tensor(soft[:, d, h], bcum[:, d, h], soft[:, d, h], ALU.subtract).then_inc(clipped, 1)
                    dve.wait_ge(clipped, n + 1)
                    way = slice(None) if d == 0 else slice(None, None, -1)
                    nc.vector.tensor_tensor_scan(out=bcum[:, d, h, way], data0=keep[:, d, way], data1=soft[:, d, h, way],
                                                 initial=0.0, op0=ALU.mult, op1=ALU.add).then_inc(summed, 1)


def gla(nc, A, C, qk, v, bcum):
    with ExitStack() as ctx:
        sb = lambda n, s, d=F32: ctx.enter_context(nc.sbuf_tensor(n, s, d))
        sem = ctx.enter_context(Semaphores(nc))
        qki = sb("gl_qk_in", [P, 2, T])
        q_dec = sb("gl_q_dec", [P, T])
        k_end = sb("gl_k_end", [P, T])
        k_tok = sb("gl_k_tok", [P, NB, DK])
        sc = sb("gl_sc", [P, 2, NB, P])
        v_h = sb("gl_v_h", [P, NB, DV])
        state = sb("gl_state", [P, 4, DV])
        dec = sb("gl_dec", [P, 2, NCH])
        o_ps = ctx.enter_context(nc.psum_tensor("gl_o", [P, NE, 2, HALF], F32))
        sc_ps = ctx.enter_context(nc.psum_tensor("gl_sc_ps", [P, 2, 4, P], F32))
        u_ps = ctx.enter_context(nc.psum_tensor("gl_u_ps", [P, 2, HALF], F32))[:, :, 0:DV]
        (d1, d2, ex_q, ex_k, ex_end, ex_dec, ex_last, m_in, m_end, m_dec, v_in, scored, masked, turned, tok, u_done, s_done,
         inter, intra, sq, ssum, rooted, inv, o_out, zeroed) = (sem(f"gl_{n}") for n in (
             "diff", "end_diff", "exp_q", "exp_k", "exp_end", "exp_dec", "exp_last", "in_ready", "end_ready", "dec_ready", "v_copied",
             "scored", "masked", "turned", "tok_ready", "u_done", "state_ready", "inter_done", "intra_done", "squared",
             "sq_summed", "rooted", "inverted", "o_out", "zeroed"))

        def chunked(ap):
            return ap.rearrange("p (n c) -> p n c", c=CH)

        def head(tile, h):
            return tile[:, bass.ds(h, 1)].rearrange("p o t -> p (o t)")

        def sums(d, h):
            return bcum[:, d, bass.ds(h, 1)].rearrange("p o t -> p (o t)")

        def at(d, h, i):
            return chunked(sums(d, h))[:, :, i:i + 1].to_broadcast([P, NCH, CH])

        REF = (CH // 2, CH - 1 - CH // 2)
        LAST = (CH - 1, 0)
        US = NCH - 1
        with nc.Block() as block:
            @block.vector
            def _(dve):
                nc.vector.memset(sc[:], 0.0).then_inc(zeroed, 1)
                dve.wait_ge(zeroed, 1)
                with dve.Fori(0, NH) as h:
                    for d in range(2):
                        n = h * 2 + d
                        dve.wait_ge(scored, n * 2)
                        if d == 0:
                            dve.wait_ge(ssum, h)
                        nc.vector.tensor_tensor(chunked(qki[:, 1]), chunked(sums(d, h)), at(d, h, REF[d]), ALU.subtract).then_inc(d1, 1)
                        dve.wait_ge(ex_q, n + 1)
                        nc.vector.tensor_tensor(qki[:, 1], qki[:, 1], head(qk, h * 2 + 1), ALU.mult).then_inc(m_in, 1)
                        dve.wait_ge(ex_k, n + 1)
                        nc.vector.tensor_tensor(qki[:, 0], qki[:, 0], head(qk, h * 2), ALU.mult).then_inc(m_in, 1)
                        for g in range(2):
                            dve.wait_ge(scored, n * 2 + (g + 1))
                            if g == 0:
                                dve.wait_ge(intra, n)
                            C.settle(dve, "dve")
                            nc.vector.copy_predicated(sc[:, d, 4 * g:4 * g + 4], C.mask[:, d:d + 1].to_broadcast([P, 4, P]).bitcast(U32),
                                                      sc_ps[:, g]).then_inc(masked, 1)
                        dve.wait_ge(ex_last, n + 1)
                        for i in range(US):
                            c = i if d == 0 else NCH - 1 - i
                            dve.wait_ge(u_done, n * US + (i + 1))
                            if i < 4:
                                dve.wait_ge(inter, n * US)
                            else:
                                dve.wait_ge(inter, n * US + (i - 3))
                            if i == 0:
                                nc.vector.tensor_copy(state[:, 0], u_ps[:, 0]).then_inc(s_done, 1)
                            else:
                                dve.wait_ge(s_done, n * US + i)
                                nc.vector.scalar_tensor_tensor(out=state[:, i % 4], in0=state[:, (i - 1) % 4], scalar=dec[:, d, c:c + 1],
                                                               in1=u_ps[:, i % 2], op0=ALU.mult, op1=ALU.add).then_inc(s_done, 1)
                    dve.wait_ge(rooted, h + 1)
                    nc.vector.reciprocal(k_end[:], k_end[:]).then_inc(inv, 1)
                    dve.wait_ge(inv, h + 1)
                    dve.wait_ge(m_dec, h * 2 + 2)
                    dve.wait_ge(m_end, h * 2 + 2)
                    for e in range(NE):
                        nc.vector.tensor_tensor(head(qk, h * 2 + e), o_ps[:, e].rearrange("p a b -> p (a b)"), k_end[:], ALU.mult).then_inc(o_out, 1)

            @block.gpsimd
            def _(pool):
                with pool.Fori(0, NH) as h:
                    pool.wait_ge(inter, h * (2 * US))
                    C.settle(pool, "pool")
                    nc.gpsimd.tensor_copy(v_h[:], v[:, bass.ds(h, 1)].rearrange("p o b e -> p (o b) e")).then_inc(v_in, 1)
                    for d in range(2):
                        n = h * 2 + d
                        pool.wait_ge(turned, n * 2)
                        if d == 0:
                            pool.wait_ge(o_out, h * NE)
                        C.settle(pool, "pool")
                        nc.gpsimd.tensor_tensor(chunked(k_end[:]), at(d, h, LAST[d]), chunked(sums(d, h)), ALU.subtract).then_inc(d2, 1)
                        pool.wait_ge(ex_end, n + 1)
                        C.settle(pool, "pool")
                        nc.gpsimd.tensor_tensor(k_end[:], k_end[:], head(qk, h * 2), ALU.mult).then_inc(m_end, 1)
                        pool.wait_ge(ex_dec, n + 1)
                        C.settle(pool, "pool")
                        nc.gpsimd.tensor_tensor(q_dec[:], q_dec[:], head(qk, h * 2 + 1), ALU.mult).then_inc(m_dec, 1)

            @block.scalar
            def _(act):
                with act.Fori(0, NH) as h:
                    for d in range(2):
                        n = h * 2 + d
                        act.wait_ge(d1, n + 1)
                        nc.scalar.activation(qki[:, 0], qki[:, 1], ACT.Exp, scale=-1.0 / TAU).then_inc(ex_k, 1)
                        act.wait_ge(ex_k, n + 1)
                        nc.scalar.activation(qki[:, 1], qki[:, 1], ACT.Exp, scale=1.0 / TAU).then_inc(ex_q, 1)
                        act.wait_ge(d2, n + 1)
                        nc.scalar.activation(k_end[:], k_end[:], ACT.Exp, scale=1.0 / TAU).then_inc(ex_end, 1)
                        act.wait_ge(s_done, n * US)
                        C.settle(act, "act")
                        nc.scalar.activation(dec[:, d].rearrange("p (n o) -> p n o", o=1), chunked(sums(d, h))[:, :, LAST[d]:LAST[d] + 1],
                                             ACT.Exp, scale=1.0 / TAU).then_inc(ex_last, 1)
                        act.wait_ge(inter, n * US)
                        C.settle(act, "act")
                        nc.scalar.activation(q_dec[:], sums(d, h), ACT.Exp, scale=1.0 / TAU).then_inc(ex_dec, 1)
                        for g in range(2):
                            act.wait_ge(turned, n * 2 + (g + 1))
                            if g == 0:
                                act.wait_ge(u_done, n * US)
                            nc.scalar.copy(k_tok[:, 4 * g:4 * g + 4], sc_ps[:, g]).then_inc(tok, 1)
                    act.wait_ge(inter, h * (2 * US) + 2 * US)
                    for e in range(NE):
                        nc.scalar.activation(qki[:, e], o_ps[:, e].rearrange("p a b -> p (a b)"), ACT.Square).then_inc(sq, 1)
                    act.wait_ge(ssum, h + 1)
                    nc.scalar.activation(k_end[:], sc_ps[:].rearrange("p a b c -> p (a b c)"), ACT.Sqrt, bias=C.eps[:, 0:1], scale=1.0 / DV).then_inc(rooted, 1)

            @block.tensor
            def _(pe):
                with pe.Fori(0, NH) as h:
                    pe.wait_ge(v_in, h + 1)
                    for d in range(2):
                        n = h * 2 + d
                        pe.wait_ge(m_in, n * 2 + 2)
                        if d == 0:
                            pe.wait_ge(rooted, h)
                        else:
                            pe.wait_ge(tok, h * 4 + 2)
                        for b in range(NB):
                            m = nc.tensor.matmul(sc_ps[:, b // 4, b % 4], qki[:, 0, b * P:(b + 1) * P], qki[:, 1, b * P:(b + 1) * P],
                                                 start=(b % 4 == 0), stop=(b % 4 == 3), skip_group_check=True)
                            if b % 4 == 3:
                                m.then_inc(scored, 1)
                        pe.wait_ge(m_end, n + 1)
                        for g in range(2):
                            pe.wait_ge(masked, n * 2 + (g + 1))
                            for b in range(4):
                                m = nc.tensor.transpose(sc_ps[:, g, b], k_end[:, (4 * g + b) * P:(4 * g + b + 1) * P], C.ident[:])
                            m.then_inc(turned, 1)
                        pe.wait_ge(masked, n * 2 + 2)
                        if d == 0:
                            pe.wait_ge(o_out, h * NE)
                        for b in range(NB):
                            for e in range(NE):
                                m = nc.tensor.matmul(o_ps[:, e, b // 4, (b % 4) * P:(b % 4 + 1) * P], v_h[:, b, e * P:(e + 1) * P],
                                                     sc[:, d, b], start=(d == 0 and b % 4 == 0), stop=False, skip_group_check=True)
                        m.then_inc(intra, 1)
                        pe.wait_ge(tok, n * 2 + 2)
                        pe.wait_ge(m_dec, n + 1)

                        def update(i):
                            c = i if d == 0 else NCH - 1 - i
                            rows = slice((c % 2) * CH, (c % 2 + 1) * CH)
                            pe.wait_ge(s_done, n * US + max(i - 1, 0))
                            nc.tensor.matmul(u_ps[:, i % 2], k_tok[rows, c // 2], v_h[rows, c // 2], start=True, stop=True,
                                             skip_group_check=True).then_inc(u_done, 1)

                        update(0)
                        for i in range(US):
                            if i + 1 < US:
                                update(i + 1)
                            c = i + 1 if d == 0 else NCH - 2 - i
                            pe.wait_ge(s_done, n * US + (i + 1))
                            for e in range(NE):
                                m = nc.tensor.matmul(o_ps[:, e, c // 8, (c % 8) * CH:(c % 8 + 1) * CH], state[:, i % 4, e * P:(e + 1) * P],
                                                     q_dec[:, c * CH:(c + 1) * CH], start=False, stop=False, skip_group_check=True)
                            m.then_inc(inter, 1)
                    pe.wait_ge(tok, h * 4 + 4)
                    for e in range(NE):
                        pe.wait_ge(sq, h * NE + (e + 1))
                        for t in range(2):
                            m = nc.tensor.matmul(sc_ps[:, t].rearrange("p a b -> p (a b)"), C.ones[:], qki[:, e, t * HALF:(t + 1) * HALF],
                                                 start=(e == 0), stop=(e == NE - 1), skip_group_check=True)
                    m.then_inc(ssum, 1)


def gla_gate(nc, A, C, xn_hi, xn_lo, o, on_hi, on_lo):
    with ExitStack() as ctx:
        sb = lambda n, s, d=F32: ctx.enter_context(nc.sbuf_tensor(n, s, d))
        sem = ctx.enter_context(Semaphores(nc))
        w = Weights(ctx, nc, sem, "r")
        gated = sb("gg_gated", [P, 2, T])
        ps = ctx.enter_context(nc.psum_tensor("gg_ps", [P, 2, 2, HALF], F32))
        silu, mixed, high, low = (sem(f"gg_{n}") for n in ("silu", "mixed", "high", "low"))
        with nc.Block() as block:
            @block.sync
            def _(sp):
                load_weights(sp, w, A["stream_r"], 0, NC)

            @block.gpsimd
            def _(pool):
                split_weights(nc, pool, C, w, NC)

            @block.tensor
            def _(pe):
                with pe.Fori(0, NC // 2) as i:
                    for s in range(2):
                        pe.wait_ge(w.split, i * 2 + (s + 1))
                        pe.wait_ge(silu, i * 2)
                        project(nc, w, s, xn_hi, xn_lo, ps[:, s]).then_inc(w.used, 1)

            @block.scalar
            def _(act):
                with act.Fori(0, NC // 2) as i:
                    for s in range(2):
                        act.wait_ge(w.used, i * 2 + (s + 1))
                        act.wait_ge(low, i * 2)
                        nc.scalar.activation(gated[:, s], ps[:, s].rearrange("p a b -> p (a b)"), ACT.Silu).then_inc(silu, 1)
                    for s in range(2):
                        act.wait_ge(mixed, i * 2 + (s + 1))
                        C.settle(act, "act")
                        nc.scalar.copy(chunk(on_hi, i * 2 + s), gated[:, s]).then_inc(high, 1)

            @block.vector
            def _(dve):
                with dve.Fori(0, NC // 2) as i:
                    for s in range(2):
                        dve.wait_ge(silu, i * 2 + (s + 1))
                        nc.vector.scalar_tensor_tensor(out=gated[:, s], in0=chunk(o, i * 2 + s), scalar=C.col(16, i * 2 + s),
                                                       in1=gated[:, s], op0=ALU.mult, op1=ALU.mult).then_inc(mixed, 1)
                    for s in range(2):
                        dve.wait_ge(high, i * 2 + (s + 1))
                        nc.vector.tensor_tensor(chunk(on_lo, i * 2 + s), gated[:, s], chunk(on_hi, i * 2 + s).bitcast(F32),
                                                ALU.subtract).then_inc(low, 1)


def chunk(tile, c):
    return tile[:, bass.ds(c, 1)].rearrange("p o t -> p (o t)")


def branch(nc, A, C, tag, stream, bias, act_hi, act_lo, xn_hi, xn_lo, m, add):
    with ExitStack() as ctx:
        sb = lambda n, s, d=F32: ctx.enter_context(nc.sbuf_tensor(n, s, d))
        sem = ctx.enter_context(Semaphores(nc))
        w = Weights(ctx, nc, sem, tag)
        gate = sb(f"{tag}_gate", [P, 2, T])
        ps = ctx.enter_context(nc.psum_tensor(f"{tag}_ps", [P, 2, 2, 2, HALF], F32))
        gated, product = (sem(f"{tag}_{n}") for n in ("gated", "product"))
        mixed = sem(f"{tag}_mixed") if add else product
        flat = lambda ap: ap.rearrange("p a b -> p (a b)")
        with nc.Block() as block:
            @block.sync
            def _(sp):
                load_weights(sp, w, A[stream], 0, 2 * NC)

            @block.gpsimd
            def _(pool):
                split_weights(nc, pool, C, w, 2 * NC)

            @block.tensor
            def _(pe):
                with pe.Fori(0, NC // 2) as i:
                    for s in range(2):
                        pe.wait_ge(gated, i * 2)
                        pe.wait_ge(w.split, i * 4 + (2 * s + 1))
                        project(nc, w, 0, xn_hi, xn_lo, ps[:, s, 0]).then_inc(w.used, 1)
                        pe.wait_ge(w.split, i * 4 + (2 * s + 2))
                        pe.wait_ge(product, i * 2)
                        project(nc, w, 1, act_hi, act_lo, ps[:, s, 1]).then_inc(w.used, 1)

            @block.scalar
            def _(act):
                with act.Fori(0, NC // 2) as i:
                    for s in range(2):
                        act.wait_ge(w.used, i * 4 + (2 * s + 1))
                        act.wait_ge(mixed, i * 2)
                        C.settle(act, "act")
                        nc.scalar.activation(gate[:, s], flat(ps[:, s, 0]), ACT.Sigmoid, bias=C.col(bias, i * 2 + s)).then_inc(gated, 1)

            @block.vector
            def _(dve):
                with dve.Fori(0, NC // 2) as i:
                    for s in range(2):
                        dve.wait_ge(w.used, i * 4 + (2 * s + 2))
                        dve.wait_ge(gated, i * 2 + (s + 1))
                        if not add:
                            nc.vector.tensor_tensor(chunk(m, i * 2 + s), flat(ps[:, s, 1]), gate[:, s], ALU.mult).then_inc(product, 1)
                        else:
                            nc.vector.tensor_tensor(gate[:, s], flat(ps[:, s, 1]), gate[:, s], ALU.mult).then_inc(product, 1)
                            dve.wait_ge(product, i * 2 + (s + 1))
                            nc.vector.tensor_tensor(chunk(m, i * 2 + s), chunk(m, i * 2 + s), gate[:, s], ALU.add).then_inc(mixed, 1)


def conv(nc, A, C, xn_hi, xn_lo, y_hi, y_lo):
    with ExitStack() as ctx:
        sb = lambda n, s, d=F32: ctx.enter_context(nc.sbuf_tensor(n, s, d))
        sem = ctx.enter_context(Semaphores(nc))
        w = Weights(ctx, nc, sem, "c")
        ca = sb("cv_ca", [P, T])
        u = sb("cv_u", [P, T + 2])
        y = sb("cv_y", [P, T])
        ps = ctx.enter_context(nc.psum_tensor("cv_ps", [P, 3, 2, HALF], F32))
        ca_out, padded, u_done, step, y_done, high, low = (sem(f"cv_{n}") for n in ("ca_out", "padded", "u_done", "step", "y_done", "high", "low"))
        flat = lambda ap: ap.rearrange("p a b -> p (a b)")
        with nc.Block() as block:
            @block.sync
            def _(sp):
                load_weights(sp, w, A["stream_conv"], 0, 3 * NC)

            @block.gpsimd
            def _(pool):
                split_weights(nc, pool, C, w, 3 * NC)

            @block.tensor
            def _(pe):
                with pe.Fori(0, NC // 2) as i:
                    for n in range(6):
                        pe.wait_ge(w.split, i * 6 + (n + 1))
                        pe.wait_ge((ca_out, u_done, y_done)[n % 3], i * 2 + n // 3)
                        project(nc, w, n % 2, xn_hi, xn_lo, ps[:, n % 3]).then_inc(w.used, 1)

            @block.scalar
            def _(act):
                with act.Fori(0, NC // 2) as i:
                    for s in range(2):
                        act.wait_ge(w.used, i * 6 + (3 * s + 1))
                        act.wait_ge(u_done, i * 2 + s)
                        nc.scalar.copy(ca[:], flat(ps[:, 0])).then_inc(ca_out, 1)
                        act.wait_ge(y_done, i * 2 + (s + 1))
                        C.settle(act, "act")
                        nc.scalar.copy(chunk(y_hi, i * 2 + s), y[:]).then_inc(high, 1)

            @block.vector
            def _(dve):
                nc.vector.memset(u[:, 0:1], 0.0).then_inc(padded, 1)
                nc.vector.memset(u[:, T + 1:T + 2], 0.0).then_inc(padded, 1)
                dve.wait_ge(padded, 2)
                with dve.Fori(0, NC // 2) as i:
                    for s in range(2):
                        c = i * 2 + s
                        dve.wait_ge(w.used, i * 6 + (3 * s + 2))
                        dve.wait_ge(ca_out, c + 1)
                        nc.vector.tensor_tensor(u[:, 1:T + 1], flat(ps[:, 1]), ca[:], ALU.mult).then_inc(u_done, 1)
                        dve.wait_ge(u_done, c + 1)
                        nc.vector.tensor_scalar(y[:], u[:, 0:T], C.col(24, c), C.col(48, c), ALU.mult, ALU.add).then_inc(step, 1)
                        dve.wait_ge(step, c * 3 + 1)
                        nc.vector.scalar_tensor_tensor(out=y[:], in0=u[:, 1:T + 1], scalar=C.col(32, c), in1=y[:], op0=ALU.mult, op1=ALU.add).then_inc(step, 1)
                        dve.wait_ge(step, c * 3 + 2)
                        nc.vector.scalar_tensor_tensor(out=y[:], in0=u[:, 2:T + 2], scalar=C.col(40, c), in1=y[:], op0=ALU.mult, op1=ALU.add).then_inc(step, 1)
                        dve.wait_ge(step, c * 3 + 3)
                        dve.wait_ge(w.used, i * 6 + (3 * s + 3))
                        nc.vector.tensor_tensor(y[:], flat(ps[:, 2]), y[:], ALU.mult).then_inc(y_done, 1)
                        dve.wait_ge(high, c + 1)
                        nc.vector.tensor_tensor(chunk(y_lo, c), y[:], chunk(y_hi, c).bitcast(F32), ALU.subtract).then_inc(low, 1)
                        dve.wait_ge(low, c + 1)


def refine_rstd(nc, dve, sem, done, rstd, root, ss, tmp, n):
    def link(ins):
        done[0] += 1
        ins.then_inc(sem, 1)
        dve.wait_ge(sem, done[0])

    link(nc.vector.reciprocal(rstd, root))
    link(nc.vector.tensor_scalar(tmp, ss, 1.0 / n, EPS, ALU.mult, ALU.add))
    link(nc.vector.tensor_tensor(tmp, tmp, rstd, ALU.mult))
    link(nc.vector.tensor_tensor(tmp, tmp, rstd, ALU.mult))
    link(nc.vector.tensor_scalar(tmp, tmp, -0.5, 1.5, ALU.mult, ALU.add))
    link(nc.vector.tensor_tensor(rstd, rstd, tmp, ALU.mult))


def out_project(nc, A, C, m, x2, ss):
    with ExitStack() as ctx:
        sb = lambda n, s, d=F32: ctx.enter_context(nc.sbuf_tensor(n, s, d))
        sem = ctx.enter_context(Semaphores(nc))
        raw = sb("op_raw", [P, 2, D])
        w_hi, w_lo = sb("op_w_hi", [P, NC, D], F32R), sb("op_w_lo", [P, NC, D], F32R)
        m_hi, m_lo = sb("op_m_hi", [P, 2, NC, P], F32R), sb("op_m_lo", [P, 2, NC, P], F32R)
        x = sb("op_x", [P, 2, D])
        junk = sb("op_junk", [P, D])
        ps = ctx.enter_context(nc.psum_tensor("op_ps", [P, 2, 2, HALF], F32))
        w_in = [sem(f"op_w_in{s}") for s in range(2)]
        x_in = [sem(f"op_x_in{s}") for s in range(2)]
        w_high, w_split, m_high, m_split, made, added, squared = (
            sem(f"op_{n}") for n in ("w_high", "w_split", "m_high", "m_split", "made", "added", "squared"))
        with nc.Block() as block:
            @block.sync
            def _(sp):
                for k in range(NC):
                    if k >= 2:
                        sp.wait_ge(w_split, k - 1)
                    sp.dma_start(raw[:, k % 2], A["w_out"][k]).then_inc(w_in[k % 2], 16)
                for b in range(NB):
                    if b >= 2:
                        sp.wait_ge(added, b - 1)
                    sp.dma_start(x[:, b % 2], A["x"][b]).then_inc(x_in[b % 2], 16)

            @block.gpsimd
            def _(pool):
                for b in range(NB):
                    pool.wait_ge(m_high, b + 1)
                    nc.gpsimd.tensor_tensor(m_lo[:, b % 2], m[:, :, b * P:(b + 1) * P], m_hi[:, b % 2].bitcast(F32), ALU.subtract).then_inc(m_split, 1)

            @block.scalar
            def _(act):
                def split_m(b):
                    if b >= 2:
                        act.wait_ge(made, b - 1)
                    nc.scalar.copy(m_hi[:, b % 2], m[:, :, b * P:(b + 1) * P]).then_inc(m_high, 1)

                split_m(0)
                split_m(1)
                for k in range(NC):
                    act.wait_ge(w_in[k % 2], 16 * (k // 2 + 1))
                    nc.scalar.copy(w_hi[:, k], raw[:, k % 2]).then_inc(w_high, 1)
                for b in range(NB):
                    if b + 2 < NB:
                        split_m(b + 2)
                    act.wait_ge(added, b + 1)
                    if b:
                        act.wait_ge(squared, b)
                    nc.scalar.activation(junk[:], x2[:, b], ACT.Square, accum_out=ss[:, b:b + 1]).then_inc(squared, 1)

            @block.tensor
            def _(pe):
                for b in range(NB):
                    pe.wait_ge(m_split, b + 1)
                    if b >= 2:
                        pe.wait_ge(added, b - 1)
                    for k in range(NC):
                        if b == 0:
                            pe.wait_ge(w_split, k + 1)
                        for i, (a, part) in enumerate(((m_hi, w_hi), (m_hi, w_lo), (m_lo, w_hi))):
                            for t in range(2):
                                last = nc.tensor.matmul(ps[:, b % 2, t], a[:, b % 2, k], part[:, k, t * HALF:(t + 1) * HALF],
                                                        start=(k == 0 and i == 0), stop=(k == NC - 1 and i == 2))
                    last.then_inc(made, 1)

            @block.vector
            def _(dve):
                for k in range(NC):
                    dve.wait_ge(w_high, k + 1)
                    nc.vector.tensor_tensor(w_lo[:, k], raw[:, k % 2], w_hi[:, k].bitcast(F32), ALU.subtract).then_inc(w_split, 1)
                for b in range(NB):
                    dve.wait_ge(made, b + 1)
                    dve.wait_ge(x_in[b % 2], 16 * (b // 2 + 1))
                    nc.vector.tensor_tensor(x2[:, b], ps[:, b % 2].rearrange("p a b -> p (a b)"), x[:, b % 2], ALU.add).then_inc(added, 1)


def norm_second(nc, A, C, x2, ss, rstd, xt_hi, xt_lo):
    with ExitStack() as ctx:
        sb = lambda n, s, d=F32: ctx.enter_context(nc.sbuf_tensor(n, s, d))
        sem = ctx.enter_context(Semaphores(nc))
        root = sb("n2_root", [P, NB])
        g2 = sb("n2_g", [P, D])
        tmp = sb("n2_tmp", [P, NB])
        xt = sb("n2_xt", [P, 2, D])
        ps = ctx.enter_context(nc.psum_tensor("n2_ps", [P, 2, NC, P], F32))
        rows_in, rooted, link, scaled, turned, high, low = (sem(f"n2_{n}") for n in ("rows_in", "rooted", "link", "scaled", "turned", "high", "low"))
        with nc.Block() as block:
            @block.sync
            def _(sp):
                sp.dma_start(g2[:], A["norm2_g"].to_broadcast([P, D])).then_inc(rows_in, 16)

            @block.scalar
            def _(act):
                nc.scalar.activation(root[:], ss[:], ACT.Sqrt, bias=C.eps[:, 0:1], scale=1.0 / D).then_inc(rooted, 1)
                for b in range(NB):
                    act.wait_ge(turned, b + 1)
                    nc.scalar.copy(xt_hi[b // 4][:, :, (b % 4) * P:(b % 4 + 1) * P], ps[:, b % 2]).then_inc(high, 1)

            @block.tensor
            def _(pe):
                for b in range(NB):
                    pe.wait_ge(scaled, b + 1)
                    if b >= 2:
                        pe.wait_ge(low, b - 1)
                    for c in range(NC):
                        last = nc.tensor.transpose(ps[:, b % 2, c], xt[:, b % 2, c * P:(c + 1) * P], C.ident[:])
                    last.then_inc(turned, 1)

            @block.vector
            def _(dve):
                dve.wait_ge(rooted, 1)
                refine_rstd(nc, dve, link, [0], rstd[:], root[:], ss[:], tmp[:], D)
                dve.wait_ge(rows_in, 16)

                def scale(b):
                    if b >= 2:
                        dve.wait_ge(turned, b - 1)
                    nc.vector.scalar_tensor_tensor(out=xt[:, b % 2], in0=x2[:, b], scalar=rstd[:, b:b + 1], in1=g2[:],
                                                   op0=ALU.mult, op1=ALU.mult).then_inc(scaled, 1)

                scale(0)
                for b in range(NB):
                    if b + 1 < NB:
                        scale(b + 1)
                    dve.wait_ge(high, b + 1)
                    nc.vector.tensor_tensor(xt_lo[b // 4][:, :, (b % 4) * P:(b % 4 + 1) * P], ps[:, b % 2],
                                            xt_hi[b // 4][:, :, (b % 4) * P:(b % 4 + 1) * P].bitcast(F32),
                                            ALU.subtract).then_inc(low, 1)


def route(nc, A, C, xt_hi, xt_lo, halves, dense_gates, experts, gates):
    with ExitStack() as ctx:
        sb = lambda n, s, d=F32: ctx.enter_context(nc.sbuf_tensor(n, s, d))
        sem = ctx.enter_context(Semaphores(nc))
        w = Weights(ctx, nc, sem, "q")
        keys = sb("rt_keys", [P, 2 * PH, NKEYS])
        q = sb("rt_q", [P, 2, T])
        s0 = sb("rt_s0", [P, 2, NB, NKEYS])
        s1 = sb("rt_s1", [P, 2, NB, NKEYS])
        top = sb("rt_top", [P, 2, NB, TOPK])
        topi = sb("rt_topi", [P, 2, 2, NB, TOPK], U32)
        topf = sb("rt_topf", [P, 2, NB, TOPK])
        cand = sb("rt_cand", [P, NB, TOPK, TOPK])
        rest = sb("rt_rest", [P, NB, TOPK, TOPK])
        hit = sb("rt_hit", [P, 2, NB, TOPK, TOPK])
        best = sb("rt_best", [P, NB, TOPK])
        besti = sb("rt_besti", [P, NB, TOPK], U32)
        where = sb("rt_where", [P, 2, NB, TOPK], U32)
        wheref = sb("rt_wheref", [P, 2, NB, TOPK])
        half = sb("rt_half", [P, 2, NB, TOPK])
        iota = sb("rt_iota", [P, TOPK])
        shifted = sb("rt_shifted", [P, NB, TOPK])
        raised = sb("rt_raised", [P, NB, TOPK])
        total = sb("rt_total", [P, NB])
        q_ps = ctx.enter_context(nc.psum_tensor("rt_q_ps", [P, 2, 2, HALF], F32))
        s_ps = ctx.enter_context(nc.psum_tensor("rt_s_ps", [P, 2, NB, NKEYS], F32))
        keys_in, q_out, made, s_out, less, exped, counted, link_, searched, picked, decode = (sem(f"rt_{n}") for n in (
            "keys_in", "q_out", "made", "s_out", "less", "exped", "counted", "link", "searched", "picked", "decode"))
        LINKS = 13
        STEPS = 14

        def slots(tile, n, h):
            return tile[..., 0:n, bass.ds(h * TOPK, TOPK)]

        with nc.Block() as block:
            @block.sync
            def _(sp):
                sp.dma_start(keys[:], A["keys"]).then_inc(keys_in, 16)
                load_weights(sp, w, A["stream_q"], 0, 2 * PH)

            @block.tensor
            def _(pe):
                pe.wait_ge(keys_in, 16)
                with pe.Fori(0, PH) as h:
                    for s in range(2):
                        pe.wait_ge(w.split, h * 2 + (s + 1))
                        pe.wait_ge(q_out, h * 2)
                        project(nc, w, s, xt_hi, xt_lo, q_ps[:, s]).then_inc(w.used, 1)
                    for s in range(2):
                        pe.wait_ge(q_out, h * 2 + (s + 1))
                        pe.wait_ge(s_out, h * 2)
                        for b in range(NB):
                            last = nc.tensor.matmul(s_ps[:, s, b], q[:, s, b * P:(b + 1) * P], chunk(keys, h * 2 + s),
                                                    start=(b % 4 == 0), stop=(b % 4 == 3), skip_group_check=True)
                        last.then_inc(made, 1)

            @block.scalar
            def _(act):
                with act.Fori(0, PH) as h:
                    for s in range(2):
                        act.wait_ge(w.used, h * 2 + (s + 1))
                        act.wait_ge(made, h * 2)
                        nc.scalar.copy(q[:, s], q_ps[:, s].rearrange("p a b -> p (a b)")).then_inc(q_out, 1)
                    for s in range(2):
                        act.wait_ge(made, h * 2 + (s + 1))
                        act.wait_ge(searched, h)
                        nc.scalar.copy(s0[:, s], s_ps[:, s]).then_inc(s_out, 1)
                    act.wait_ge(less, h + 1)
                    nc.scalar.activation(raised[:], shifted[:], ACT.Exp).then_inc(exped, 1)

            @block.vector
            def _(dve):
                with dve.Fori(0, PH // 2) as i:
                    for p in range(2):
                        h = i * 2 + p
                        steps = [0]

                        def link(ins, h=h, steps=steps):
                            steps[0] += 1
                            ins.then_inc(link_, 1)
                            dve.wait_ge(link_, h * LINKS + steps[0])
                            C.settle(dve, "dve")

                        def top16(source, left, values, indices, n, end=None):
                            for at in range(2):
                                src = source if at == 0 else left
                                for c in range(n):
                                    ins = nc.vector.max(values(c, at), src(c))
                                link(ins)
                                for c in range(n):
                                    ins = nc.vector.max_index(indices(c, at), values(c, at), src(c))
                                if at == 0:
                                    for c in range(n):
                                        ins = nc.vector.match_replace(left(c), values(c, at), src(c), NEG)
                                if at == 0 or end is None:
                                    link(ins)
                                else:
                                    ins.then_inc(end, 1)

                        dve.wait_ge(s_out, h * 2 + 2)
                        dve.wait_ge(picked, i * 2)
                        C.settle(dve, "dve")
                        rows = lambda t: lambda c: t[:, c // NB, c % NB]
                        top16(rows(s0), rows(s1), lambda c, a: top[:, c // NB, c % NB, 8 * a:8 * a + 8],
                              lambda c, a, p=p: topi[:, p, c // NB, c % NB, 8 * a:8 * a + 8], 2 * NB, searched)
                        link(nc.vector.tensor_tensor(cand[:], top[:, 0].unsqueeze(3).to_broadcast([P, NB, TOPK, TOPK]),
                                                     top[:, 1].unsqueeze(2).to_broadcast([P, NB, TOPK, TOPK]), ALU.add))
                        flat = lambda t: lambda b: t[:, b].rearrange("p a b -> p (a b)")
                        top16(flat(cand), flat(rest), lambda b, a: best[:, b, 8 * a:8 * a + 8], lambda b, a: besti[:, b, 8 * a:8 * a + 8], NB)
                        nc.vector.tensor_tensor(shifted[:], best[:], best[:, :, 0:1].to_broadcast([P, NB, TOPK]), ALU.subtract).then_inc(less, 1)
                        nc.vector.tensor_scalar(where[:, 0], besti[:], 4, None, ALU.logical_shift_right)
                        link(nc.vector.tensor_scalar(where[:, 1], besti[:], TOPK - 1, None, ALU.bitwise_and))
                        link(nc.vector.tensor_copy(wheref[:], where[:]))
                        dve.wait_ge(picked, h)
                        C.settle(dve, "dve")
                        dve.wait_ge(counted, 1)
                        for side in range(2):
                            ins = nc.vector.tensor_tensor(hit[:, side].rearrange("p b k i -> p (b k) i"),
                                                          wheref[:, side].rearrange("p b k -> p (b k)").unsqueeze(2).to_broadcast([P, NB * TOPK, TOPK]),
                                                          iota[:].unsqueeze(1).to_broadcast([P, NB * TOPK, TOPK]), ALU.is_equal)
                        ins.then_inc(decode, 1)
                        dve.wait_ge(exped, h + 1)
                        link(nc.vector.tensor_reduce(total[:], raised[:], AX.X, ALU.add))
                        link(nc.vector.reciprocal(total[:], total[:]))
                        for tile, b0, b1 in ((dense_gates, 0, DB), (gates, DB, NB)):
                            ins = nc.vector.tensor_tensor(slots(tile, b1 - b0, h), raised[:, b0:b1],
                                                          total[:, b0:b1].unsqueeze(2).to_broadcast([P, b1 - b0, TOPK]), ALU.mult)
                        link(ins)
                        assert steps[0] == LINKS, steps[0]

            @block.gpsimd
            def _(pool):
                nc.gpsimd.iota(iota[:], [[1, TOPK]], base=0, channel_multiplier=0, allow_small_or_imprecise_dtypes=True).then_inc(counted, 1)
                pool.wait_ge(counted, 1)
                for s in range(2):
                    split_chunk(nc, pool, C, w, s, s, 16)
                nc.gpsimd.memset(half[:], 0.0).then_inc(counted, 1)
                pool.wait_ge(counted, 2)

                def decode_head(h, p):
                    steps = [0]

                    def link(ins):
                        steps[0] += 1
                        ins.then_inc(picked_steps, 1)
                        pool.wait_ge(picked_steps, h * STEPS + steps[0])
                        C.settle(pool, "pool")

                    pool.wait_ge(decode, h + 1)
                    C.settle(pool, "pool")
                    link(nc.gpsimd.tensor_copy(topf[:], topi[:, p]))
                    for side in range(2):
                        link(nc.gpsimd.tensor_tensor(hit[:, side], hit[:, side], topf[:, side].unsqueeze(2).to_broadcast([P, NB, TOPK, TOPK]), ALU.mult))
                        n = TOPK // 2
                        while n > 1:
                            link(nc.gpsimd.tensor_tensor(hit[:, side, ..., 0:n], hit[:, side, ..., 0:n], hit[:, side, ..., n:2 * n], ALU.add))
                            n //= 2
                        link(nc.gpsimd.tensor_tensor(half[:, side], hit[:, side, ..., 0], hit[:, side, ..., 1], ALU.add))
                    link(nc.gpsimd.tensor_scalar(topf[:, 0], half[:, 0], float(NKEYS), None, ALU.mult))
                    for side in range(2):
                        nc.gpsimd.tensor_copy(slots(halves[:, side], DB, h), half[:, side, 0:DB])
                    link(nc.gpsimd.tensor_tensor(topf[:, 0], topf[:, 0], half[:, 1], ALU.add))
                    link(nc.gpsimd.tensor_copy(slots(experts, NB - DB, h), topf[:, 0, DB:NB]))
                    assert steps[0] == STEPS, steps[0]
                    pool.sem_inc(picked, 1)

                picked_steps = sem("rt_picked_steps")
                with pool.Fori(0, PH // 2 - 1) as i:
                    for p in range(2):
                        for s in range(2):
                            pool.wait_ge(w.used, i * 4 + (2 * p + s + 1))
                            split_chunk(nc, pool, C, w, s, i * 4 + (2 * p + s + 2), i * 32 + (16 * (p + 2)))
                        decode_head(i * 2 + p, p)
                for s in range(2):
                    pool.wait_ge(w.used, 2 * PH - 3 + s)
                    split_chunk(nc, pool, C, w, s, 2 * PH - 2 + s, 16 * PH)
                decode_head(PH - 2, 0)
                decode_head(PH - 1, 1)


def gate_tables(nc, A, C, halves, gates, gate_chunks):
    with ExitStack() as ctx:
        sb = lambda n, s, d=F32: ctx.enter_context(nc.sbuf_tensor(n, s, d))
        sem = ctx.enter_context(Semaphores(nc))
        table = sb("gt_table", [P, 2, NKEYS, 64])
        cols = sb("gt_cols", [P, 3, P])
        first, second = sb("gt_first", [P, 4, 4, NKEYS]), sb("gt_second", [P, 4, 4, NKEYS])
        iota = sb("gt_iota", [P, NKEYS])
        t_ps = ctx.enter_context(nc.psum_tensor("gt_t_ps", [P, 4, P], F32))
        g_ps = ctx.enter_context(nc.psum_tensor("gt_g_ps", [P, 4, 4, NKEYS], F32))
        counted, turned, cols_out, hot, made, out_, stored0, stored1 = (
            sem(f"gt_{n}") for n in ("counted", "turned", "cols_out", "hot", "made", "out", "stored0", "stored1"))
        stored = (stored0, stored1)
        QUADS = P // 4
        SLOT = 4
        with nc.Block() as block:
            @block.gpsimd
            def _(pool):
                nc.gpsimd.iota(iota[:], [[1, NKEYS]], base=0, channel_multiplier=0, allow_small_or_imprecise_dtypes=True).then_inc(counted, 1)

            @block.tensor
            def _(pe):
                pe.sem_inc(made, SLOT)
                for b in range(DB):
                    if b:
                        pe.wait_ge(cols_out, b)
                    for n, tile in enumerate((halves[:, 0, b], halves[:, 1, b], gates[:, b])):
                        last = nc.tensor.transpose(t_ps[:, n], tile, C.ident[:])
                    last.then_inc(turned, 1)
                    with pe.Fori(0, QUADS // SLOT) as i:
                        for p in range(SLOT):
                            q = i * SLOT + (b * QUADS + p)
                            pe.wait_ge(hot, q + 1)
                            pe.wait_ge(out_, q + 1)
                            for t in range(4):
                                last = nc.tensor.matmul(g_ps[:, p, t], second[:, p, t], first[:, p, t], start=(t == 0), stop=(t == 3),
                                                        skip_group_check=True)
                            last.then_inc(made, 1)

            @block.vector
            def _(dve):
                dve.wait_ge(counted, 1)
                for b in range(DB):
                    dve.wait_ge(turned, b + 1)
                    if b:
                        dve.wait_ge(hot, b * QUADS)
                    nc.vector.tensor_copy(cols[:], t_ps[:, 0:3]).then_inc(cols_out, 1)
                    dve.wait_ge(cols_out, b + 1)
                    C.settle(dve, "dve")
                    with dve.Fori(0, QUADS // SLOT) as i:
                        for p in range(SLOT):
                            dve.wait_ge(made, i * SLOT + (b * QUADS + p + 1))
                            for t in range(4):
                                at = bass.ds((i * SLOT + p) * 4 + t, 1)
                                nc.vector.tensor_scalar(first[:, p, t], iota[:], cols[:, 0, at], None, ALU.is_equal)
                                last = nc.vector.tensor_scalar(second[:, p, t], iota[:], cols[:, 1, at], cols[:, 2, at], ALU.is_equal, ALU.mult)
                            last.then_inc(hot, 1)

            @block.scalar
            def _(act):
                act.sem_inc(out_, SLOT)
                for b in range(DB):
                    for n in range(2):
                        if b:
                            act.wait_ge(stored[n], 16 * b)
                        with act.Fori(0, QUADS // 2 // SLOT) as i:
                            for p in range(SLOT):
                                act.wait_ge(made, i * SLOT + (b * QUADS + n * QUADS // 2 + p + 1 + SLOT))
                                C.settle(act, "act")
                                nc.scalar.copy(table[:, n, :, bass.ds((i * SLOT + p) * 4, 4)].rearrange("p k t -> p t k"), g_ps[:, p]).then_inc(out_, 1)

            @block.sync
            def _(sp):
                for b in range(DB):
                    for n in range(2):
                        sp.wait_ge(out_, b * QUADS + (n + 1) * QUADS // 2 + SLOT)
                        sp.dma_start(gate_chunks[:, :, b * P + n * 64:b * P + (n + 1) * 64].rearrange("a i t -> i a t"), table[:, n]).then_inc(stored[n], 16)
                for n in range(2):
                    sp.wait_ge(stored[n], 16 * DB)


def peer(nc, A, C, x2, rstd, xd_hi, xd_lo, experts, gates, gate_chunks):
    GU = 32
    GROUPS = NKEYS // GROUP
    HALF_BLOCK = SLOTS // GU
    assert GROUPS == (NB - DB) * 2 * HALF_BLOCK and GU % RING == 0
    TURNS = DB * 2
    BANKS = 4
    with ExitStack() as ctx:
        sb = lambda n, s, d=F32: ctx.enter_context(nc.sbuf_tensor(n, s, d))
        sem = ctx.enter_context(Semaphores(nc))
        u_raw = sb("pe_u_raw", [P, 2, NC, P])
        u_hi, u_lo = sb("pe_u_hi", [P, 2, NC, P], F32R), sb("pe_u_lo", [P, 2, NC, P], F32R)
        v_raw = sb("pe_v_raw", [P, 2, D])
        v_hi, v_lo = sb("pe_v_hi", [P, GROUP, D], F32R), sb("pe_v_lo", [P, GROUP, D], F32R)
        g_in = sb("pe_g_in", [P, 2, DT])
        a = sb("pe_a", [P, 2, DT])
        a_hi, a_lo = sb("pe_a_hi", [P, GROUP, DT], F32R), sb("pe_a_lo", [P, GROUP, DT], F32R)
        ring = sb("pe_ring", [P, RING, D])
        xt = sb("pe_xt", [P, D])
        g2 = sb("pe_g2", [P, D])
        acc = sb("pe_acc", [P, D])
        index = sb("pe_index", [P, 2, GU], U32)
        hidden = sb("pe_hidden", [P, 2, GU])
        active = sb("pe_active", [P, SLOTS])
        weight = sb("pe_weight", [P, SLOTS])
        h_ps = ctx.enter_context(nc.psum_tensor("pe_h_ps", [P, 2, DT], F32))
        o_ps = ctx.enter_context(nc.psum_tensor("pe_o_ps", [P, BANKS, HALF], F32))
        ring_in = [sem(f"pe_ring_in{s}") for s in range(RING)]
        u_in, v_in, gate_in = ([sem(f"pe_{n}_in{s}") for s in range(2)] for n in ("u", "v", "g"))
        (rows_in, used, indexed, gelued, xt_ready, weighed, zeroed, summed, u_high, u_split, v_high, v_split,
         h_done, act_done, gated, a_high, a_split, o_done, added) = (sem(f"pe_{n}") for n in (
             "rows_in", "used", "indexed", "gelued", "xt_ready", "weighed", "zeroed", "summed", "u_high", "u_split", "v_high",
             "v_split", "h_done", "act_done", "gated", "a_high", "a_split", "o_done", "added"))
        POOL_RUNS = [(0, 4), (4, 8), (8, 12), (12, 16), (16, GU)]
        CREDIT = GU

        def row_of(table, c):
            return table[bass.ds(c, 1)].rearrange("o p k -> (o p) k")

        with nc.Block() as block:
            @block.sync
            def _(sp):
                sp.dma_start(g2[:], A["norm2_g"].to_broadcast([P, D])).then_inc(rows_in, 16)
                ut, vt = A["peer_ut"].rearrange("c p k m -> c p (k m)"), A["peer_v"].rearrange("(c p) d -> c p d", p=P)

                def load_u(p, row):
                    sp.dma_start(u_raw[:, p].rearrange("p k m -> p (k m)"), row).then_inc(u_in[p], 16)

                def load_gate_and_v(p, c):
                    sp.dma_start(g_in[:, p], row_of(gate_chunks, c)).then_inc(gate_in[p], 16)
                    sp.dma_start(v_raw[:, p], row_of(vt, c)).then_inc(v_in[p], 16)

                for p in range(2):
                    load_u(p, ut[p])
                for p in range(2):
                    load_gate_and_v(p, p)
                for p in range(2):
                    sp.wait_ge(u_split, p + 1)
                    load_u(p, ut[2 + p])
                with sp.Fori(0, NKEYS // 2 - 2) as i:
                    for p in range(2):
                        sp.wait_ge(gated, i * 2 + (p + 1))
                        sp.wait_ge(v_split, i * 2 + (p + 1))
                        load_gate_and_v(p, i * 2 + (p + 2))
                        sp.wait_ge(u_split, i * 2 + (p + 3))
                        load_u(p, row_of(ut, i * 2 + (p + 4)))
                for p in range(2):
                    sp.wait_ge(gated, NKEYS - 3 + p)
                    sp.wait_ge(v_split, NKEYS - 3 + p)
                    load_gate_and_v(p, NKEYS - 2 + p)
                    sp.wait_ge(u_split, NKEYS - 1 + p)
                    load_u(p, ut[p])

            @block.gpsimd
            def _(pool):
                def u_low(s, c):
                    pool.wait_ge(u_high, c + 1)
                    nc.gpsimd.tensor_tensor(u_lo[:, s], u_raw[:, s], u_hi[:, s].bitcast(F32), ALU.subtract).then_inc(u_split, 1)

                u_low(0, 0)
                u_low(1, 1)
                with pool.Fori(0, NB - DB) as b:
                    for table in (A["peer_u"], A["peer_v"]):
                        with pool.Fori(0, HALF_BLOCK // 2) as i:
                            for p in range(2):
                                g = b * (2 * HALF_BLOCK) + i * 2 + (p + (HALF_BLOCK if table is A["peer_v"] else 0))
                                for j in range(GROUP + 1):
                                    for n in range(*POOL_RUNS[j]):
                                        if n == 0:
                                            pool.wait_ge(indexed, g + 1)
                                        pool.wait_ge(used, g * GU + (n + 1 + CREDIT - RING))
                                        C.settle(pool, "pool")
                                        nc.gpsimd.indirect_dma_start(ring[:, n % RING], None, table,
                                                                     bass.IndirectOffsetOnAxis(index[:, p, n:n + 1], 0)).then_inc(ring_in[n % RING], 16)
                                    if j < GROUP:
                                        u_low(j % 2, g * GROUP + (j + 2))

            @block.scalar
            def _(act):
                def u_high_part(s, in16):
                    act.wait_ge(u_in[s], in16)
                    nc.scalar.copy(u_hi[:, s], u_raw[:, s]).then_inc(u_high, 1)

                act.wait_ge(used, CREDIT)
                u_high_part(0, 16)
                u_high_part(1, 16)
                with act.Fori(0, NB - DB) as b:
                    for side in range(2):
                        with act.Fori(0, HALF_BLOCK // 2) as i:
                            for p in range(2):
                                g = b * (2 * HALF_BLOCK) + i * 2 + (p + HALF_BLOCK * side)
                                act.wait_ge(used, g * GU)
                                C.settle(act, "act")
                                nc.scalar.copy(index[:, p], experts[:, bass.ds(b, 1), bass.ds((i * 2 + p) * GU, GU)]
                                               .rearrange("q o k -> q (o k)")).then_inc(indexed, 1)
                                for j in range(GROUP):
                                    c = g * GROUP + j
                                    act.wait_ge(h_done, c + 1)
                                    act.wait_ge(a_split, g * GROUP + (j - j % 2))
                                    nc.scalar.activation(a[:, j % 2], h_ps[:, j % 2], ACT.Gelu).then_inc(act_done, 1)
                                    act.wait_ge(u_in[j % 2], g * (GROUP // 2 * 16) + (16 * (j // 2 + 2)))
                                    nc.scalar.copy(u_hi[:, j % 2], u_raw[:, j % 2]).then_inc(u_high, 1)
                                    act.wait_ge(v_in[j % 2], g * (GROUP // 2 * 16) + (16 * (j // 2 + 1)))
                                    act.wait_ge(o_done, g * TURNS)
                                    nc.scalar.copy(v_hi[:, j], v_raw[:, j % 2]).then_inc(v_high, 1)
                                    act.wait_ge(gated, c + 1)
                                    nc.scalar.copy(a_hi[:, j], a[:, j % 2]).then_inc(a_high, 1)
                                if side == 0:
                                    act.wait_ge(used, g * GU + (CREDIT + GU))
                                    C.settle(act, "act")
                                    nc.scalar.activation(active[:, bass.ds((i * 2 + p) * GU, GU)], hidden[:, p], ACT.Gelu).then_inc(gelued, 1)

            @block.tensor
            def _(pe):
                def hidden_of(g, j):
                    pe.wait_ge(u_split, g * GROUP + (j + 1))
                    if j >= 2:
                        pe.wait_ge(act_done, g * GROUP + (j - 1))
                    for k in range(NC):
                        for i, (u, x) in enumerate(((u_hi, xd_hi), (u_hi, xd_lo), (u_lo, xd_hi))):
                            last = nc.tensor.matmul(h_ps[:, j % 2], u[:, j % 2, k], x[:, k], start=(k == 0 and i == 0),
                                                    stop=(k == NC - 1 and i == 2))
                    last.then_inc(h_done, 1)

                def out_of(g):
                    pe.wait_ge(v_split, g * GROUP + GROUP)
                    pe.wait_ge(a_split, g * GROUP + GROUP)
                    for n in range(TURNS):
                        tb, half = n // 2, n % 2
                        pe.wait_ge(added, g * TURNS + (n + 1))
                        for j in range(GROUP):
                            for i, (x, v) in enumerate(((a_hi, v_hi), (a_hi, v_lo), (a_lo, v_hi))):
                                last = nc.tensor.matmul(o_ps[:, n % BANKS], x[:, j, tb * P:(tb + 1) * P], v[:, j, half * HALF:(half + 1) * HALF],
                                                        start=(j == 0 and i == 0), stop=(j == GROUP - 1 and i == 2))
                        last.then_inc(o_done, 1)

                hidden_of(0, 0)
                hidden_of(0, 1)
                with pe.Fori(0, GROUPS - 1) as g:
                    for j in range(2, GROUP + 2):
                        hidden_of(g, j)
                    out_of(g)
                hidden_of(GROUPS - 1, 2)
                hidden_of(GROUPS - 1, 3)
                out_of(GROUPS - 1)

            @block.vector
            def _(dve):
                nc.vector.memset(weight[:], 0.0).then_inc(used, CREDIT)
                dve.sem_inc(added, BANKS)
                dve.wait_ge(rows_in, 16)

                def dense_v(g, j):
                    dve.wait_ge(v_high, g * GROUP + (j + 1))
                    nc.vector.tensor_tensor(v_lo[:, j], v_raw[:, j % 2], v_hi[:, j].bitcast(F32), ALU.subtract).then_inc(v_split, 1)

                def dense_gate(g, j):
                    c = g * GROUP + j
                    dve.wait_ge(gate_in[j % 2], g * (GROUP // 2 * 16) + (16 * (j // 2 + 1)))
                    dve.wait_ge(act_done, c + 1)
                    nc.vector.tensor_tensor(a[:, j % 2], a[:, j % 2], g_in[:, j % 2], ALU.mult).then_inc(gated, 1)

                def dense_low(g, j):
                    dve.wait_ge(a_high, g * GROUP + (j + 1))
                    nc.vector.tensor_tensor(a_lo[:, j], a[:, j % 2], a_hi[:, j].bitcast(F32), ALU.subtract).then_inc(a_split, 1)

                def dense_add(g, n):
                    place = x2[:, n // 2, (n % 2) * HALF:(n % 2 + 1) * HALF]
                    dve.wait_ge(o_done, g * TURNS + (n + 1))
                    nc.vector.tensor_tensor(place, o_ps[:, n % BANKS], place, ALU.add).then_inc(added, 1)

                def group(g, gathered):
                    for j in range(GROUP):
                        gathered(4 * j)
                        gathered(4 * j + 1)
                        dense_gate(g, j)
                        dense_v(g, j)
                        gathered(4 * j + 2)
                        gathered(4 * j + 3)
                        dense_low(g, j)
                    for n in range(TURNS):
                        gathered(16 + 2 * n)
                        gathered(17 + 2 * n)
                        dense_add(g, n)

                with dve.Fori(0, NB - DB) as b:
                    row = x2[:, bass.ds(b + DB, 1)].rearrange("p o d -> p (o d)")
                    dve.wait_ge(summed, b)
                    nc.vector.memset(acc[:], 0.0).then_inc(zeroed, 1)
                    nc.vector.scalar_tensor_tensor(out=xt[:], in0=row, scalar=rstd[:, bass.ds(b + DB, 1)], in1=g2[:], op0=ALU.mult, op1=ALU.mult).then_inc(xt_ready, 1)
                    dve.wait_ge(xt_ready, b + 1)
                    C.settle(dve, "dve")
                    with dve.Fori(0, HALF_BLOCK // 2) as i:
                        for p in range(2):
                            g = b * (2 * HALF_BLOCK) + i * 2 + p
                            dve.wait_ge(gelued, b * HALF_BLOCK + i * 2)

                            def dot(n, g=g, p=p):
                                dve.wait_ge(ring_in[n % RING], g * (GU // RING * 16) + (n // RING + 1) * 16)
                                nc.vector.tensor_tensor_reduce(out=ring[:, n % RING], in0=ring[:, n % RING], in1=xt[:], scale=1.0, scalar=0.0, op0=ALU.mult,
                                                               op1=ALU.add, accum_out=hidden[:, p, n:n + 1]).then_inc(used, 1)

                            group(g, dot)
                    dve.wait_ge(gelued, (b + 1) * HALF_BLOCK)
                    nc.vector.tensor_tensor(weight[:], active[:], gates[:, bass.ds(b, 1)].rearrange("p o k -> p (o k)"), ALU.mult).then_inc(weighed, 1)
                    dve.wait_ge(weighed, b + 1)
                    dve.wait_ge(zeroed, b + 1)
                    C.settle(dve, "dve")
                    with dve.Fori(0, HALF_BLOCK // 2) as i:
                        for p in range(2):
                            g = b * (2 * HALF_BLOCK) + i * 2 + (HALF_BLOCK + p)

                            def add(n, g=g, p=p, i=i):
                                dve.wait_ge(ring_in[n % RING], g * (GU // RING * 16) + (n // RING + 1) * 16)
                                dve.wait_ge(used, g * GU + (CREDIT + n - 1))
                                into = acc[:] if n % 2 else row
                                nc.vector.scalar_tensor_tensor(out=into, in0=ring[:, n % RING], scalar=weight[:, bass.ds((i * 2 + p) * GU + n, 1)],
                                                               in1=into, op0=ALU.mult, op1=ALU.add).then_inc(used, 1)

                            group(g, add)
                    dve.wait_ge(used, (b + 1) * (2 * SLOTS) + CREDIT)
                    nc.vector.tensor_tensor(row, row, acc[:], ALU.add).then_inc(summed, 1)


def final_norm(nc, A, C, x2, out):
    with ExitStack() as ctx:
        sb = lambda n, s, d=F32: ctx.enter_context(nc.sbuf_tensor(n, s, d))
        sem = ctx.enter_context(Semaphores(nc))
        gf = sb("fn_g", [P, D])
        junk = sb("fn_junk", [P, D])
        res = sb("fn_res", [P, NB, D])
        ss, root, rstd, tmp = (sb(f"fn_{n}", [P, NB]) for n in ("ss", "root", "rstd", "tmp"))
        row_in, squared, rooted, link, normed, stored = (sem(f"fn_{n}") for n in ("row_in", "squared", "rooted", "link", "normed", "stored"))
        with nc.Block() as block:
            @block.sync
            def _(sp):
                sp.dma_start(gf[:], A["final_g"].to_broadcast([P, D])).then_inc(row_in, 16)
                for b in range(NB):
                    sp.wait_ge(normed, b + 1)
                    sp.dma_start(out[b * P:(b + 1) * P], res[:, b]).then_inc(stored, 16)
                sp.wait_ge(stored, 16 * NB)

            @block.scalar
            def _(act):
                for b in range(NB):
                    if b:
                        act.wait_ge(squared, b)
                    nc.scalar.activation(junk[:], x2[:, b], ACT.Square, accum_out=ss[:, b:b + 1]).then_inc(squared, 1)
                act.wait_ge(squared, NB)
                nc.scalar.activation(root[:], ss[:], ACT.Sqrt, bias=C.eps[:, 0:1], scale=1.0 / D).then_inc(rooted, 1)

            @block.vector
            def _(dve):
                dve.wait_ge(rooted, 1)
                refine_rstd(nc, dve, link, [0], rstd[:], root[:], ss[:], tmp[:], D)
                dve.wait_ge(row_in, 16)
                for b in range(NB):
                    nc.vector.scalar_tensor_tensor(out=res[:, b], in0=x2[:, b], scalar=rstd[:, b:b + 1], in1=gf[:], op0=ALU.mult, op1=ALU.mult).then_inc(normed, 1)


def build(nc, A, gate_chunks, out):
    with ExitStack() as ctx:
        C = Consts(ctx, nc)

        def sb(c, n, shape, d=F32, side=None):
            return c.enter_context(nc.sbuf_tensor(n, shape, d, side=side) if side else nc.sbuf_tensor(n, shape, d))

        with ExitStack() as mixer:
            m = sb(mixer, "qk_then_o_then_m", [P, NC, T])
            with ExitStack() as normed:
                xn_hi, xn_lo = sb(normed, "xn_hi", [P, NC, T], F32R), sb(normed, "xn_lo", [P, NC, T], F32R)
                norm_first(nc, A, C, xn_hi, xn_lo)
                with ExitStack() as g:
                    v = sb(g, "v", [P, NH, NB, DV])
                    bcum = sb(g, "bcum", [P, 2, NH, T])
                    gla_inputs(nc, A, C, xn_hi, xn_lo, m, v, bcum)
                    gla(nc, A, C, m, v, bcum)
                with ExitStack() as g:
                    hi, lo = sb(g, "branch_hi", [P, NC, T], F32R), sb(g, "branch_lo", [P, NC, T], F32R)
                    gla_gate(nc, A, C, xn_hi, xn_lo, m, hi, lo)
                    branch(nc, A, C, "bb", "stream_b", 64, hi, lo, xn_hi, xn_lo, m, False)
                    conv(nc, A, C, xn_hi, xn_lo, hi, lo)
                    branch(nc, A, C, "ba", "stream_a", 56, hi, lo, xn_hi, xn_lo, m, True)
            x2 = sb(ctx, "x2", [P, NB, D], side="right")
            ss, rstd = sb(ctx, "ss2", [P, NB], side="right"), sb(ctx, "rstd2", [P, NB], side="right")
            out_project(nc, A, C, m, x2, ss)
        with ExitStack() as second:
            xd_hi, xd_lo = sb(second, "xd_hi", [P, NC, DT], F32R), sb(second, "xd_lo", [P, NC, DT], F32R)
            experts, gates = sb(second, "experts", [P, NB - DB, SLOTS], U32), sb(second, "gates", [P, NB - DB, SLOTS])
            with ExitStack() as routed:
                halves, dense_gates = sb(routed, "halves", [P, 2, DB, SLOTS]), sb(routed, "dense_gates", [P, DB, SLOTS])
                with ExitStack() as t:
                    xg_hi, xg_lo = sb(t, "xg_hi", [P, NC, T - DT], F32R), sb(t, "xg_lo", [P, NC, T - DT], F32R)
                    norm_second(nc, A, C, x2, ss, rstd, (xd_hi, xg_hi), (xd_lo, xg_lo))
                    route(nc, A, C, (xd_hi, xg_hi), (xd_lo, xg_lo), halves, dense_gates, experts, gates)
                gate_tables(nc, A, C, halves, dense_gates, gate_chunks)
            peer(nc, A, C, x2, rstd, xd_hi, xd_lo, experts, gates, gate_chunks)
        final_norm(nc, A, C, x2, out)


def feature_chunks(w):
    return w.reshape(NC, P, w.shape[1] // P, P).transpose(2, 1, 0, 3)


def kernel(**inputs):
    import concourse.bacc as bacc
    from concourse.bass_utils import run_bass_kernel_spmd

    I = {k: np.asarray(a) for k, a in inputs.items()}
    one = lambda k: I[k][0]
    cut = np.cumsum([D, D, D, NH * DK, NH * DK, D, D, RANK, RANK, D, D])[:-1]
    xa, ba, ca, q, k, v, r, zf, zb, ga, gb = np.split(one("w_in"), cut, axis=1)
    z = np.zeros((D, P), np.float32)
    z[:, 0:RANK], z[:, 32:32 + RANK] = zf, zb
    up = np.zeros((P, NH * DK), np.float32)
    up[0:RANK], up[32:32 + RANK] = one("decay_up_f"), one("decay_up_b")
    pairs = lambda *ws: np.stack([feature_chunks(w) for w in ws], 1).reshape(-1, P, NC, P)
    col = lambda a: a.reshape(-1, P).T
    cols = np.concatenate([col(one("norm1_g")), col(one("decay_bias_f")), col(one("decay_bias_b")), col(one("gla_norm_g")),
                           col(one("conv_w")), col(one("conv_b")), col(one("gate_bias"))], 1)
    arrays = {
        "x": I["x"].reshape(NB, P, D),
        "cols": cols,
        "up": up,
        "stream_g": np.concatenate([feature_chunks(z), pairs(k, q), feature_chunks(v).reshape(NH, 2, P, NC, P)[:, ::-1].reshape(-1, P, NC, P)]),
        "stream_r": feature_chunks(r),
        "stream_b": pairs(gb, one("wb_proj")),
        "stream_conv": pairs(ca, xa, ba),
        "stream_a": pairs(ga, one("wa_proj")),
        "w_out": one("w_out").reshape(NC, P, D),
        "stream_q": feature_chunks(one("peer_wq")),
        "keys": one("peer_keys").reshape(2 * PH, NKEYS, P).transpose(2, 0, 1),
        "norm2_g": I["norm2_g"].reshape(1, D),
        "final_g": I["final_norm_g"].reshape(1, D),
        "peer_u": one("peer_u"),
        "peer_ut": feature_chunks(one("peer_u").T),
        "peer_v": one("peer_v"),
    }
    arrays = {n: np.ascontiguousarray(a) for n, a in arrays.items()}
    nc = bacc.Bacc("TRN2", target_bir_lowering=False, num_devices=1)
    A = {n: nc.dram_tensor(f"in_{n}", a.shape, mybir.dt.from_np(a.dtype), kind="ExternalInput").ap() for n, a in arrays.items()}
    out = nc.dram_tensor("out_x", (T, D), F32, kind="ExternalOutput").ap()
    gate_chunks = nc.dram_tensor("gate_chunks", (NKEYS, P, DT), F32, kind="Internal").ap()
    build(nc, A, gate_chunks, out)
    r = run_bass_kernel_spmd(nc, [{f"in_{n}": a for n, a in arrays.items()}], core_ids=[0])
    return np.asarray(r.results[0]["out_x"]).reshape(1, T, D)


class Consts:
    NCOL = 72

    def __init__(self, ctx, nc):
        sb = lambda n, s, d=F32: ctx.enter_context(nc.sbuf_tensor(n, s, d))
        self.cols = sb("c_cols", [P, self.NCOL])
        self.up = sb("c_up", [P, NH * DK])
        self.ident = sb("c_ident", [P, P])
        self.ones = sb("c_ones", [P, P])
        self.mask = sb("c_mask", [P, 2, P])
        self.eps = sb("c_eps", [P, 1])
        self.begun = ctx.enter_context(nc.semaphore("c_begun"))
        self.passed = {e: ctx.enter_context(nc.semaphore(f"c_passed_{e}")) for e in ("act", "dve", "pool")}

    def settle(self, engine, name):
        engine.sem_inc(self.passed[name], 1)

    def col(self, first, c):
        return self.cols[:, bass.ds(c + first, 1)]

    def norm1_g(self, c):
        return self.cols[:, c:c + 1]

    def decay_bias(self, d, h):
        return self.cols[:, 8 + 4 * d + h:9 + 4 * d + h]
```

```python
import numpy as np
import concourse.bass as bass
from concourse import mybir
from contextlib import ExitStack

F32 = mybir.dt.float32
F32R = mybir.dt.float32r
U32 = mybir.dt.uint32
ALU = mybir.AluOpType
ACT = mybir.ActivationFunctionType
AX = mybir.AxisListType

P = 128
T = 1024
D = 1024
NB = T // P
NC = D // P
HALF = 512
NH = 4
DK = 128
DV = 256
NE = DV // P
CH = 64
NCH = T // CH
RANK = 16
TAU = 16.0
EPS = 1e-6
PH = 8
NKEYS = 128
TOPK = 16
SLOTS = PH * TOPK
RING = 8
DB = 5
DT = DB * P
GROUP = 4
NEG = -3.4e38

S_Z, S_KQ, S_V, S_R, S_BG, S_CONV, S_AG = 0, 1, 9, 17, 25, 41, 65


class Semaphores:

    def __init__(self, nc):
        self.nc, self.taken = nc, []

    def __call__(self, name):
        self.taken.append(self.nc.alloc_semaphore(name))
        return self.taken[-1]

    def __enter__(self):
        return self

    def __exit__(self, *error):
        if error[0] is None:
            self.nc.clear_and_free_semaphores(self.taken)
            self.nc.all_engine_barrier()


class Weights:

    def __init__(self, ctx, nc, sem, tag):
        self.raw = ctx.enter_context(nc.sbuf_tensor(f"w_raw_{tag}", [P, 2, NC, P], F32))
        self.hi = ctx.enter_context(nc.sbuf_tensor(f"w_hi_{tag}", [P, 2, NC, P], F32R))
        self.lo = ctx.enter_context(nc.sbuf_tensor(f"w_lo_{tag}", [P, 2, NC, P], F32R))
        self.loaded = [sem(f"w_loaded{s}_{tag}") for s in range(2)]
        self.high, self.split, self.used = sem(f"w_high_{tag}"), sem(f"w_split_{tag}"), sem(f"w_used_{tag}")


def load_weights(sp, w, stream, first, count):
    for s in range(2):
        sp.dma_start(w.raw[:, s], stream[first + s]).then_inc(w.loaded[s], 16)
    with sp.Fori(1, count // 2) as i:
        for s in range(2):
            sp.wait_ge(w.split, i * 2 + s - 1)
            sp.dma_start(w.raw[:, s], stream[bass.ds(i * 2 + (first + s), 1)].rearrange("o p k m -> (o p) k m")).then_inc(w.loaded[s], 16)
    if count % 2:
        sp.wait_ge(w.split, count - 2)
        sp.dma_start(w.raw[:, 0], stream[first + count - 1]).then_inc(w.loaded[0], 16)


def split_chunk(nc, pool, C, w, s, n, loaded16):
    pool.wait_ge(w.loaded[s], loaded16)
    C.settle(pool, "pool")
    nc.gpsimd.tensor_copy(w.hi[:, s], w.raw[:, s]).then_inc(w.high, 1)
    pool.wait_ge(w.high, n + 1)
    nc.gpsimd.tensor_tensor(w.lo[:, s], w.raw[:, s], w.hi[:, s].bitcast(F32), ALU.subtract).then_inc(w.split, 1)


def split_weights(nc, pool, C, w, count):
    for s in range(2):
        split_chunk(nc, pool, C, w, s, s, 16)
    with pool.Fori(1, count // 2) as i:
        for s in range(2):
            pool.wait_ge(w.used, i * 2 + s - 1)
            split_chunk(nc, pool, C, w, s, i * 2 + s, i * 16 + 16)


def project(nc, w, s, act_hi, act_lo, out):
    last = None
    for k in range(NC):
        for part, act, flag in ((w.hi, act_hi, 0), (w.hi, act_lo, 1), (w.lo, act_hi, 2)):
            for t in range(2):
                last = nc.tensor.matmul(out[:, t], part[:, s, k], half_of(act, t)[:, k],
                                        start=(k == 0 and flag == 0), stop=(k == NC - 1 and flag == 2))
    return last


def half_of(act, t):
    return act[t] if isinstance(act, tuple) else act[:, :, t * HALF:(t + 1) * HALF]


def norm_first(nc, A, C, xn_hi, xn_lo):
    with ExitStack() as ctx:
        sb = lambda n, s, d=F32: ctx.enter_context(nc.sbuf_tensor(n, s, d))
        sem = ctx.enter_context(Semaphores(nc))
        x = sb("n1_x", [P, NB, D])
        junk = sb("n1_junk", [P, D])
        ss = sb("n1_ss", [P, NB])
        rs = sb("n1_rs", [P, NB])
        rstd = sb("n1_rstd", [P, NB])
        ps = ctx.enter_context(nc.psum_tensor("n1_ps", [P, 2, 2, HALF], F32))
        x_in = [sem(f"n1_x_in{b}") for b in range(NB // 2)]
        consts_in, squared, rooted, inverted, scaled, turned, high, low = (
            sem(f"n1_{n}") for n in ("consts_in", "squared", "rooted", "inverted", "scaled", "turned", "high", "low"))
        made = sem("n1_consts_made")
        filled = sem("n1_consts_filled")
        with nc.Block() as block:
            @block.sync
            def _(sp):
                sp.dma_start(C.cols[:], A["cols"]).then_inc(consts_in, 16)
                for b in range(NB // 2):
                    sp.dma_start(x[:, 2 * b:2 * b + 2], A["x"][2 * b:2 * b + 2].rearrange("b p d -> p b d")).then_inc(x_in[b], 16)
                sp.dma_start(C.up[:], A["up"]).then_inc(consts_in, 16)

            @block.gpsimd
            def _(pool):
                nc.gpsimd.memset(C.ident[:], 0.0).then_inc(filled, 1)
                nc.gpsimd.memset(C.ones[:], 1.0).then_inc(filled, 1)
                nc.gpsimd.memset(C.mask[:], 1.0).then_inc(filled, 1)
                nc.gpsimd.memset(C.eps[:], EPS).then_inc(C.begun, 1)
                pool.wait_ge(filled, 3)
                nc.gpsimd.affine_select(out=C.ident[:], in_=C.ident[:], compare_op=ALU.not_equal, fill=1.0, base=0,
                                        pattern=[[-1, P]], channel_multiplier=1).then_inc(made, 1)
                nc.gpsimd.affine_select(out=C.mask[:, 0], in_=C.mask[:, 0], compare_op=ALU.is_ge, fill=0.0, base=0,
                                        pattern=[[1, P]], channel_multiplier=-1).then_inc(made, 1)
                nc.gpsimd.affine_select(out=C.mask[:, 1], in_=C.mask[:, 1], compare_op=ALU.is_ge, fill=0.0, base=0,
                                        pattern=[[-1, P]], channel_multiplier=1).then_inc(made, 1)
                pool.wait_ge(made, 3)
                nc.gpsimd.memset(C.mask[0:CH, 0, CH:P], 0.0).then_inc(made, 1)
                nc.gpsimd.memset(C.mask[CH:P, 1, 0:CH], 0.0).then_inc(made, 1)

            @block.scalar
            def _(act):
                act.wait_ge(C.begun, 1)
                for b in range(NB):
                    act.wait_ge(x_in[b // 2], 16)
                    if b:
                        act.wait_ge(squared, b)
                    nc.scalar.activation(junk[:], x[:, b], ACT.Square, accum_out=ss[:, b:b + 1]).then_inc(squared, 1)
                act.wait_ge(squared, NB)
                nc.scalar.activation(rs[:], ss[:], ACT.Sqrt, bias=C.eps[:, 0:1], scale=1.0 / D).then_inc(rooted, 1)
                act.wait_ge(consts_in, 32)
                for c in range(NC):
                    act.wait_ge(turned, c + 1)
                    nc.scalar.mul(xn_hi[:, c], ps[:, c % 2].rearrange("p a b -> p (a b)"), C.norm1_g(c)).then_inc(high, 1)

            @block.vector
            def _(dve):
                dve.wait_ge(rooted, 1)
                nc.vector.reciprocal(rstd[:], rs[:]).then_inc(inverted, 1)
                dve.wait_ge(inverted, 1)
                for b in range(NB):
                    nc.vector.tensor_scalar(x[:, b], x[:, b], rstd[:, b:b + 1], None, ALU.mult).then_inc(scaled, 1)
                for c in range(NC):
                    dve.wait_ge(high, c + 1)
                    nc.vector.scalar_tensor_tensor(out=xn_lo[:, c], in0=ps[:, c % 2].rearrange("p a b -> p (a b)"), scalar=C.norm1_g(c),
                                                   in1=xn_hi[:, c].bitcast(F32), op0=ALU.mult, op1=ALU.subtract).then_inc(low, 1)

            @block.tensor
            def _(pe):
                pe.wait_ge(made, 5)
                for c in range(NC):
                    if c >= 2:
                        pe.wait_ge(low, c - 1)
                    for b in range(NB):
                        if c == 0:
                            pe.wait_ge(scaled, b + 1)
                        last = nc.tensor.transpose(ps[:, c % 2, b // 4, (b % 4) * P:(b % 4 + 1) * P], x[:, b, c * P:(c + 1) * P], C.ident[:])
                    last.then_inc(turned, 1)


def gla_inputs(nc, A, C, xn_hi, xn_lo, qk, v, bcum):
    with ExitStack() as ctx:
        sb = lambda n, s, d=F32: ctx.enter_context(nc.sbuf_tensor(n, s, d))
        sem = ctx.enter_context(Semaphores(nc))
        w = Weights(ctx, nc, sem, "g")
        z = sb("gi_z", [P, T])
        keep = sb("gi_keep", [P, 2, T], mybir.dt.bfloat16)
        kept = sem("gi_kept")
        ps = ctx.enter_context(nc.psum_tensor("gi_ps", [P, 4, 2, HALF], F32))
        soft = v[:, :].rearrange("p h b e -> p (h b e)")[:, 0:2 * NH * T].rearrange("p (d h t) -> p d h t", d=2, h=NH)
        z_out, up_done, up_out, exped, logged, clipped, summed, out_ = (
            sem(f"gi_{n}") for n in ("z_out", "up_done", "up_out", "exped", "logged", "clipped", "summed", "out"))
        absed, v_high = sem("gi_absed"), sem("gi_v_high")
        v_done, v_out = sem("gi_v_done"), sem("gi_v_out")
        n_qk = 1 + 2 * NH
        n_chunks = n_qk + 2 * NH
        with nc.Block() as block:
            @block.sync
            def _(sp):
                load_weights(sp, w, A["stream_g"], 0, n_chunks)

            @block.gpsimd
            def _(pool):
                nc.gpsimd.memset(keep[:], 1.0).then_inc(kept, 1)
                pool.wait_ge(kept, 1)
                for d, at in ((0, 0), (1, CH - 1)):
                    nc.gpsimd.memset(keep[:, d].rearrange("p (n c) -> p n c", c=CH)[:, :, at:at + 1], 0.0).then_inc(kept, 1)
                split_weights(nc, pool, C, w, n_qk - 1)
                pool.wait_ge(w.used, n_qk - 2)
                split_chunk(nc, pool, C, w, 0, n_qk - 1, 16 * (n_qk + 1) // 2)
                pool.wait_ge(w.used, n_qk - 1)
                split_chunk(nc, pool, C, w, 1, n_qk, 16 * (n_qk + 1) // 2)
                pool.wait_ge(w.used, n_qk)
                split_chunk(nc, pool, C, w, 0, n_qk + 1, 16 * (n_qk + 3) // 2)

            @block.tensor
            def _(pe):
                pe.wait_ge(w.split, 1)
                project(nc, w, 0, xn_hi, xn_lo, ps[:, 0]).then_inc(w.used, 1)
                pe.wait_ge(z_out, 1)
                for n in range(2 * NH):
                    d, h = n // NH, n % NH
                    if n >= 2:
                        pe.wait_ge(absed, n - 1)
                    for t in range(2):
                        last = nc.tensor.matmul(ps[:, 2 + n % 2, t], C.up[32 * d:32 * d + RANK, h * DK:(h + 1) * DK],
                                                z[32 * d:32 * d + RANK, t * HALF:(t + 1) * HALF], start=True, stop=True)
                    last.then_inc(up_done, 1)
                with pe.Fori(0, NH) as h:
                    for s in range(2):
                        pe.wait_ge(w.split, h * 2 + (2 + s))
                        pe.wait_ge(out_, h * 2 + (s + 1))
                        project(nc, w, 1 - s, xn_hi, xn_lo, ps[:, s]).then_inc(w.used, 1)
                pe.wait_ge(out_, 2 * NH + 2)
                with pe.Fori(0, NH) as h:
                    pe.wait_ge(w.split, h * 2 + (n_qk + 2))
                    for b in range(NB):
                        if b % 2 == 0:
                            pe.wait_ge(v_out, h * 4 + b // 2)
                        for k in range(NC):
                            for i, (a, part) in enumerate(((xn_hi, w.hi), (xn_lo, w.hi), (xn_hi, w.lo))):
                                last = nc.tensor.matmul(
                                    ps[:, b // 4, (b // 2) % 2, (b % 2) * DV:(b % 2 + 1) * DV].rearrange("p (a m) -> p a m", a=2),
                                    a[:, k, b * P:(b + 1) * P], part[:, :, k], start=(b % 2 == 0 and k == 0 and i == 0),
                                    stop=(b % 2 == 1 and k == NC - 1 and i == 2), skip_group_check=True)
                        if b % 2:
                            last.then_inc(v_done, 1)

            @block.scalar
            def _(act):
                act.wait_ge(w.used, 1)
                nc.scalar.copy(z[:], ps[:, 0].rearrange("p a b -> p (a b)")).then_inc(z_out, 1)
                for n in range(2 * NH):
                    act.wait_ge(up_out, n + 1)
                    nc.scalar.activation(soft[:, n // NH, n % NH], ps[:, 2 + n % 2].rearrange("p a b -> p (a b)"), ACT.Abs,
                                         bias=C.decay_bias(n // NH, n % NH)).then_inc(absed, 1)
                def key_and_query(h):
                    for s in range(2):
                        act.wait_ge(w.used, h * 2 + (s + 2))
                        C.settle(act, "act")
                        nc.scalar.mul(qk[:, bass.ds(h * 2 + s, 1)].rearrange("p o t -> p (o t)"), ps[:, s].rearrange("p a b -> p (a b)"),
                                      1.0 if s == 0 else DK ** -0.5).then_inc(out_, 1)

                act.sem_inc(out_, 2)
                key_and_query(0)
                act.wait_ge(absed, 2 * NH)
                nc.scalar.activation(soft, soft, ACT.Exp, scale=-1.0).then_inc(exped, 1)
                key_and_query(1)
                act.wait_ge(exped, 1)
                nc.scalar.activation(soft, soft, ACT.Ln, bias=1.0).then_inc(logged, 1)
                with act.Fori(2, NH) as h:
                    key_and_query(h)
                act.wait_ge(summed, 2 * NH)

                def values(h):
                    for g in range(4):
                        act.wait_ge(v_done, h * 4 + (g + 1))
                        C.settle(act, "act")
                        nc.scalar.copy(v[:, bass.ds(h, 1), 2 * g:2 * g + 2].rearrange("p o b e -> p (o b e)"),
                                       ps[:, g // 2, g % 2]).then_inc(v_out, 1)

                with act.Fori(0, NH - 1) as h:
                    values(h)
                    for s in (1, 0):
                        act.wait_ge(w.loaded[s], h * 16 + 16 * ((n_qk + 1) // 2 + (2 if s == 0 else 1)))
                        nc.scalar.copy(w.hi[:, s], w.raw[:, s]).then_inc(v_high, 1)
                values(NH - 1)

            @block.vector
            def _(dve):
                for n in range(2 * NH):
                    d, h = n // NH, n % NH
                    dve.wait_ge(up_done, n + 1)
                    y = ps[:, 2 + n % 2].rearrange("p a b -> p (a b)")
                    nc.vector.tensor_scalar(bcum[:, d, h], y, C.decay_bias(d, h), 0.0, ALU.add, ALU.min).then_inc(up_out, 1)
                dve.wait_ge(logged, 1)
                dve.wait_ge(kept, 3)
                dve.wait_ge(up_out, 2 * NH)
                for n in range(2 * NH):
                    d, h = n // NH, n % NH
                    nc.vector.tensor_tensor(soft[:, d, h], bcum[:, d, h], soft[:, d, h], ALU.subtract).then_inc(clipped, 1)
                    dve.wait_ge(clipped, n + 1)
                    way = slice(None) if d == 0 else slice(None, None, -1)
                    nc.vector.tensor_tensor_scan(out=bcum[:, d, h, way], data0=keep[:, d, way], data1=soft[:, d, h, way],
                                                 initial=0.0, op0=ALU.mult, op1=ALU.add).then_inc(summed, 1)
                with dve.Fori(0, NH - 1) as h:
                    for n, s in enumerate((1, 0)):
                        dve.wait_ge(v_high, h * 2 + (n + 1))
                        nc.vector.tensor_tensor(w.lo[:, s], w.raw[:, s], w.hi[:, s].bitcast(F32), ALU.subtract).then_inc(w.split, 1)


def gla(nc, A, C, qk, v, bcum):
    with ExitStack() as ctx:
        sb = lambda n, s, d=F32: ctx.enter_context(nc.sbuf_tensor(n, s, d))
        sem = ctx.enter_context(Semaphores(nc))
        qki = sb("gl_qk_in", [P, 2, T])
        q_dec = sb("gl_q_dec", [P, T])
        k_end = sb("gl_k_end", [P, T])
        k_tok = sb("gl_k_tok", [P, NB, DK])
        sc = sb("gl_sc", [P, 2, NB, P])
        v_h = sb("gl_v_h", [P, NB, DV])
        state = sb("gl_state", [P, 4, DV])
        dec = sb("gl_dec", [P, 2, NCH])
        o_ps = ctx.enter_context(nc.psum_tensor("gl_o", [P, NE, 2, HALF], F32))
        sc_ps = ctx.enter_context(nc.psum_tensor("gl_sc_ps", [P, 2, 4, P], F32))
        u_ps = ctx.enter_context(nc.psum_tensor("gl_u_ps", [P, 2, HALF], F32))[:, :, 0:DV]
        (d1, d2, ex_q, ex_k, ex_end, ex_dec, ex_last, m_in, m_end, m_dec, v_in, scored, masked, turned, tok, u_done, s_done,
         inter, intra, sq, ssum, rooted, inv, o_out, zeroed) = (sem(f"gl_{n}") for n in (
             "diff", "end_diff", "exp_q", "exp_k", "exp_end", "exp_dec", "exp_last", "in_ready", "end_ready", "dec_ready", "v_copied",
             "scored", "masked", "turned", "tok_ready", "u_done", "state_ready", "inter_done", "intra_done", "squared",
             "sq_summed", "rooted", "inverted", "o_out", "zeroed"))

        def chunked(ap):
            return ap.rearrange("p (n c) -> p n c", c=CH)

        def head(tile, h):
            return tile[:, bass.ds(h, 1)].rearrange("p o t -> p (o t)")

        def sums(d, h):
            return bcum[:, d, bass.ds(h, 1)].rearrange("p o t -> p (o t)")

        def at(d, h, i):
            return chunked(sums(d, h))[:, :, i:i + 1].to_broadcast([P, NCH, CH])

        REF = (CH // 2, CH - 1 - CH // 2)
        LAST = (CH - 1, 0)
        US = NCH - 1
        with nc.Block() as block:
            @block.vector
            def _(dve):
                nc.vector.memset(sc[:], 0.0).then_inc(zeroed, 1)
                dve.wait_ge(zeroed, 1)

                def difference(h, d):
                    dve.wait_ge(scored, (h * 2 + d) * 2)
                    if d == 0:
                        dve.wait_ge(ssum, h)
                    nc.vector.tensor_tensor(chunked(qki[:, 1]), chunked(sums(d, h)), at(d, h, REF[d]), ALU.subtract).then_inc(d1, 1)

                def queries_in(h, d):
                    dve.wait_ge(ex_q, h * 2 + (d + 1))
                    nc.vector.tensor_tensor(qki[:, 1], qki[:, 1], head(qk, h * 2 + 1), ALU.mult).then_inc(m_in, 1)

                def keys_in(h, d):
                    dve.wait_ge(ex_k, h * 2 + (d + 1))
                    nc.vector.tensor_tensor(qki[:, 0], qki[:, 0], head(qk, h * 2), ALU.mult).then_inc(m_in, 1)

                ahead = {4: difference, 9: queries_in, 11: keys_in}
                with dve.Fori(0, NH) as h:
                    for d in range(2):
                        n = h * 2 + d
                        if d == 0:
                            difference(h, 0)
                            queries_in(h, 0)
                            keys_in(h, 0)
                        for g in range(2):
                            dve.wait_ge(scored, n * 2 + (g + 1))
                            if g == 0:
                                dve.wait_ge(intra, n)
                            C.settle(dve, "dve")
                            nc.vector.copy_predicated(sc[:, d, 4 * g:4 * g + 4], C.mask[:, d:d + 1].to_broadcast([P, 4, P]).bitcast(U32),
                                                      sc_ps[:, g]).then_inc(masked, 1)
                        dve.wait_ge(ex_last, n + 1)
                        for i in range(US):
                            if d == 0 and i in ahead:
                                ahead[i](h, 1)
                            c = i if d == 0 else NCH - 1 - i
                            dve.wait_ge(u_done, n * US + (i + 1))
                            if i < 4:
                                dve.wait_ge(inter, n * US)
                            else:
                                dve.wait_ge(inter, n * US + (i - 3))
                            if i == 0:
                                nc.vector.tensor_copy(state[:, 0], u_ps[:, 0]).then_inc(s_done, 1)
                            else:
                                dve.wait_ge(s_done, n * US + i)
                                nc.vector.scalar_tensor_tensor(out=state[:, i % 4], in0=state[:, (i - 1) % 4], scalar=dec[:, d, c:c + 1],
                                                               in1=u_ps[:, i % 2], op0=ALU.mult, op1=ALU.add).then_inc(s_done, 1)
                    dve.wait_ge(rooted, h + 1)
                    nc.vector.reciprocal(k_end[:], k_end[:]).then_inc(inv, 1)
                    dve.wait_ge(inv, h + 1)
                    dve.wait_ge(m_dec, h * 2 + 2)
                    dve.wait_ge(m_end, h * 2 + 2)
                    for e in range(NE):
                        nc.vector.tensor_tensor(head(qk, h * 2 + e), o_ps[:, e].rearrange("p a b -> p (a b)"), k_end[:], ALU.mult).then_inc(o_out, 1)

            @block.gpsimd
            def _(pool):
                with pool.Fori(0, NH) as h:
                    pool.wait_ge(inter, h * (2 * US))
                    C.settle(pool, "pool")
                    nc.gpsimd.tensor_copy(v_h[:], v[:, bass.ds(h, 1)].rearrange("p o b e -> p (o b) e")).then_inc(v_in, 1)
                    for d in range(2):
                        n = h * 2 + d
                        pool.wait_ge(turned, n * 2)
                        if d == 0:
                            pool.wait_ge(o_out, h * NE)
                        C.settle(pool, "pool")
                        nc.gpsimd.tensor_tensor(chunked(k_end[:]), at(d, h, LAST[d]), chunked(sums(d, h)), ALU.subtract).then_inc(d2, 1)
                        pool.wait_ge(ex_end, n + 1)
                        C.settle(pool, "pool")
                        nc.gpsimd.tensor_tensor(k_end[:], k_end[:], head(qk, h * 2), ALU.mult).then_inc(m_end, 1)
                        pool.wait_ge(ex_dec, n + 1)
                        C.settle(pool, "pool")
                        nc.gpsimd.tensor_tensor(q_dec[:], q_dec[:], head(qk, h * 2 + 1), ALU.mult).then_inc(m_dec, 1)

            @block.scalar
            def _(act):
                with act.Fori(0, NH) as h:
                    for d in range(2):
                        n = h * 2 + d
                        act.wait_ge(d1, n + 1)
                        nc.scalar.activation(qki[:, 0], qki[:, 1], ACT.Exp, scale=-1.0 / TAU).then_inc(ex_k, 1)
                        act.wait_ge(ex_k, n + 1)
                        nc.scalar.activation(qki[:, 1], qki[:, 1], ACT.Exp, scale=1.0 / TAU).then_inc(ex_q, 1)
                        act.wait_ge(d2, n + 1)
                        nc.scalar.activation(k_end[:], k_end[:], ACT.Exp, scale=1.0 / TAU).then_inc(ex_end, 1)
                        act.wait_ge(s_done, n * US)
                        C.settle(act, "act")
                        nc.scalar.activation(dec[:, d].rearrange("p (n o) -> p n o", o=1), chunked(sums(d, h))[:, :, LAST[d]:LAST[d] + 1],
                                             ACT.Exp, scale=1.0 / TAU).then_inc(ex_last, 1)
                        act.wait_ge(inter, n * US)
                        C.settle(act, "act")
                        nc.scalar.activation(q_dec[:], sums(d, h), ACT.Exp, scale=1.0 / TAU).then_inc(ex_dec, 1)
                        for g in range(2):
                            act.wait_ge(turned, n * 2 + (g + 1))
                            if g == 0:
                                act.wait_ge(u_done, n * US)
                            nc.scalar.copy(k_tok[:, 4 * g:4 * g + 4], sc_ps[:, g]).then_inc(tok, 1)
                    act.wait_ge(inter, h * (2 * US) + 2 * US)
                    for e in range(NE):
                        nc.scalar.activation(qki[:, e], o_ps[:, e].rearrange("p a b -> p (a b)"), ACT.Square).then_inc(sq, 1)
                    act.wait_ge(ssum, h + 1)
                    nc.scalar.activation(k_end[:], sc_ps[:].rearrange("p a b c -> p (a b c)"), ACT.Sqrt, bias=C.eps[:, 0:1], scale=1.0 / DV).then_inc(rooted, 1)

            @block.tensor
            def _(pe):
                with pe.Fori(0, NH) as h:
                    pe.wait_ge(v_in, h + 1)
                    for d in range(2):
                        n = h * 2 + d
                        pe.wait_ge(m_in, n * 2 + 2)
                        if d == 0:
                            pe.wait_ge(rooted, h)
                        else:
                            pe.wait_ge(tok, h * 4 + 2)
                        for b in range(NB):
                            m = nc.tensor.matmul(sc_ps[:, b // 4, b % 4], qki[:, 0, b * P:(b + 1) * P], qki[:, 1, b * P:(b + 1) * P],
                                                 start=(b % 4 == 0), stop=(b % 4 == 3), skip_group_check=True)
                            if b % 4 == 3:
                                m.then_inc(scored, 1)
                        pe.wait_ge(m_end, n + 1)
                        for g in range(2):
                            pe.wait_ge(masked, n * 2 + (g + 1))
                            for b in range(4):
                                m = nc.tensor.transpose(sc_ps[:, g, b], k_end[:, (4 * g + b) * P:(4 * g + b + 1) * P], C.ident[:])
                            m.then_inc(turned, 1)
                        pe.wait_ge(masked, n * 2 + 2)
                        if d == 0:
                            pe.wait_ge(o_out, h * NE)
                        for b in range(NB):
                            for e in range(NE):
                                m = nc.tensor.matmul(o_ps[:, e, b // 4, (b % 4) * P:(b % 4 + 1) * P], v_h[:, b, e * P:(e + 1) * P],
                                                     sc[:, d, b], start=(d == 0 and b % 4 == 0), stop=False, skip_group_check=True)
                        m.then_inc(intra, 1)
                        pe.wait_ge(tok, n * 2 + 2)
                        pe.wait_ge(m_dec, n + 1)

                        def update(i):
                            c = i if d == 0 else NCH - 1 - i
                            rows = slice((c % 2) * CH, (c % 2 + 1) * CH)
                            pe.wait_ge(s_done, n * US + max(i - 1, 0))
                            nc.tensor.matmul(u_ps[:, i % 2], k_tok[rows, c // 2], v_h[rows, c // 2], start=True, stop=True,
                                             skip_group_check=True).then_inc(u_done, 1)

                        update(0)
                        for i in range(US):
                            if i + 1 < US:
                                update(i + 1)
                            c = i + 1 if d == 0 else NCH - 2 - i
                            pe.wait_ge(s_done, n * US + (i + 1))
                            for e in range(NE):
                                m = nc.tensor.matmul(o_ps[:, e, c // 8, (c % 8) * CH:(c % 8 + 1) * CH], state[:, i % 4, e * P:(e + 1) * P],
                                                     q_dec[:, c * CH:(c + 1) * CH], start=False, stop=False, skip_group_check=True)
                            m.then_inc(inter, 1)
                    pe.wait_ge(tok, h * 4 + 4)
                    for e in range(NE):
                        pe.wait_ge(sq, h * NE + (e + 1))
                        for t in range(2):
                            m = nc.tensor.matmul(sc_ps[:, t].rearrange("p a b -> p (a b)"), C.ones[:], qki[:, e, t * HALF:(t + 1) * HALF],
                                                 start=(e == 0), stop=(e == NE - 1), skip_group_check=True)
                    m.then_inc(ssum, 1)


def gla_gate(nc, A, C, xn_hi, xn_lo, o, on_hi, on_lo):
    with ExitStack() as ctx:
        sb = lambda n, s, d=F32: ctx.enter_context(nc.sbuf_tensor(n, s, d))
        sem = ctx.enter_context(Semaphores(nc))
        w = Weights(ctx, nc, sem, "r")
        gated = sb("gg_gated", [P, 2, T])
        ps = ctx.enter_context(nc.psum_tensor("gg_ps", [P, 2, 2, HALF], F32))
        silu, mixed, high, low = (sem(f"gg_{n}") for n in ("silu", "mixed", "high", "low"))
        with nc.Block() as block:
            @block.sync
            def _(sp):
                load_weights(sp, w, A["stream_r"], 0, NC)

            @block.gpsimd
            def _(pool):
                split_weights(nc, pool, C, w, NC)

            @block.tensor
            def _(pe):
                with pe.Fori(0, NC // 2) as i:
                    for s in range(2):
                        pe.wait_ge(w.split, i * 2 + (s + 1))
                        pe.wait_ge(silu, i * 2)
                        project(nc, w, s, xn_hi, xn_lo, ps[:, s]).then_inc(w.used, 1)

            @block.scalar
            def _(act):
                with act.Fori(0, NC // 2) as i:
                    for s in range(2):
                        act.wait_ge(w.used, i * 2 + (s + 1))
                        act.wait_ge(low, i * 2)
                        nc.scalar.activation(gated[:, s], ps[:, s].rearrange("p a b -> p (a b)"), ACT.Silu).then_inc(silu, 1)
                    for s in range(2):
                        act.wait_ge(mixed, i * 2 + (s + 1))
                        C.settle(act, "act")
                        nc.scalar.copy(chunk(on_hi, i * 2 + s), gated[:, s]).then_inc(high, 1)

            @block.vector
            def _(dve):
                with dve.Fori(0, NC // 2) as i:
                    for s in range(2):
                        dve.wait_ge(silu, i * 2 + (s + 1))
                        nc.vector.scalar_tensor_tensor(out=gated[:, s], in0=chunk(o, i * 2 + s), scalar=C.col(16, i * 2 + s),
                                                       in1=gated[:, s], op0=ALU.mult, op1=ALU.mult).then_inc(mixed, 1)
                    for s in range(2):
                        dve.wait_ge(high, i * 2 + (s + 1))
                        nc.vector.tensor_tensor(chunk(on_lo, i * 2 + s), gated[:, s], chunk(on_hi, i * 2 + s).bitcast(F32),
                                                ALU.subtract).then_inc(low, 1)


def chunk(tile, c):
    return tile[:, bass.ds(c, 1)].rearrange("p o t -> p (o t)")


def branch(nc, A, C, tag, stream, bias, act_hi, act_lo, xn_hi, xn_lo, m, add):
    with ExitStack() as ctx:
        sb = lambda n, s, d=F32: ctx.enter_context(nc.sbuf_tensor(n, s, d))
        sem = ctx.enter_context(Semaphores(nc))
        w = Weights(ctx, nc, sem, tag)
        gate = sb(f"{tag}_gate", [P, 2, T])
        ps = ctx.enter_context(nc.psum_tensor(f"{tag}_ps", [P, 2, 2, 2, HALF], F32))
        gated, product = (sem(f"{tag}_{n}") for n in ("gated", "product"))
        mixed = sem(f"{tag}_mixed") if add else product
        flat = lambda ap: ap.rearrange("p a b -> p (a b)")
        with nc.Block() as block:
            @block.sync
            def _(sp):
                load_weights(sp, w, A[stream], 0, 2 * NC)

            @block.gpsimd
            def _(pool):
                split_weights(nc, pool, C, w, 2 * NC)

            @block.tensor
            def _(pe):
                with pe.Fori(0, NC // 2) as i:
                    for s in range(2):
                        pe.wait_ge(gated, i * 2)
                        pe.wait_ge(w.split, i * 4 + (2 * s + 1))
                        project(nc, w, 0, xn_hi, xn_lo, ps[:, s, 0]).then_inc(w.used, 1)
                        pe.wait_ge(w.split, i * 4 + (2 * s + 2))
                        pe.wait_ge(product, i * 2)
                        project(nc, w, 1, act_hi, act_lo, ps[:, s, 1]).then_inc(w.used, 1)

            @block.scalar
            def _(act):
                with act.Fori(0, NC // 2) as i:
                    for s in range(2):
                        act.wait_ge(w.used, i * 4 + (2 * s + 1))
                        act.wait_ge(mixed, i * 2)
                        C.settle(act, "act")
                        nc.scalar.activation(gate[:, s], flat(ps[:, s, 0]), ACT.Sigmoid, bias=C.col(bias, i * 2 + s)).then_inc(gated, 1)

            @block.vector
            def _(dve):
                with dve.Fori(0, NC // 2) as i:
                    for s in range(2):
                        dve.wait_ge(w.used, i * 4 + (2 * s + 2))
                        dve.wait_ge(gated, i * 2 + (s + 1))
                        if not add:
                            nc.vector.tensor_tensor(chunk(m, i * 2 + s), flat(ps[:, s, 1]), gate[:, s], ALU.mult).then_inc(product, 1)
                        else:
                            nc.vector.tensor_tensor(gate[:, s], flat(ps[:, s, 1]), gate[:, s], ALU.mult).then_inc(product, 1)
                            dve.wait_ge(product, i * 2 + (s + 1))
                            nc.vector.tensor_tensor(chunk(m, i * 2 + s), chunk(m, i * 2 + s), gate[:, s], ALU.add).then_inc(mixed, 1)


def conv(nc, A, C, xn_hi, xn_lo, y_hi, y_lo):
    with ExitStack() as ctx:
        sb = lambda n, s, d=F32: ctx.enter_context(nc.sbuf_tensor(n, s, d))
        sem = ctx.enter_context(Semaphores(nc))
        w = Weights(ctx, nc, sem, "c")
        ca = sb("cv_ca", [P, T])
        u = sb("cv_u", [P, T + 2])
        y = sb("cv_y", [P, T])
        ps = ctx.enter_context(nc.psum_tensor("cv_ps", [P, 3, 2, HALF], F32))
        ca_out, padded, u_done, step, y_done, high, low = (sem(f"cv_{n}") for n in ("ca_out", "padded", "u_done", "step", "y_done", "high", "low"))
        flat = lambda ap: ap.rearrange("p a b -> p (a b)")
        with nc.Block() as block:
            @block.sync
            def _(sp):
                load_weights(sp, w, A["stream_conv"], 0, 3 * NC)

            @block.gpsimd
            def _(pool):
                split_weights(nc, pool, C, w, 3 * NC)

            @block.tensor
            def _(pe):
                with pe.Fori(0, NC // 2) as i:
                    for n in range(6):
                        pe.wait_ge(w.split, i * 6 + (n + 1))
                        pe.wait_ge((ca_out, u_done, y_done)[n % 3], i * 2 + n // 3)
                        project(nc, w, n % 2, xn_hi, xn_lo, ps[:, n % 3]).then_inc(w.used, 1)

            @block.scalar
            def _(act):
                with act.Fori(0, NC // 2) as i:
                    for s in range(2):
                        act.wait_ge(w.used, i * 6 + (3 * s + 1))
                        act.wait_ge(u_done, i * 2 + s)
                        nc.scalar.copy(ca[:], flat(ps[:, 0])).then_inc(ca_out, 1)
                        act.wait_ge(y_done, i * 2 + (s + 1))
                        C.settle(act, "act")
                        nc.scalar.copy(chunk(y_hi, i * 2 + s), y[:]).then_inc(high, 1)

            @block.vector
            def _(dve):
                nc.vector.memset(u[:, 0:1], 0.0).then_inc(padded, 1)
                nc.vector.memset(u[:, T + 1:T + 2], 0.0).then_inc(padded, 1)
                dve.wait_ge(padded, 2)
                with dve.Fori(0, NC // 2) as i:
                    for s in range(2):
                        c = i * 2 + s
                        dve.wait_ge(w.used, i * 6 + (3 * s + 2))
                        dve.wait_ge(ca_out, c + 1)
                        nc.vector.tensor_tensor(u[:, 1:T + 1], flat(ps[:, 1]), ca[:], ALU.mult).then_inc(u_done, 1)
                        dve.wait_ge(u_done, c + 1)
                        nc.vector.tensor_scalar(y[:], u[:, 0:T], C.col(24, c), C.col(48, c), ALU.mult, ALU.add).then_inc(step, 1)
                        dve.wait_ge(step, c * 3 + 1)
                        nc.vector.scalar_tensor_tensor(out=y[:], in0=u[:, 1:T + 1], scalar=C.col(32, c), in1=y[:], op0=ALU.mult, op1=ALU.add).then_inc(step, 1)
                        dve.wait_ge(step, c * 3 + 2)
                        nc.vector.scalar_tensor_tensor(out=y[:], in0=u[:, 2:T + 2], scalar=C.col(40, c), in1=y[:], op0=ALU.mult, op1=ALU.add).then_inc(step, 1)
                        dve.wait_ge(step, c * 3 + 3)
                        dve.wait_ge(w.used, i * 6 + (3 * s + 3))
                        nc.vector.tensor_tensor(y[:], flat(ps[:, 2]), y[:], ALU.mult).then_inc(y_done, 1)
                        dve.wait_ge(high, c + 1)
                        nc.vector.tensor_tensor(chunk(y_lo, c), y[:], chunk(y_hi, c).bitcast(F32), ALU.subtract).then_inc(low, 1)
                        dve.wait_ge(low, c + 1)


def refine_rstd(nc, dve, sem, done, rstd, root, ss, tmp, n):
    def link(ins):
        done[0] += 1
        ins.then_inc(sem, 1)
        dve.wait_ge(sem, done[0])

    link(nc.vector.reciprocal(rstd, root))
    link(nc.vector.tensor_scalar(tmp, ss, 1.0 / n, EPS, ALU.mult, ALU.add))
    link(nc.vector.tensor_tensor(tmp, tmp, rstd, ALU.mult))
    link(nc.vector.tensor_tensor(tmp, tmp, rstd, ALU.mult))
    link(nc.vector.tensor_scalar(tmp, tmp, -0.5, 1.5, ALU.mult, ALU.add))
    link(nc.vector.tensor_tensor(rstd, rstd, tmp, ALU.mult))


def out_project(nc, A, C, m, x2, ss):
    with ExitStack() as ctx:
        sb = lambda n, s, d=F32: ctx.enter_context(nc.sbuf_tensor(n, s, d))
        sem = ctx.enter_context(Semaphores(nc))
        raw = sb("op_raw", [P, 2, D])
        w_hi, w_lo = sb("op_w_hi", [P, NC, D], F32R), sb("op_w_lo", [P, NC, D], F32R)
        m_hi, m_lo = sb("op_m_hi", [P, 2, NC, P], F32R), sb("op_m_lo", [P, 2, NC, P], F32R)
        x = sb("op_x", [P, 2, D])
        junk = sb("op_junk", [P, D])
        ps = ctx.enter_context(nc.psum_tensor("op_ps", [P, 2, 2, HALF], F32))
        w_in = [sem(f"op_w_in{s}") for s in range(2)]
        x_in = [sem(f"op_x_in{s}") for s in range(2)]
        w_high, w_split, m_high, m_split, made, added, squared = (
            sem(f"op_{n}") for n in ("w_high", "w_split", "m_high", "m_split", "made", "added", "squared"))
        with nc.Block() as block:
            @block.sync
            def _(sp):
                for k in range(NC):
                    if k >= 2:
                        sp.wait_ge(w_split, k - 1)
                    sp.dma_start(raw[:, k % 2], A["w_out"][k]).then_inc(w_in[k % 2], 16)
                for b in range(NB):
                    if b >= 2:
                        sp.wait_ge(added, b - 1)
                    sp.dma_start(x[:, b % 2], A["x"][b]).then_inc(x_in[b % 2], 16)

            @block.gpsimd
            def _(pool):
                for b in range(NB):
                    pool.wait_ge(m_high, b + 1)
                    nc.gpsimd.tensor_tensor(m_lo[:, b % 2], m[:, :, b * P:(b + 1) * P], m_hi[:, b % 2].bitcast(F32), ALU.subtract).then_inc(m_split, 1)

            @block.scalar
            def _(act):
                def split_m(b):
                    if b >= 2:
                        act.wait_ge(made, b - 1)
                    nc.scalar.copy(m_hi[:, b % 2], m[:, :, b * P:(b + 1) * P]).then_inc(m_high, 1)

                split_m(0)
                split_m(1)
                for k in range(NC):
                    act.wait_ge(w_in[k % 2], 16 * (k // 2 + 1))
                    nc.scalar.copy(w_hi[:, k], raw[:, k % 2]).then_inc(w_high, 1)
                for b in range(NB):
                    if b + 2 < NB:
                        split_m(b + 2)
                    act.wait_ge(added, b + 1)
                    if b:
                        act.wait_ge(squared, b)
                    nc.scalar.activation(junk[:], x2[:, b], ACT.Square, accum_out=ss[:, b:b + 1]).then_inc(squared, 1)

            @block.tensor
            def _(pe):
                for b in range(NB):
                    pe.wait_ge(m_split, b + 1)
                    if b >= 2:
                        pe.wait_ge(added, b - 1)
                    for k in range(NC):
                        if b == 0:
                            pe.wait_ge(w_split, k + 1)
                        for i, (a, part) in enumerate(((m_hi, w_hi), (m_hi, w_lo), (m_lo, w_hi))):
                            for t in range(2):
                                last = nc.tensor.matmul(ps[:, b % 2, t], a[:, b % 2, k], part[:, k, t * HALF:(t + 1) * HALF],
                                                        start=(k == 0 and i == 0), stop=(k == NC - 1 and i == 2))
                    last.then_inc(made, 1)

            @block.vector
            def _(dve):
                for k in range(NC):
                    dve.wait_ge(w_high, k + 1)
                    nc.vector.tensor_tensor(w_lo[:, k], raw[:, k % 2], w_hi[:, k].bitcast(F32), ALU.subtract).then_inc(w_split, 1)
                for b in range(NB):
                    dve.wait_ge(made, b + 1)
                    dve.wait_ge(x_in[b % 2], 16 * (b // 2 + 1))
                    nc.vector.tensor_tensor(x2[:, b], ps[:, b % 2].rearrange("p a b -> p (a b)"), x[:, b % 2], ALU.add).then_inc(added, 1)


def norm_second(nc, A, C, ident, x2, ss, rstd, xt_hi, xt_lo):
    with ExitStack() as ctx:
        sb = lambda n, s, d=F32: ctx.enter_context(nc.sbuf_tensor(n, s, d))
        sem = ctx.enter_context(Semaphores(nc))
        root = sb("n2_root", [P, NB])
        g2 = sb("n2_g", [P, D])
        tmp = sb("n2_tmp", [P, NB])
        xt = sb("n2_xt", [P, 2, D])
        ps = ctx.enter_context(nc.psum_tensor("n2_ps", [P, 2, NC, P], F32))
        rows_in, rooted, link, scaled, turned, high, low = (sem(f"n2_{n}") for n in ("rows_in", "rooted", "link", "scaled", "turned", "high", "low"))
        made = sem("n2_made")
        with nc.Block() as block:
            @block.gpsimd
            def _(pool):
                nc.gpsimd.memset(ident[:], 0.0).then_inc(made, 1)
                pool.wait_ge(made, 1)
                nc.gpsimd.affine_select(out=ident[:], in_=ident[:], compare_op=ALU.not_equal, fill=1.0, base=0,
                                        pattern=[[-1, P]], channel_multiplier=1).then_inc(made, 1)

            @block.sync
            def _(sp):
                sp.dma_start(g2[:], A["norm2_g"].to_broadcast([P, D])).then_inc(rows_in, 16)

            @block.scalar
            def _(act):
                nc.scalar.activation(root[:], ss[:], ACT.Sqrt, bias=C.eps[:, 0:1], scale=1.0 / D).then_inc(rooted, 1)
                for b in range(NB):
                    act.wait_ge(turned, b + 1)
                    nc.scalar.copy(xt_hi[b // 4][:, :, (b % 4) * P:(b % 4 + 1) * P], ps[:, b % 2]).then_inc(high, 1)

            @block.tensor
            def _(pe):
                pe.wait_ge(made, 2)
                for b in range(NB):
                    pe.wait_ge(scaled, b + 1)
                    if b >= 2:
                        pe.wait_ge(low, b - 1)
                    for c in range(NC):
                        last = nc.tensor.transpose(ps[:, b % 2, c], xt[:, b % 2, c * P:(c + 1) * P], ident[:])
                    last.then_inc(turned, 1)

            @block.vector
            def _(dve):
                dve.wait_ge(rooted, 1)
                refine_rstd(nc, dve, link, [0], rstd[:], root[:], ss[:], tmp[:], D)
                dve.wait_ge(rows_in, 16)

                def scale(b):
                    if b >= 2:
                        dve.wait_ge(turned, b - 1)
                    nc.vector.scalar_tensor_tensor(out=xt[:, b % 2], in0=x2[:, b], scalar=rstd[:, b:b + 1], in1=g2[:],
                                                   op0=ALU.mult, op1=ALU.mult).then_inc(scaled, 1)

                scale(0)
                for b in range(NB):
                    if b + 1 < NB:
                        scale(b + 1)
                    dve.wait_ge(high, b + 1)
                    nc.vector.tensor_tensor(xt_lo[b // 4][:, :, (b % 4) * P:(b % 4 + 1) * P], ps[:, b % 2],
                                            xt_hi[b // 4][:, :, (b % 4) * P:(b % 4 + 1) * P].bitcast(F32),
                                            ALU.subtract).then_inc(low, 1)


def route(nc, A, C, xt_hi, xt_lo, xe_hi, xe_lo, halves, dense_gates, experts, gates):
    with ExitStack() as ctx:
        sb = lambda n, s, d=F32: ctx.enter_context(nc.sbuf_tensor(n, s, d))
        sem = ctx.enter_context(Semaphores(nc))
        w = Weights(ctx, nc, sem, "q")
        keys = sb("rt_keys", [P, 2 * PH, NKEYS])
        q = sb("rt_q", [P, 2, T])
        s0 = sb("rt_s0", [P, 2, NB, NKEYS])
        s1 = sb("rt_s1", [P, 2, NB, NKEYS])
        top = sb("rt_top", [P, 2, NB, TOPK])
        topi = sb("rt_topi", [P, 2, 2, NB, TOPK], U32)
        topf = sb("rt_topf", [P, 2, NB, TOPK])
        cand = sb("rt_cand", [P, NB, TOPK, TOPK])
        hit = sb("rt_hit", [P, 2, NB, TOPK, TOPK])
        rest = hit[:, 1]
        best = sb("rt_best", [P, NB, TOPK])
        besti = sb("rt_besti", [P, NB, TOPK], U32)
        where = sb("rt_where", [P, 2, NB, TOPK], U32)
        wheref = sb("rt_wheref", [P, 2, NB, TOPK])
        half = sb("rt_half", [P, 2, NB, TOPK])
        iota = sb("rt_iota", [P, TOPK])
        shifted = sb("rt_shifted", [P, NB, TOPK])
        total = sb("rt_total", [P, NB])
        q_ps = ctx.enter_context(nc.psum_tensor("rt_q_ps", [P, 2, 2, HALF], F32))
        s_ps = ctx.enter_context(nc.psum_tensor("rt_s_ps", [P, 2, NB, NKEYS], F32))
        keys_in, q_out, made, s_out, less, exped, counted, link_, searched, picked, decode = (sem(f"rt_{n}") for n in (
            "keys_in", "q_out", "made", "s_out", "less", "exped", "counted", "link", "searched", "picked", "decode"))
        LINKS = 13
        STEPS = 14

        def slots(tile, n, h):
            return tile[..., 0:n, bass.ds(h * TOPK, TOPK)]

        with nc.Block() as block:
            @block.sync
            def _(sp):
                sp.dma_start(keys[:], A["keys"]).then_inc(keys_in, 16)
                load_weights(sp, w, A["stream_q"], 0, 2 * PH)

            @block.tensor
            def _(pe):
                pe.wait_ge(keys_in, 16)
                with pe.Fori(0, PH) as h:
                    for s in range(2):
                        pe.wait_ge(w.split, h * 2 + (s + 1))
                        pe.wait_ge(q_out, h * 2)
                        project(nc, w, s, xt_hi, xt_lo, q_ps[:, s]).then_inc(w.used, 1)
                    for s in range(2):
                        pe.wait_ge(q_out, h * 2 + (s + 1))
                        pe.wait_ge(s_out, h * 2)
                        for b in range(NB):
                            last = nc.tensor.matmul(s_ps[:, s, b], q[:, s, b * P:(b + 1) * P], chunk(keys, h * 2 + s),
                                                    start=(b % 4 == 0), stop=(b % 4 == 3), skip_group_check=True)
                        last.then_inc(made, 1)

            @block.scalar
            def _(act):
                def queries(used):
                    for s in range(2):
                        act.wait_ge(w.used, used + (s + 1))
                        nc.scalar.copy(q[:, s], q_ps[:, s].rearrange("p a b -> p (a b)")).then_inc(q_out, 1)

                def head(h, more):
                    for s in range(2):
                        act.wait_ge(made, h * 2 + (s + 1))
                        act.wait_ge(searched, h + 1)
                        nc.scalar.copy(s0[:, s], s_ps[:, s]).then_inc(s_out, 1)
                    if more:
                        queries(h * 2 + 2)
                    act.wait_ge(less, h + 1)
                    nc.scalar.activation(shifted[:], shifted[:], ACT.Exp).then_inc(exped, 1)

                act.sem_inc(searched, 1)
                nc.scalar.copy(xe_hi, xt_hi[1][:, :, 0:DT - HALF])
                nc.scalar.copy(xe_lo, xt_lo[1][:, :, 0:DT - HALF])
                queries(0)
                with act.Fori(0, PH - 1) as h:
                    head(h, True)
                head(PH - 1, False)

            @block.vector
            def _(dve):
                with dve.Fori(0, PH // 2) as i:
                    for p in range(2):
                        h = i * 2 + p
                        steps = [0]

                        def link(ins, h=h, steps=steps):
                            steps[0] += 1
                            ins.then_inc(link_, 1)
                            dve.wait_ge(link_, h * LINKS + steps[0])
                            C.settle(dve, "dve")

                        def top16(source, left, values, indices, n, end=None):
                            for at in range(2):
                                src = source if at == 0 else left
                                for c in range(n):
                                    ins = nc.vector.max(values(c, at), src(c))
                                link(ins)
                                for c in range(n):
                                    ins = nc.vector.max_index(indices(c, at), values(c, at), src(c))
                                if at == 0:
                                    for c in range(n):
                                        ins = nc.vector.match_replace(left(c), values(c, at), src(c), NEG)
                                if at == 0 or end is None:
                                    link(ins)
                                else:
                                    ins.then_inc(end, 1)

                        dve.wait_ge(s_out, h * 2 + 2)
                        dve.wait_ge(picked, h + 1)
                        C.settle(dve, "dve")
                        rows = lambda t: lambda c: t[:, c // NB, c % NB]
                        top16(rows(s0), rows(s1), lambda c, a: top[:, c // NB, c % NB, 8 * a:8 * a + 8],
                              lambda c, a, p=p: topi[:, p, c // NB, c % NB, 8 * a:8 * a + 8], 2 * NB, searched)
                        link(nc.vector.tensor_tensor(cand[:], top[:, 0].unsqueeze(3).to_broadcast([P, NB, TOPK, TOPK]),
                                                     top[:, 1].unsqueeze(2).to_broadcast([P, NB, TOPK, TOPK]), ALU.add))
                        dve.wait_ge(picked, h + 2)
                        C.settle(dve, "dve")
                        flat = lambda t: lambda b: t[:, b].rearrange("p a b -> p (a b)")
                        top16(flat(cand), flat(rest), lambda b, a: best[:, b, 8 * a:8 * a + 8], lambda b, a: besti[:, b, 8 * a:8 * a + 8], NB)
                        nc.vector.tensor_tensor(shifted[:], best[:], best[:, :, 0:1].to_broadcast([P, NB, TOPK]), ALU.subtract).then_inc(less, 1)
                        nc.vector.tensor_scalar(where[:, 0], besti[:], 4, None, ALU.logical_shift_right)
                        link(nc.vector.tensor_scalar(where[:, 1], besti[:], TOPK - 1, None, ALU.bitwise_and))
                        link(nc.vector.tensor_copy(wheref[:], where[:]))
                        dve.wait_ge(counted, 1)
                        for side in range(2):
                            ins = nc.vector.tensor_tensor(hit[:, side].rearrange("p b k i -> p (b k) i"),
                                                          wheref[:, side].rearrange("p b k -> p (b k)").unsqueeze(2).to_broadcast([P, NB * TOPK, TOPK]),
                                                          iota[:].unsqueeze(1).to_broadcast([P, NB * TOPK, TOPK]), ALU.is_equal)
                        ins.then_inc(decode, 1)
                        dve.wait_ge(exped, h + 1)
                        link(nc.vector.tensor_reduce(total[:], shifted[:], AX.X, ALU.add))
                        link(nc.vector.reciprocal(total[:], total[:]))
                        for tile, b0, b1 in ((dense_gates, 0, DB), (gates, DB, NB)):
                            ins = nc.vector.tensor_tensor(slots(tile, b1 - b0, h), shifted[:, b0:b1],
                                                          total[:, b0:b1].unsqueeze(2).to_broadcast([P, b1 - b0, TOPK]), ALU.mult)
                        link(ins)
                        assert steps[0] == LINKS, steps[0]

            @block.gpsimd
            def _(pool):
                nc.gpsimd.iota(iota[:], [[1, TOPK]], base=0, channel_multiplier=0, allow_small_or_imprecise_dtypes=True).then_inc(counted, 1)
                pool.wait_ge(counted, 1)
                for s in range(2):
                    split_chunk(nc, pool, C, w, s, s, 16)
                nc.gpsimd.memset(half[:], 0.0).then_inc(counted, 1)
                pool.wait_ge(counted, 2)

                def decode_head(h, p):
                    steps = [0]

                    def link(ins):
                        steps[0] += 1
                        ins.then_inc(picked_steps, 1)
                        pool.wait_ge(picked_steps, h * STEPS + steps[0])
                        C.settle(pool, "pool")

                    pool.wait_ge(decode, h + 1)
                    C.settle(pool, "pool")
                    link(nc.gpsimd.tensor_copy(topf[:], topi[:, p]))
                    for side in range(2):
                        link(nc.gpsimd.tensor_tensor(hit[:, side], hit[:, side], topf[:, side].unsqueeze(2).to_broadcast([P, NB, TOPK, TOPK]), ALU.mult))
                        n = TOPK // 2
                        while n > 1:
                            link(nc.gpsimd.tensor_tensor(hit[:, side, ..., 0:n], hit[:, side, ..., 0:n], hit[:, side, ..., n:2 * n], ALU.add))
                            n //= 2
                        link(nc.gpsimd.tensor_tensor(half[:, side], hit[:, side, ..., 0], hit[:, side, ..., 1], ALU.add))
                    link(nc.gpsimd.tensor_scalar(topf[:, 0], half[:, 0], float(NKEYS), None, ALU.mult))
                    for side in range(2):
                        nc.gpsimd.tensor_copy(slots(halves[:, side], DB, h), half[:, side, 0:DB])
                    link(nc.gpsimd.tensor_tensor(topf[:, 0], topf[:, 0], half[:, 1], ALU.add))
                    link(nc.gpsimd.tensor_copy(slots(experts, NB - DB, h), topf[:, 0, DB:NB]))
                    assert steps[0] == STEPS, steps[0]
                    pool.sem_inc(picked, 1)

                picked_steps = sem("rt_picked_steps")
                pool.sem_inc(picked, 2)
                for s in range(2):
                    pool.wait_ge(w.used, s + 1)
                    split_chunk(nc, pool, C, w, s, 2 + s, 32)
                with pool.Fori(0, PH // 2 - 1) as i:
                    for p in range(2):
                        for s in range(2):
                            pool.wait_ge(w.used, i * 4 + (2 * p + s + 3))
                            split_chunk(nc, pool, C, w, s, i * 4 + (2 * p + s + 4), i * 32 + (16 * (p + 3)))
                        decode_head(i * 2 + p, p)
                decode_head(PH - 2, 0)
                decode_head(PH - 1, 1)


def gate_tables(nc, A, C, ident, halves, gates, gate_chunks):
    BATCH = 8
    SLOT = 4
    QUADS = P // 4
    ROUNDS = P // BATCH // SLOT
    with ExitStack() as ctx:
        sb = lambda n, s, d=F32: ctx.enter_context(nc.sbuf_tensor(n, s, d))
        sem = ctx.enter_context(Semaphores(nc))
        table = sb("gt_table", [P, 2, NKEYS, 64])
        cols = sb("gt_cols", [P, 3, P])
        rows = sb("gt_rows", [P, SLOT, 2, BATCH, NKEYS])
        gate8 = sb("gt_gate8", [P, SLOT, BATCH])
        iota = sb("gt_iota", [P, NKEYS])
        t_ps = ctx.enter_context(nc.psum_tensor("gt_t_ps", [P, 4, P], F32))
        BANKS = 4
        g_ps = ctx.enter_context(nc.psum_tensor("gt_g_ps", [P, BANKS, 4, NKEYS], F32))
        counted, turned, cols_out, equaled, copied, gated_pool, gated_dve, made, out_, stored0, stored1 = (
            sem(f"gt_{n}") for n in ("counted", "turned", "cols_out", "equaled", "copied", "gated_pool", "gated_dve", "made", "out", "stored0", "stored1"))
        stored = (stored0, stored1)
        MADE = SLOT * BATCH // 4
        with nc.Block() as block:
            @block.gpsimd
            def _(pool):
                nc.gpsimd.iota(iota[:], [[1, NKEYS]], base=0, channel_multiplier=0, allow_small_or_imprecise_dtypes=True).then_inc(counted, 1)
                for b in range(DB):
                    with pool.Fori(0, ROUNDS) as i:
                        for p in range(SLOT - 1):
                            pool.wait_ge(equaled, i * SLOT + (b * SLOT * ROUNDS + p + 1))
                            C.settle(pool, "pool")
                            nc.gpsimd.tensor_copy(gate8[:, p], cols[:, 2, bass.ds(i * (SLOT * BATCH) + p * BATCH, BATCH)]).then_inc(copied, 1)
                            pool.wait_ge(copied, i * (SLOT - 1) + (b * (SLOT - 1) * ROUNDS + p + 1))
                            nc.gpsimd.tensor_tensor(rows[:, p, 1], rows[:, p, 1], gate8[:, p].unsqueeze(2).to_broadcast([P, BATCH, NKEYS]),
                                                    ALU.mult).then_inc(gated_pool, 1)

            @block.tensor
            def _(pe):
                for b in range(DB):
                    if b:
                        pe.wait_ge(cols_out, b)
                    for n, tile in enumerate((halves[:, 0, b], halves[:, 1, b], gates[:, b])):
                        last = nc.tensor.transpose(t_ps[:, n], tile, ident[:])
                    last.then_inc(turned, 1)
                    with pe.Fori(0, ROUNDS) as i:
                        for q in range(MADE):
                            p = q * 4 // BATCH
                            if q % 2 == 0 and p < SLOT - 1:
                                pe.wait_ge(gated_pool, i * (SLOT - 1) + (b * (SLOT - 1) * ROUNDS + p + 1))
                            elif q % 2 == 0:
                                pe.wait_ge(gated_dve, i + (b * ROUNDS + 1))
                            pe.wait_ge(out_, i * MADE + (b * QUADS + q + 1))
                            for t in range(4):
                                at = q % 2 * 4 + t
                                last = nc.tensor.matmul(g_ps[:, q % BANKS, t], rows[:, p, 1, at], rows[:, p, 0, at], start=(t == 0), stop=(t == 3),
                                                        skip_group_check=True)
                            last.then_inc(made, 1)

            @block.vector
            def _(dve):
                dve.sem_inc(made, MADE)
                dve.wait_ge(counted, 1)
                for b in range(DB):
                    dve.wait_ge(turned, b + 1)
                    if b:
                        dve.wait_ge(gated_pool, b * (SLOT - 1) * ROUNDS)
                    nc.vector.tensor_copy(cols[:], t_ps[:, 0:3]).then_inc(cols_out, 1)
                    dve.wait_ge(cols_out, b + 1)
                    C.settle(dve, "dve")
                    with dve.Fori(0, ROUNDS) as i:
                        for p in range(SLOT):
                            tokens = bass.ds(i * (SLOT * BATCH) + p * BATCH, BATCH)
                            dve.wait_ge(made, i * MADE + (b * QUADS + (p + 1) * BATCH // 4))
                            nc.vector.tensor_tensor(rows[:, p], iota[:].unsqueeze(1).unsqueeze(1).to_broadcast([P, 2, BATCH, NKEYS]),
                                                    cols[:, 0:2, tokens].unsqueeze(3).to_broadcast([P, 2, BATCH, NKEYS]), ALU.is_equal).then_inc(equaled, 1)
                        dve.wait_ge(equaled, i * SLOT + (b * SLOT * ROUNDS + SLOT))
                        nc.vector.tensor_tensor(rows[:, p, 1], rows[:, p, 1], cols[:, 2, tokens].unsqueeze(2).to_broadcast([P, BATCH, NKEYS]),
                                                ALU.mult).then_inc(gated_dve, 1)

            @block.scalar
            def _(act):
                act.sem_inc(out_, BANKS)
                for b in range(DB):
                    for n in range(2):
                        if b:
                            act.wait_ge(stored[n], 16 * b)
                        with act.Fori(0, QUADS // 2 // BANKS) as i:
                            for p in range(BANKS):
                                act.wait_ge(made, i * BANKS + (b * QUADS + n * QUADS // 2 + p + 1 + MADE))
                                C.settle(act, "act")
                                nc.scalar.copy(table[:, n, :, bass.ds((i * BANKS + p) * 4, 4)].rearrange("p k t -> p t k"), g_ps[:, p]).then_inc(out_, 1)

            @block.sync
            def _(sp):
                for b in range(DB):
                    for n in range(2):
                        sp.wait_ge(out_, b * QUADS + (n + 1) * QUADS // 2 + BANKS)
                        sp.dma_start(gate_chunks[:, :, b * P + n * 64:b * P + (n + 1) * 64].rearrange("a i t -> i a t"), table[:, n]).then_inc(stored[n], 16)
                for n in range(2):
                    sp.wait_ge(stored[n], 16 * DB)


def peer(nc, A, C, x2, rstd, xd_hi, xd_lo, experts, gates, gate_chunks):
    GROUPS = NKEYS // GROUP
    SIZES = (24, 24, 24, 24, 32)
    GU = max(SIZES)
    STEPS = len(SIZES)
    REST = GROUPS - (NB - DB) * 2 * STEPS
    assert REST >= 0 and sum(SIZES) == SLOTS and not any(n % RING for n in SIZES) and len(set(SIZES[:-1])) == 1 and STEPS % 2 == 1
    TURNS = DB * 2
    BANKS = 4
    with ExitStack() as ctx:
        sb = lambda n, s, d=F32: ctx.enter_context(nc.sbuf_tensor(n, s, d))
        sem = ctx.enter_context(Semaphores(nc))
        u_raw = sb("pe_u_raw", [P, 2, NC, P])
        u_hi, u_lo = sb("pe_u_hi", [P, 2, NC, P], F32R), sb("pe_u_lo", [P, 2, NC, P], F32R)
        v_raw = sb("pe_v_raw", [P, 2, D])
        v_hi, v_lo = sb("pe_v_hi", [P, GROUP, D], F32R), sb("pe_v_lo", [P, GROUP, D], F32R)
        g_in = sb("pe_g_in", [P, 2, DT])
        a = sb("pe_a", [P, DT])
        a_hi, a_lo = sb("pe_a_hi", [P, GROUP, DT], F32R), sb("pe_a_lo", [P, GROUP, DT], F32R)
        ring = sb("pe_ring", [P, RING, D])
        xt = sb("pe_xt", [P, D])
        acc = xt
        g2 = sb("pe_g2", [P, D])
        index = sb("pe_index", [P, 3, GU], U32)
        hidden = sb("pe_hidden", [P, 3, GU])
        weight = sb("pe_weight", [P, SLOTS])
        h_ps = ctx.enter_context(nc.psum_tensor("pe_h_ps", [P, 2, 2, HALF], F32))
        o_ps = ctx.enter_context(nc.psum_tensor("pe_o_ps", [P, BANKS, HALF], F32))
        ring_in = [sem(f"pe_ring_in{s}") for s in range(RING)]
        u_in, v_in, gate_in = ([sem(f"pe_{n}_in{s}") for s in range(2)] for n in ("u", "v", "g"))
        (rows_in, used, indexed, gelued, xt_ready, weighed, zeroed, summed, u_high, u_split, v_high, v_split,
         h_done, act_done, gated, a_high, a_split, o_done, added) = (sem(f"pe_{n}") for n in (
             "rows_in", "used", "indexed", "gelued", "xt_ready", "weighed", "zeroed", "summed", "u_high", "u_split", "v_high",
             "v_split", "h_done", "act_done", "gated", "a_high", "a_split", "o_done", "added"))
        CREDIT = GU

        def steps_of(loop, body):
            with loop(0, STEPS // 2) as i:
                for p in range(2):
                    body(i * 2 + p, SIZES[0], p)
            body(STEPS - 1, SIZES[-1], 2)

        def row_of(table, c):
            return table[bass.ds(c, 1)].rearrange("o p k -> (o p) k")

        with nc.Block() as block:
            @block.sync
            def _(sp):
                sp.dma_start(g2[:], A["norm2_g"].to_broadcast([P, D])).then_inc(rows_in, 16)
                ut, vt = A["peer_ut"].rearrange("c p k m -> c p (k m)"), A["peer_v"].rearrange("(c p) d -> c p d", p=P)

                def load_u(p, row):
                    sp.dma_start(u_raw[:, p].rearrange("p k m -> p (k m)"), row).then_inc(u_in[p], 16)

                def load_gate_and_v(p, c):
                    sp.dma_start(g_in[:, p], row_of(gate_chunks, c)).then_inc(gate_in[p], 16)
                    sp.dma_start(v_raw[:, p], row_of(vt, c)).then_inc(v_in[p], 16)

                for p in range(2):
                    load_u(p, ut[p])
                for p in range(2):
                    load_gate_and_v(p, p)
                for p in range(2):
                    sp.wait_ge(u_split, p + 1)
                    load_u(p, ut[2 + p])
                with sp.Fori(0, NKEYS // 2 - 2) as i:
                    for p in range(2):
                        sp.wait_ge(a_split, i * 2 + (p + 1))
                        sp.wait_ge(v_split, i * 2 + (p + 1))
                        load_gate_and_v(p, i * 2 + (p + 2))
                        sp.wait_ge(u_split, i * 2 + (p + 3))
                        load_u(p, row_of(ut, i * 2 + (p + 4)))
                for p in range(2):
                    sp.wait_ge(a_split, NKEYS - 3 + p)
                    sp.wait_ge(v_split, NKEYS - 3 + p)
                    load_gate_and_v(p, NKEYS - 2 + p)
                    sp.wait_ge(u_split, NKEYS - 1 + p)
                    load_u(p, ut[p])

            @block.gpsimd
            def _(pool):
                def u_low(s, c):
                    pool.wait_ge(u_high, c + 1)
                    nc.gpsimd.tensor_tensor(u_lo[:, s], u_raw[:, s], u_hi[:, s].bitcast(F32), ALU.subtract).then_inc(u_split, 1)

                u_low(0, 0)
                u_low(1, 1)
                with pool.Fori(0, NB - DB) as b:
                    for side, table in enumerate((A["peer_u"], A["peer_v"])):
                        def step(k, size, place, b=b, side=side, table=table):
                            g = b * (2 * STEPS) + side * STEPS + k
                            rows = b * (2 * SLOTS) + side * SLOTS + k * SIZES[0]
                            pool.wait_ge(indexed, g + 1)
                            for j in range(GROUP + 1):
                                for n in range(j * size // 8, (j + 1) * size // 8 if j < GROUP else size):
                                    pool.wait_ge(used, rows + (n + 1 + CREDIT - RING))
                                    C.settle(pool, "pool")
                                    nc.gpsimd.indirect_dma_start(ring[:, n % RING], None, table,
                                                                 bass.IndirectOffsetOnAxis(index[:, place, n:n + 1], 0)).then_inc(ring_in[n % RING], 16)
                                if j < GROUP:
                                    u_low(j % 2, g * GROUP + (j + 2))

                        steps_of(pool.Fori, step)
                with pool.Fori(GROUPS - REST, GROUPS) as g:
                    for j in range(GROUP):
                        u_low(j % 2, g * GROUP + (j + 2))

            @block.scalar
            def _(act):
                def u_high_part(s, in16):
                    act.wait_ge(u_in[s], in16)
                    nc.scalar.copy(u_hi[:, s], u_raw[:, s]).then_inc(u_high, 1)

                act.sem_inc(gelued, 2)
                act.wait_ge(used, CREDIT)
                u_high_part(0, 16)
                u_high_part(1, 16)

                def dense(g, between=None):
                    for j in range(GROUP):
                        c = g * GROUP + j
                        act.wait_ge(h_done, c + 1)
                        nc.scalar.activation(a[:].rearrange("p (n t) -> p n t", n=2), h_ps[:, j % 2, :, 0:DT // 2], ACT.Gelu).then_inc(act_done, 1)
                        act.wait_ge(u_in[j % 2], g * (GROUP // 2 * 16) + (16 * (j // 2 + 2)))
                        nc.scalar.copy(u_hi[:, j % 2], u_raw[:, j % 2]).then_inc(u_high, 1)
                        act.wait_ge(v_in[j % 2], g * (GROUP // 2 * 16) + (16 * (j // 2 + 1)))
                        act.wait_ge(o_done, g * TURNS)
                        nc.scalar.copy(v_hi[:, j], v_raw[:, j % 2]).then_inc(v_high, 1)
                        act.wait_ge(gated, c + 1)
                        nc.scalar.copy(a_hi[:, j], g_in[:, j % 2]).then_inc(a_high, 1)
                        if j == GROUP // 2 and between:
                            between()

                def indices(b, side, k, size, place):
                    act.wait_ge(used, b * (2 * SLOTS) + side * SLOTS + k * SIZES[0] + (CREDIT - SIZES[0]))
                    C.settle(act, "act")
                    nc.scalar.copy(index[:, place, 0:size], experts[:, bass.ds(b, 1), bass.ds(k * SIZES[0], size)]
                                   .rearrange("q o k -> q (o k)")).then_inc(indexed, 1)

                def gelu_rows(b, k):
                    size, first, place = SIZES[k], k * SIZES[0], k % 2 if k < STEPS - 1 else 2
                    act.wait_ge(used, b * (2 * SLOTS) + (first + size + CREDIT))
                    nc.scalar.activation(weight[:, first:first + size], hidden[:, place, 0:size], ACT.Gelu).then_inc(gelued, 1)

                with act.Fori(0, NB - DB) as b:
                    for k, size in enumerate(SIZES):
                        indices(b, 0, k, size, k % 2 if k < STEPS - 1 else 2)
                        dense(b * (2 * STEPS) + k, (lambda b=b, k=k: gelu_rows(b, k - 1)) if k else None)

                    for k, size in enumerate(SIZES):
                        indices(b, 1, k, size, k % 2 if k < STEPS - 1 else 2)
                        if k == 0:
                            gelu_rows(b, STEPS - 1)
                        dense(b * (2 * STEPS) + (STEPS + k))
                with act.Fori(GROUPS - REST, GROUPS) as g:
                    dense(g)

            @block.tensor
            def _(pe):
                def hidden_of(g, j):
                    pe.wait_ge(u_split, g * GROUP + (j + 1))
                    if j >= 2:
                        pe.wait_ge(act_done, g * GROUP + (j - 1))
                    for k in range(NC):
                        for i, (u, x) in enumerate(((u_hi, xd_hi), (u_hi, xd_lo), (u_lo, xd_hi))):
                            for n in range(2):
                                last = nc.tensor.matmul(h_ps[:, j % 2, n, 0:DT // 2], u[:, j % 2, k], x[:, k, n * DT // 2:(n + 1) * DT // 2], start=(k == 0 and i == 0),
                                                        stop=(k == NC - 1 and i == 2))
                    last.then_inc(h_done, 1)

                def out_of(g):
                    pe.wait_ge(v_split, g * GROUP + GROUP)
                    pe.wait_ge(a_split, g * GROUP + GROUP)
                    for n in range(TURNS):
                        tb, half = n // 2, n % 2
                        before = max(m for m in range(-TURNS, n) if m % TURNS % BANKS == n % BANKS)
                        pe.wait_ge(added, g * TURNS + (before + 1 + BANKS))
                        for j in range(GROUP):
                            for i, (x, v) in enumerate(((a_hi, v_hi), (a_hi, v_lo), (a_lo, v_hi))):
                                last = nc.tensor.matmul(o_ps[:, n % BANKS], x[:, j, tb * P:(tb + 1) * P], v[:, j, half * HALF:(half + 1) * HALF],
                                                        start=(j == 0 and i == 0), stop=(j == GROUP - 1 and i == 2))
                        last.then_inc(o_done, 1)

                hidden_of(0, 0)
                hidden_of(0, 1)
                with pe.Fori(0, GROUPS - 1) as g:
                    for j in range(2, GROUP + 2):
                        hidden_of(g, j)
                    out_of(g)
                hidden_of(GROUPS - 1, 2)
                hidden_of(GROUPS - 1, 3)
                out_of(GROUPS - 1)

            @block.vector
            def _(dve):
                nc.vector.memset(weight[:], 0.0).then_inc(used, CREDIT)
                dve.sem_inc(added, BANKS)
                dve.wait_ge(rows_in, 16)

                def dense_v(g, j):
                    dve.wait_ge(v_high, g * GROUP + (j + 1))
                    nc.vector.tensor_tensor(v_lo[:, j], v_raw[:, j % 2], v_hi[:, j].bitcast(F32), ALU.subtract).then_inc(v_split, 1)

                def dense_gate(g, j):
                    c = g * GROUP + j
                    dve.wait_ge(gate_in[j % 2], g * (GROUP // 2 * 16) + (16 * (j // 2 + 1)))
                    dve.wait_ge(act_done, c + 1)
                    nc.vector.tensor_tensor(g_in[:, j % 2], a[:], g_in[:, j % 2], ALU.mult).then_inc(gated, 1)

                def dense_low(g, j):
                    dve.wait_ge(a_high, g * GROUP + (j + 1))
                    nc.vector.tensor_tensor(a_lo[:, j], g_in[:, j % 2], a_hi[:, j].bitcast(F32), ALU.subtract).then_inc(a_split, 1)

                def dense_add(g, n):
                    place = x2[:, n // 2, (n % 2) * HALF:(n % 2 + 1) * HALF]
                    dve.wait_ge(o_done, g * TURNS + (n + 1))
                    nc.vector.tensor_tensor(place, o_ps[:, n % BANKS], place, ALU.add).then_inc(added, 1)

                def group(g, size, gathered):
                    dense = [step for j in range(GROUP) for step in ((dense_gate, dense_v, j), (dense_low, None, j))]
                    dense += [(dense_add, None, n) for n in range(TURNS)]
                    for at, (first, second, j) in enumerate(dense):
                        for n in range(at * size // len(dense), (at + 1) * size // len(dense)):
                            gathered(n)
                        first(g, j)
                        if second:
                            second(g, j)

                with dve.Fori(0, NB - DB) as b:
                    row = x2[:, bass.ds(b + DB, 1)].rearrange("p o d -> p (o d)")
                    dve.wait_ge(summed, b)
                    nc.vector.scalar_tensor_tensor(out=xt[:], in0=row, scalar=rstd[:, bass.ds(b + DB, 1)], in1=g2[:], op0=ALU.mult, op1=ALU.mult).then_inc(xt_ready, 1)
                    dve.wait_ge(xt_ready, b + 1)
                    C.settle(dve, "dve")

                    def dots(k, size, place, b=b):
                        rows = b * (2 * SLOTS // RING * 16) + k * (SIZES[0] // RING * 16)
                        dve.wait_ge(gelued, b * STEPS + (k + 1))

                        def dot(n):
                            dve.wait_ge(ring_in[n % RING], rows + (n // RING + 1) * 16)
                            nc.vector.tensor_tensor_reduce(out=ring[:, n % RING], in0=ring[:, n % RING], in1=xt[:], scale=1.0, scalar=0.0, op0=ALU.mult,
                                                           op1=ALU.add, accum_out=hidden[:, place, n:n + 1]).then_inc(used, 1)

                        group(b * (2 * STEPS) + k, size, dot)

                    steps_of(dve.Fori, dots)
                    dve.wait_ge(gelued, b * STEPS + (STEPS + 2))
                    nc.vector.memset(acc[:], 0.0).then_inc(zeroed, 1)
                    nc.vector.tensor_tensor(weight[:], weight[:], gates[:, bass.ds(b, 1)].rearrange("p o k -> p (o k)"), ALU.mult).then_inc(weighed, 1)
                    dve.wait_ge(weighed, b + 1)
                    dve.wait_ge(zeroed, b + 1)
                    C.settle(dve, "dve")

                    def sums(k, size, place, b=b):
                        rows = b * (2 * SLOTS // RING * 16) + (SLOTS // RING * 16) + k * (SIZES[0] // RING * 16)

                        def add(n):
                            dve.wait_ge(ring_in[n % RING], rows + (n // RING + 1) * 16)
                            dve.wait_ge(used, b * (2 * SLOTS) + SLOTS + k * SIZES[0] + (CREDIT + n - 1))
                            into = acc[:] if n % 2 else row
                            nc.vector.scalar_tensor_tensor(out=into, in0=ring[:, n % RING], scalar=weight[:, bass.ds(k * SIZES[0] + n, 1)] if place < 2
                                                           else weight[:, k * SIZES[0] + n:k * SIZES[0] + n + 1],
                                                           in1=into, op0=ALU.mult, op1=ALU.add).then_inc(used, 1)

                        group(b * (2 * STEPS) + STEPS + k, size, add)

                    steps_of(dve.Fori, sums)
                    dve.wait_ge(used, (b + 1) * (2 * SLOTS) + CREDIT)
                    nc.vector.tensor_tensor(row, row, acc[:], ALU.add).then_inc(summed, 1)
                with dve.Fori(GROUPS - REST, GROUPS) as g:
                    group(g, 0, None)


def final_norm(nc, A, C, x2, out):
    with ExitStack() as ctx:
        sb = lambda n, s, d=F32: ctx.enter_context(nc.sbuf_tensor(n, s, d))
        sem = ctx.enter_context(Semaphores(nc))
        gf = sb("fn_g", [P, D])
        junk = sb("fn_junk", [P, D])
        res = sb("fn_res", [P, NB, D])
        ss, root, rstd, tmp = (sb(f"fn_{n}", [P, NB]) for n in ("ss", "root", "rstd", "tmp"))
        row_in, squared, rooted, link, normed, stored = (sem(f"fn_{n}") for n in ("row_in", "squared", "rooted", "link", "normed", "stored"))
        with nc.Block() as block:
            @block.sync
            def _(sp):
                sp.dma_start(gf[:], A["final_g"].to_broadcast([P, D])).then_inc(row_in, 16)
                for b in range(NB):
                    sp.wait_ge(normed, b + 1)
                    sp.dma_start(out[b * P:(b + 1) * P], res[:, b]).then_inc(stored, 16)
                sp.wait_ge(stored, 16 * NB)

            @block.scalar
            def _(act):
                for b in range(NB):
                    if b:
                        act.wait_ge(squared, b)
                    nc.scalar.activation(junk[:], x2[:, b], ACT.Square, accum_out=ss[:, b:b + 1]).then_inc(squared, 1)
                act.wait_ge(squared, NB)
                nc.scalar.activation(root[:], ss[:], ACT.Sqrt, bias=C.eps[:, 0:1], scale=1.0 / D).then_inc(rooted, 1)

            @block.vector
            def _(dve):
                dve.wait_ge(rooted, 1)
                refine_rstd(nc, dve, link, [0], rstd[:], root[:], ss[:], tmp[:], D)
                dve.wait_ge(row_in, 16)
                for b in range(NB):
                    nc.vector.scalar_tensor_tensor(out=res[:, b], in0=x2[:, b], scalar=rstd[:, b:b + 1], in1=gf[:], op0=ALU.mult, op1=ALU.mult).then_inc(normed, 1)


def build(nc, A, gate_chunks, out):
    with ExitStack() as ctx:
        C = Consts(ctx, nc)

        def sb(c, n, shape, d=F32, side=None):
            return c.enter_context(nc.sbuf_tensor(n, shape, d, side=side) if side else nc.sbuf_tensor(n, shape, d))

        with ExitStack() as mixer:
            C.place_mixers(mixer, nc)
            m = sb(mixer, "qk_then_o_then_m", [P, NC, T])
            with ExitStack() as normed:
                xn_hi, xn_lo = sb(normed, "xn_hi", [P, NC, T], F32R), sb(normed, "xn_lo", [P, NC, T], F32R)
                norm_first(nc, A, C, xn_hi, xn_lo)
                with ExitStack() as g:
                    v = sb(g, "v", [P, NH, NB, DV])
                    bcum = sb(g, "bcum", [P, 2, NH, T])
                    gla_inputs(nc, A, C, xn_hi, xn_lo, m, v, bcum)
                    gla(nc, A, C, m, v, bcum)
                with ExitStack() as g:
                    hi, lo = sb(g, "branch_hi", [P, NC, T], F32R), sb(g, "branch_lo", [P, NC, T], F32R)
                    gla_gate(nc, A, C, xn_hi, xn_lo, m, hi, lo)
                    branch(nc, A, C, "bb", "stream_b", 64, hi, lo, xn_hi, xn_lo, m, False)
                    conv(nc, A, C, xn_hi, xn_lo, hi, lo)
                    branch(nc, A, C, "ba", "stream_a", 56, hi, lo, xn_hi, xn_lo, m, True)
            x2 = sb(ctx, "x2", [P, NB, D], side="right")
            ss, rstd = sb(ctx, "ss2", [P, NB], side="right"), sb(ctx, "rstd2", [P, NB], side="right")
            out_project(nc, A, C, m, x2, ss)
        with ExitStack() as second:
            xd_hi, xd_lo = sb(second, "xd_hi", [P, NC, DT], F32R), sb(second, "xd_lo", [P, NC, DT], F32R)
            experts, gates = sb(second, "experts", [P, NB - DB, SLOTS], U32), sb(second, "gates", [P, NB - DB, SLOTS])
            with ExitStack() as routed:
                ident = sb(routed, "ident", [P, P])
                halves, dense_gates = sb(routed, "halves", [P, 2, DB, SLOTS]), sb(routed, "dense_gates", [P, DB, SLOTS])
                with ExitStack() as t:
                    xg_hi, xg_lo = sb(t, "xg_hi", [P, NC, HALF], F32R), sb(t, "xg_lo", [P, NC, HALF], F32R)
                    xt_hi, xt_lo = (xd_hi[:, :, 0:HALF], xg_hi), (xd_lo[:, :, 0:HALF], xg_lo)
                    norm_second(nc, A, C, ident, x2, ss, rstd, xt_hi, xt_lo)
                    route(nc, A, C, xt_hi, xt_lo, xd_hi[:, :, HALF:DT], xd_lo[:, :, HALF:DT], halves, dense_gates, experts, gates)
                gate_tables(nc, A, C, ident, halves, dense_gates, gate_chunks)
            peer(nc, A, C, x2, rstd, xd_hi, xd_lo, experts, gates, gate_chunks)
        final_norm(nc, A, C, x2, out)


def feature_chunks(w):
    return w.reshape(NC, P, w.shape[1] // P, P).transpose(2, 1, 0, 3)


def kernel(**inputs):
    import concourse.bacc as bacc
    from concourse.bass_utils import run_bass_kernel_spmd

    I = {k: np.asarray(a) for k, a in inputs.items()}
    one = lambda k: I[k][0]
    cut = np.cumsum([D, D, D, NH * DK, NH * DK, D, D, RANK, RANK, D, D])[:-1]
    xa, ba, ca, q, k, v, r, zf, zb, ga, gb = np.split(one("w_in"), cut, axis=1)
    z = np.zeros((D, P), np.float32)
    z[:, 0:RANK], z[:, 32:32 + RANK] = zf, zb
    up = np.zeros((P, NH * DK), np.float32)
    up[0:RANK], up[32:32 + RANK] = one("decay_up_f"), one("decay_up_b")
    pairs = lambda *ws: np.stack([feature_chunks(w) for w in ws], 1).reshape(-1, P, NC, P)
    col = lambda a: a.reshape(-1, P).T
    cols = np.concatenate([col(one("norm1_g")), col(one("decay_bias_f")), col(one("decay_bias_b")), col(one("gla_norm_g")),
                           col(one("conv_w")), col(one("conv_b")), col(one("gate_bias"))], 1)
    arrays = {
        "x": I["x"].reshape(NB, P, D),
        "cols": cols,
        "up": up,
        "stream_g": np.concatenate([feature_chunks(z), pairs(k, q), feature_chunks(v).reshape(NH, 2, P, NC, P)[:, ::-1].reshape(-1, P, NC, P)]),
        "stream_r": feature_chunks(r),
        "stream_b": pairs(gb, one("wb_proj")),
        "stream_conv": pairs(ca, xa, ba),
        "stream_a": pairs(ga, one("wa_proj")),
        "w_out": one("w_out").reshape(NC, P, D),
        "stream_q": feature_chunks(one("peer_wq")),
        "keys": one("peer_keys").reshape(2 * PH, NKEYS, P).transpose(2, 0, 1),
        "norm2_g": I["norm2_g"].reshape(1, D),
        "final_g": I["final_norm_g"].reshape(1, D),
        "peer_u": one("peer_u"),
        "peer_ut": feature_chunks(one("peer_u").T),
        "peer_v": one("peer_v"),
    }
    arrays = {n: np.ascontiguousarray(a) for n, a in arrays.items()}
    nc = bacc.Bacc("TRN2", target_bir_lowering=False, num_devices=1)
    A = {n: nc.dram_tensor(f"in_{n}", a.shape, mybir.dt.from_np(a.dtype), kind="ExternalInput").ap() for n, a in arrays.items()}
    out = nc.dram_tensor("out_x", (T, D), F32, kind="ExternalOutput").ap()
    gate_chunks = nc.dram_tensor("gate_chunks", (NKEYS, P, DT), F32, kind="Internal").ap()
    build(nc, A, gate_chunks, out)
    r = run_bass_kernel_spmd(nc, [{f"in_{n}": a for n, a in arrays.items()}], core_ids=[0])
    return np.asarray(r.results[0]["out_x"]).reshape(1, T, D)


class Consts:
    NCOL = 72

    def __init__(self, ctx, nc):
        self.eps = ctx.enter_context(nc.sbuf_tensor("c_eps", [P, 1], F32))
        self.begun = ctx.enter_context(nc.semaphore("c_begun"))
        self.passed = {e: ctx.enter_context(nc.semaphore(f"c_passed_{e}")) for e in ("act", "dve", "pool")}

    def place_mixers(self, ctx, nc):
        sb = lambda n, s, d=F32: ctx.enter_context(nc.sbuf_tensor(n, s, d))
        self.cols = sb("c_cols", [P, self.NCOL])
        self.up = sb("c_up", [P, NH * DK])
        self.ident = sb("c_ident", [P, P])
        self.ones = sb("c_ones", [P, P])
        self.mask = sb("c_mask", [P, 2, P])

    def settle(self, engine, name):
        engine.sem_inc(self.passed[name], 1)

    def col(self, first, c):
        return self.cols[:, bass.ds(c + first, 1)]

    def norm1_g(self, c):
        return self.cols[:, c:c + 1]

    def decay_bias(self, d, h):
        return self.cols[:, 8 + 4 * d + h:9 + 4 * d + h]
```
